# Optimizing a Trainium2 kernel written in Bass

```python
import math
import jax, jax.numpy as jnp
from jax import lax
import numpy as np

D_MODEL = 1024
BATCH = 1
SEQ = 1024
DEPTH = 1
DEC_BATCH = 8
DEC_SEQ = 1
PAST_LEN = 8192
PAGE_SIZE = 128

CHUNK = 128
A_HEADS = 8
A_WIDTH = D_MODEL
A_HEAD_DIM = A_WIDTH // A_HEADS
POOL_WINDOWS = (2, 4, 8, 16)
POOL_GROUPS = len(POOL_WINDOWS)
B_WIDTH = D_MODEL // 2
B_GROUP_DIM = B_WIDTH // POOL_GROUPS
B_OUT_GROUP = D_MODEL // POOL_GROUPS
W_MAX = max(POOL_WINDOWS)
POOL_STATE = W_MAX - 1
PROJ_COLS = 2 * A_WIDTH + B_WIDTH + 2 * D_MODEL
N_EXPERT_GROUPS = 4
EXPERTS_PER_GROUP = 8
N_EXPERTS = N_EXPERT_GROUPS * EXPERTS_PER_GROUP
TOP_K_IN_GROUP = 2
D_EXPERT = 128
N_MOD = 6
EPS = 1e-6

kernel_name = "hybrid_chunkgmlp_pool_hmoe_step"

def rms_norm(x, g):
    xf = x.astype(jnp.float32)
    y = xf * lax.rsqrt(jnp.mean(xf * xf, axis=-1, keepdims=True) + EPS)
    return (y * g.astype(jnp.float32)).astype(x.dtype)

def layer_norm(x, g, b):
    xf = x.astype(jnp.float32)
    mu = jnp.mean(xf, axis=-1, keepdims=True)
    xc = xf - mu
    var = jnp.mean(xc * xc, axis=-1, keepdims=True)
    y = xc * lax.rsqrt(var + EPS) * g.astype(jnp.float32) + b.astype(jnp.float32)
    return y.astype(x.dtype)

def chunk_mix(v, w_s, b_s):
    bsz, t, _ = v.shape
    l = min(t, CHUNK)
    n = t // l
    vr = v.reshape(bsz, n, l, A_HEADS, A_HEAD_DIM)
    w = jnp.tril(w_s[:, :l, :l])
    out = jnp.einsum("hij,bnjhc->bnihc", w, vr)
    out = out + b_s[:, :l].T[None, None, :, :, None]
    return out.reshape(bsz, t, A_WIDTH)

def pool_mix(p, prefix, pos0, w_pool, pool_scale):
    bsz, t, c = p.shape
    n_prev = prefix.shape[1]
    xb = jnp.concatenate([prefix, p], axis=1)
    xf = xb.astype(jnp.float32)
    xpad = jnp.pad(xf, ((0, 0), (W_MAX, 0), (0, 0)))
    cs0 = jnp.concatenate([jnp.zeros((bsz, 1, c), jnp.float32),
                           jnp.cumsum(xpad, axis=1)], axis=1)
    start = W_MAX + n_prev + 1
    pos = pos0 + jnp.arange(t, dtype=jnp.int32)
    pf = p.astype(jnp.float32)
    groups = []
    for gi, w in enumerate(POOL_WINDOWS):
        sl = slice(gi * B_GROUP_DIM, (gi + 1) * B_GROUP_DIM)
        wsum = cs0[:, start:start + t, sl] - cs0[:, start - w:start - w + t, sl]
        cnt = jnp.minimum(pos + 1, w).astype(jnp.float32)[None, :, None]
        groups.append(wsum / cnt - pf[:, :, sl])
    d = jnp.stack(groups, axis=2)
    y = jnp.einsum("btgc,gco->btgo", d, w_pool.astype(jnp.float32))
    y = y.reshape(bsz, t, D_MODEL) * pool_scale.astype(jnp.float32)
    new_state = xb[:, -POOL_STATE:]
    return y.astype(p.dtype), new_state

def token_mixers(h, prefix, pos0, w_in, ln_v_g, ln_v_b, w_spatial, b_spatial,
                 w_pool, pool_scale, w_out):
    z = jnp.einsum("btd,dk->btk", h, w_in)
    u = z[..., :A_WIDTH]
    v = z[..., A_WIDTH:2 * A_WIDTH]
    p = z[..., 2 * A_WIDTH:2 * A_WIDTH + B_WIDTH]
    ga = z[..., 2 * A_WIDTH + B_WIDTH:2 * A_WIDTH + B_WIDTH + D_MODEL]
    gb = z[..., 2 * A_WIDTH + B_WIDTH + D_MODEL:]
    u = jax.nn.gelu(u)
    v = layer_norm(jax.nn.gelu(v), ln_v_g, ln_v_b)
    y_a = u * chunk_mix(v, w_spatial, b_spatial)
    y_b, new_pool = pool_mix(p, prefix, pos0, w_pool, pool_scale)
    merged = jax.nn.sigmoid(ga) * y_a + jax.nn.sigmoid(gb) * y_b
    return jnp.einsum("btd,de->bte", merged, w_out), new_pool, v

def hier_moe(h, w_router_grp, b_router_grp, w_router_exp, b_router_exp,
             w_exp_gate, w_exp_up, w_exp_down):
    bsz, t, _ = h.shape
    grp_logits = jnp.einsum("btd,dg->btg", h, w_router_grp).astype(jnp.float32) \
        + b_router_grp.astype(jnp.float32)
    grp_prob = jax.nn.softmax(grp_logits, axis=-1)
    g_idx = jnp.argmax(grp_logits, axis=-1)
    p_g = jnp.take_along_axis(grp_prob, g_idx[..., None], axis=-1)
    exp_logits = jnp.einsum("btd,de->bte", h, w_router_exp).astype(jnp.float32) \
        + b_router_exp.astype(jnp.float32)
    exp_logits = exp_logits.reshape(bsz, t, N_EXPERT_GROUPS, EXPERTS_PER_GROUP)
    sel = jnp.take_along_axis(exp_logits, g_idx[..., None, None], axis=2)[..., 0, :]
    top_v, top_i = lax.top_k(sel, TOP_K_IN_GROUP)
    top_w = jax.nn.softmax(top_v, axis=-1) * p_g
    expert_id = g_idx[..., None] * EXPERTS_PER_GROUP + top_i
    combine = jnp.sum(jax.nn.one_hot(expert_id, N_EXPERTS, dtype=jnp.float32)
                      * top_w[..., None], axis=2)
    gate = jnp.einsum("btd,edf->btef", h, w_exp_gate)
    up = jnp.einsum("btd,edf->btef", h, w_exp_up)
    act = jax.nn.silu(gate) * up * combine[..., None].astype(h.dtype)
    return jnp.einsum("btef,efd->btd", act, w_exp_down)

def trunk_layer(x, c, prefix, pos0, w_ada, b_ada, g_pre_mix, g_post_mix, g_pre_ffn,
                g_post_ffn, w_in, ln_v_g, ln_v_b, w_spatial, b_spatial, w_pool,
                pool_scale, w_out, w_router_grp, b_router_grp, w_router_exp,
                b_router_exp, w_exp_gate, w_exp_up, w_exp_down):
    mod = jnp.einsum("bd,de->be", jax.nn.silu(c), w_ada) + b_ada
    sh1, sc1, gt1, sh2, sc2, gt2 = [m[:, None, :] for m in jnp.split(mod, N_MOD, axis=-1)]
    h = rms_norm(x, g_pre_mix) * (1 + sc1) + sh1
    y, new_pool, v = token_mixers(h, prefix, pos0, w_in, ln_v_g, ln_v_b, w_spatial,
                                  b_spatial, w_pool, pool_scale, w_out)
    x = x + gt1 * rms_norm(y, g_post_mix)
    h2 = rms_norm(x, g_pre_ffn) * (1 + sc2) + sh2
    f = hier_moe(h2, w_router_grp, b_router_grp, w_router_exp, b_router_exp,
                 w_exp_gate, w_exp_up, w_exp_down)
    x = x + gt2 * rms_norm(f, g_post_ffn)
    return x, new_pool, v

def setup_inputs(seed: int = 0) -> dict:
    key = jax.random.key(seed)
    ks = jax.random.split(key, 32)
    f32 = jnp.float32
    nrm = lambda k, shape, s: jax.random.normal(k, shape, f32) * s
    gain = lambda k, shape: 1.0 + 0.1 * jax.random.normal(k, shape, f32)
    L = DEPTH
    return {
        "x_prompt": nrm(ks[0], (BATCH, SEQ, D_MODEL), 1.0),
        "x_sample": nrm(ks[1], (DEC_BATCH, DEC_SEQ, D_MODEL), 1.0),
        "c_prompt": nrm(ks[2], (BATCH, D_MODEL), 1.0),
        "c_sample": nrm(ks[3], (DEC_BATCH, D_MODEL), 1.0),
        "state_pool": nrm(ks[4], (L, DEC_BATCH, POOL_STATE, B_WIDTH), 1.0),
        "w_ada": nrm(ks[5], (L, D_MODEL, N_MOD * D_MODEL), 0.3 * D_MODEL ** -0.5),
        "b_ada": nrm(ks[6], (L, N_MOD * D_MODEL), 0.02),
        "g_pre_mix": gain(ks[7], (L, D_MODEL)),
        "g_post_mix": gain(ks[8], (L, D_MODEL)),
        "g_pre_ffn": gain(ks[9], (L, D_MODEL)),
        "g_post_ffn": gain(ks[10], (L, D_MODEL)),
        "w_in": nrm(ks[11], (L, D_MODEL, PROJ_COLS), D_MODEL ** -0.5),
        "ln_v_g": gain(ks[12], (L, A_WIDTH)),
        "ln_v_b": nrm(ks[13], (L, A_WIDTH), 0.02),
        "w_spatial": nrm(ks[14], (L, A_HEADS, CHUNK, CHUNK), CHUNK ** -0.5),
        "b_spatial": gain(ks[15], (L, A_HEADS, CHUNK)),
        "w_pool": nrm(ks[16], (L, POOL_GROUPS, B_GROUP_DIM, B_OUT_GROUP), B_GROUP_DIM ** -0.5),
        "pool_scale": gain(ks[17], (L, D_MODEL)),
        "w_out": nrm(ks[18], (L, D_MODEL, D_MODEL), D_MODEL ** -0.5),
        "w_router_grp": nrm(ks[19], (L, D_MODEL, N_EXPERT_GROUPS), D_MODEL ** -0.5),
        "b_router_grp": nrm(ks[20], (L, N_EXPERT_GROUPS), 0.01),
        "w_router_exp": nrm(ks[21], (L, D_MODEL, N_EXPERTS), D_MODEL ** -0.5),
        "b_router_exp": nrm(ks[22], (L, N_EXPERTS), 0.01),
        "w_exp_gate": nrm(ks[23], (L, N_EXPERTS, D_MODEL, D_EXPERT), D_MODEL ** -0.5),
        "w_exp_up": nrm(ks[24], (L, N_EXPERTS, D_MODEL, D_EXPERT), D_MODEL ** -0.5),
        "w_exp_down": nrm(ks[25], (L, N_EXPERTS, D_EXPERT, D_MODEL), D_EXPERT ** -0.5),
    }

def reference(x_prompt, x_sample, c_prompt, c_sample, state_pool, w_ada, b_ada,
              g_pre_mix, g_post_mix, g_pre_ffn, g_post_ffn, w_in, ln_v_g, ln_v_b,
              w_spatial, b_spatial, w_pool, pool_scale, w_out, w_router_grp,
              b_router_grp, w_router_exp, b_router_exp, w_exp_gate, w_exp_up,
              w_exp_down):
    xp = x_prompt
    xs = x_sample
    pool_p, pool_s, v_s = [], [], []
    for l in range(DEPTH):
        w = (w_ada[l], b_ada[l], g_pre_mix[l], g_post_mix[l], g_pre_ffn[l],
             g_post_ffn[l], w_in[l], ln_v_g[l], ln_v_b[l], w_spatial[l], b_spatial[l],
             w_pool[l], pool_scale[l], w_out[l], w_router_grp[l], b_router_grp[l],
             w_router_exp[l], b_router_exp[l], w_exp_gate[l], w_exp_up[l],
             w_exp_down[l])
        empty = jnp.zeros((xp.shape[0], 0, B_WIDTH), xp.dtype)
        xp, np_state, _ = trunk_layer(xp, c_prompt, empty, 0, *w)
        xs, ns_state, vs = trunk_layer(xs, c_sample, state_pool[l], PAST_LEN, *w)
        pool_p.append(np_state)
        pool_s.append(ns_state)
        v_s.append(vs)
    state_pool_prompt = jnp.stack(pool_p, axis=0)
    state_pool_sample = jnp.stack(pool_s, axis=0)
    chunk_v_sample = jnp.stack(v_s, axis=0)
    return (xp, xs, state_pool_prompt, state_pool_sample, chunk_v_sample)


_drawn_inputs = setup_inputs


def setup_inputs(seed=0):
    import zlib

    import numpy as np

    out = dict(_drawn_inputs(seed))
    spreads = {}
    factors = {'g_post_ffn': 3.259,
     'ln_v_b': 2.774,
     'b_spatial': 2.685,
     'b_router_grp': 5.039,
     'b_router_exp': 4.071}
    for name, (base, spread) in spreads.items():
        noise = np.random.default_rng([zlib.crc32(name.encode()), seed]).standard_normal(out[name].shape)
        drawn = base * np.exp(spread * noise) if base else spread * noise
        out[name] = __import__('jax').numpy.asarray(drawn.astype(out[name].dtype))
    for name, factor in factors.items():
        out[name] = (out[name] * factor).astype(out[name].dtype)
    return out
```

```python
from contextlib import ExitStack

import concourse.bass as bass
from concourse import mybir

F32 = mybir.dt.float32
F32R = mybir.dt.float32r
BF16 = mybir.dt.bfloat16
U32 = mybir.dt.uint32
ALU = mybir.AluOpType
ACT = mybir.ActivationFunctionType
AX_X = mybir.AxisListType.X

P = 128
EPS = 1e-6
PAST_ALL = 1 << 20


def wait(eng, sem, value):
    if isinstance(value, int) and value <= 0:
        return
    eng.wait_ge(sem, value)


def wait_apart(eng, sem, value, passed):
    eng.wait_ge(sem, value)
    eng.sem_inc(passed, 1)


def wait_apart_if(eng, sem, value, passed):
    if isinstance(value, int) and value <= 0:
        return
    wait_apart(eng, sem, value, passed)


def run_steps(eng, step, first, last, loop_from, loop_to, many=2):
    assert (loop_to - loop_from) % many == 0
    for q in range(first, loop_from):
        step(q, q % many, q // many, False)
    with eng.Fori(0, (loop_to - loop_from) // many) as i:
        for s in range(many):
            q0 = loop_from + s
            step(i * many + q0, q0 % many, i + q0 // many, True)
    for q in range(loop_to, last):
        step(q, q % many, q // many, False)


class Place:

    def __init__(self, nc, at, end):
        self.nc, self.at, self.end = nc, at, end

    def __call__(self, name, shape, dt):
        size = mybir.dt.size(dt)
        for n in shape[1:]:
            size *= n
        t = self.nc.alloc_sbuf_tensor_at(name, shape, dt, offset=self.at)
        self.at += (size + 31) // 32 * 32
        assert self.at <= self.end, (name, self.at, self.end)
        return t


def trunk_step(nc, x_prompt, x_sample, c_prompt, c_sample, state_pool, w_ada, b_ada, g_pre_mix,
               g_post_mix, g_pre_ffn, g_post_ffn, w_in, ln_v_g, ln_v_b, w_spatial, b_spatial, w_pool,
               pool_scale, w_out, w_router_grp, b_router_grp, w_router_exp, b_router_exp,
               w_exp_gate, w_exp_up, w_exp_down, y_prompt, y_sample, pool_prompt, pool_sample,
               chunk_v):
    _, SEQ, D = x_prompt.shape
    NS = x_sample.shape[0]
    KD = D // P
    NT = SEQ // P
    TOK = SEQ + NS
    NC = NS + 1
    PRM = NS
    AW = D
    BW = state_pool.shape[3]
    PST = state_pool.shape[2]
    NG = BW // P
    HD = w_spatial.shape[1]
    NMOD = w_ada.shape[2] // P
    NQ = NT + 1
    assert HD == KD == NT == 8 and NG == 4

    xp = x_prompt.rearrange("b (t p) d -> (b t) p d", p=P)
    xs = x_sample.rearrange("b s d -> (b s) d")
    w_in_k = w_in[0].rearrange("(k p) n -> p k n", p=P)
    w_ada_k = w_ada[0].rearrange("(k p) n -> p k n", p=P)

    v_dram = nc.dram_tensor("v_normed", [NT, P, AW], F32).ap()
    NE = w_exp_gate.shape[1]
    FE = w_exp_gate.shape[3]
    NGR = w_router_grp.shape[2]
    EPG = NE // NGR
    NL = 8 + NE
    SLOTS = NQ * P
    h2_dram = nc.dram_tensor("h2", [TOK, D], F32).ap()
    list_dram = nc.dram_tensor("token_lists", [SLOTS * NE, 2], U32).ap()
    out_dram = nc.dram_tensor("expert_outs", [2 * TOK, D], F32).ap()
    merged_dram = nc.dram_tensor("merged", [KD, P, SEQ], F32).ap()

    with ExitStack() as ctx:
        def sem(name):
            return ctx.enter_context(nc.semaphore(name))

        def sems(name, n):
            return [sem(f"{name}{i}") for i in range(n)]

        HG = 4
        BASE = (nc.sbuf_base + 31) // 32 * 32
        END = nc.sbuf_usable_end // 32 * 32
        keep = Place(nc, BASE, BASE + 14336)

        ident = keep("ident", [P, P], F32)
        vecT = keep("vecT", [P, NMOD + 5 * KD], F32)
        cT = keep("cT", [P, KD, NC], F32)
        modT = keep("modT", [P, NMOD, NC], F32)
        A1T = keep("A1T", [P, KD, NC], F32)
        ss = keep("ss", [P, 2], F32)
        ms = keep("ms", [P, 2], F32)
        rstd = keep("rstd", [P, 2], F32)
        bn6 = keep("bn6", [P, 2, 6], F32)
        mv = keep("mv", [P, 2], F32)
        ve = keep("ve", [P, 1], F32)
        vr = keep("vr", [P, 1], F32)
        mhalf = keep("mhalf", [P, 1], F32)
        inv_n = keep("inv_n", [P, 16], F32)
        invc = keep("invc", [P, 16], F32)
        psh = keep("psh", [P, KD], F32)
        w00 = keep("w00", [NS, HD], F32)
        w00d = keep("w00d", [NS, HD, NS], F32)
        mergedS = keep("mergedS", [P, KD, NS], F32)

        rowsT = keep("rowsT", [P, 4, KD, NC], F32)
        sel = keep("sel", [NC, P], F32)
        wr = keep("wr", [P, KD, NL], F32)
        biasr = keep("biasr", [P, NL], F32)
        iota8 = keep("iota8", [P, 8], F32)
        upper = keep("upper", [P, P], BF16)
        ones = keep("ones", [P, P], BF16)
        lg = keep("lg", [P, NL], F32)
        gtop = keep("gtop", [P, 8], F32)
        gix = keep("gix", [P, 8], U32)
        gid = keep("gid", [P, 1], F32)
        ohg = keep("ohg", [P, NGR], F32)
        t32 = keep("t32", [P, NE], F32)
        s8 = keep("s8", [P, 8], F32)
        etop = keep("etop", [P, 8], F32)
        eix = keep("eix", [P, 8], U32)
        ei = keep("ei", [P, 2], F32)
        oh12 = keep("oh12", [P, 2, 8], F32)
        m12 = keep("m12", [P, 2, NE], F32)
        mb = keep("mb", [P, NE], BF16)
        mrun = keep("mrun", [P, NE], BF16)
        ngm = keep("ngm", [P, 1], F32)
        exg = keep("exg", [P, NGR], F32)
        se = keep("se", [P, 1], F32)
        dm = keep("dm", [P, 1], F32)
        e12 = keep("e12", [P, 1], F32)
        pg = keep("pg", [P, 1], F32)
        e1 = keep("e1", [P, 1], F32)
        rw = keep("rw", [P, 1], F32)
        wts = keep("wts", [P, NQ, 2], F32)
        eid = keep("eid", [P, 2], F32)
        mp = keep("mp", [P, 2, NE], F32)
        pos = keep("pos", [P, 2], F32)
        lrow = [keep(f"lrow{i}", [P, 1], U32) for i in range(2)]
        tid = keep("tid", [P, 1], F32)
        tidu = keep("tidu", [P, 2, 2], U32)
        none_u = keep("none_u", [P, NQ * NE * 2], U32)
        lst = keep("lst", [P, NE, 2], U32)
        idx = [keep(f"idx{i}", [P, 2], U32) for i in range(HG)]
        most = keep("most", [P, 1], F32)
        most_u = keep("most_u", [P, 1], U32)
        ss2 = keep("ss2", [P, 4], F32)
        ms2 = keep("ms2", [P, 4], F32)
        rs2 = keep("rs2", [P, 4], F32)

        big = Place(nc, keep.end, END)
        hT_hi = big("hT_hi", [P, KD, TOK], F32R)
        lo_at = big.at
        hT_lo = big("hT_lo", [P, KD, TOK], F32R)
        early = Place(nc, lo_at, big.at)
        adaV = early("adaV", [P, 4, KD, 256], F32)

        v = Place(nc, big.at, END)
        wv_hi = v("wv_hi", [P, KD, AW], F32R)
        wv_lo = v("wv_lo", [P, KD, AW], F32R)
        wv_raw = v("wv_raw", [P, 2, AW], F32)
        lng = v("lng", [P, AW], F32)
        lnb = v("lnb", [P, AW], F32)
        xbuf = v("xbuf", [P, 2, D], F32)
        xn = v("xn", [P, D], F32)
        h = v("h", [P, KD, P], F32)
        ht_hi = [v(f"ht_hi{i}", [P, KD, P], F32R) for i in range(2)]
        ht_lo = [v(f"ht_lo{i}", [P, KD, P], F32R) for i in range(2)]
        vg = v("vg", [P, 2, AW], F32)
        early = Place(nc, keep.end, lo_at)
        c9 = early("c9", [NC, D], F32)
        sc9 = early("sc9", [NC, D], F32)
        vecs = early("vecs", [NMOD + 5 * KD, P], F32)

        f = Place(nc, big.at, END)
        wraw = f("wraw", [P, 3, KD, P], F32)
        w_hi = [f(f"w_hi{i}", [P, KD, P], F32R) for i in range(2)]
        w_lo = [f(f"w_lo{i}", [P, KD, P], F32R) for i in range(2)]
        adaF = f("adaF", [P, 4, KD, 256], F32)
        dT = f("dT", [P, NG, TOK], F32)
        bsb = f("bsb", [P, HD, P], F32)
        wsT = f("wsT", [P, HD, P], F32)
        pooling = Place(nc, f.at, f.at + 5 * 4096)
        pT = [pooling(f"pT{i}", [P, 16 + SEQ], F32) for i in range(2)]
        pa = pooling("pa", [P, 16 + SEQ], F32)
        pb = pooling("pb", [P, 16 + SEQ], F32)
        u = f("u", [P, SEQ], F32)
        ta = f("ta", [P, SEQ], F32)
        tb = f("tb", [P, SEQ], F32)
        m0 = f("m0", [P, SEQ], F32)
        yb1 = f("yb1", [P, SEQ], F32)
        pooling = Place(nc, f.at, f.at + 2 * 4096)
        ws = pooling("ws", [P, HD, P], F32)
        spr = pooling("spr", [NS * PST, BW], F32)
        spT = pooling("spT", [P, NG, NS * PST], F32)
        mg = f("mg", [P, 2, SEQ], F32)
        vf = f("vf", [P, 2, NT, P], F32)
        vfs = f("vfs", [NS, 2, P], F32)
        wpl = f("wpl", [P, 2, P], F32)
        psm = f("psm", [P, NG, NS], F32)
        pws = f("pws", [P, NG, NS], F32)
        ptail = f("ptail", [P, NG, PST], F32)
        ptok = f("ptok", [PST, BW], F32)
        pstok = f("pstok", [NS, BW], F32)
        fix = f("fix", [P, 16], F32)
        smp = f("smp", [P, 5, KD, NS], F32)
        w = Place(nc, keep.end, END)
        x2 = w("x2", [P, NQ, D], F32)
        rws = w("rws", [NC, 4, D], F32)
        G2b = w("G2b", [P, D], F32)
        ring_at = w.at
        wo_hi = w("wo_hi", [P, KD, D], F32R)
        wo_lo = w("wo_lo", [P, KD, D], F32R)
        wo_raw = w("wo_raw", [P, 2, D], F32)
        mt = w("mt", [P, 2, KD, P], F32)
        mt_hi = [w(f"mt_hi{i}", [P, KD, P], F32R) for i in range(2)]
        mt_lo = [w(f"mt_lo{i}", [P, KD, P], F32R) for i in range(2)]
        moe_at = w.at
        xw = w("xw", [P, 2, D], F32)
        G1b = w("G1b", [P, D], F32)
        A2b = w("A2b", [P, D], F32)
        B2b = w("B2b", [P, D], F32)
        yt = w("yt", [P, D], F32)
        h2 = w("h2buf", [P, 2, D], F32)
        h2T = w("h2T", [P, 2, KD, P], F32)

        RING = 8
        e = Place(nc, ring_at, moe_at)
        wgu = [e(f"wgu{i}", [P, 2, KD, FE], F32) for i in range(RING)]
        wd = [e(f"wd{i}", [P, D], F32) for i in range(RING)]
        e = Place(nc, moe_at, END)
        hg = [e(f"hg{i}", [P, D], F32) for i in range(HG)]
        hgT = [e(f"hgT{i}", [P, KD, P], F32) for i in range(2)]
        ysb = e("ysb", [P, 2, D], F32)
        sil = e("sil", [P, 2, FE], F32)
        actv = e("actv", [P, 2, FE], F32)
        actT = e("actT", [P, 2, P], F32)
        e = Place(nc, ring_at, moe_at)
        yg = e("yg", [P, 2, 2, D], F32)
        f1 = e("f1", [P, 2, D], F32)
        ff = e("ff", [P, 2, D], F32)
        fj = e("fj", [P, D], F32)
        fo = e("fo", [P, 2, D], F32)

        PS = ctx.enter_context(nc.psum_tensor("PS", [P, 8, 512], F32))

        def banks(a, n):
            return PS[:, a:a + n, :].rearrange("p b n -> p (b n)")

        rowsT_made = sem("rowsT_made")
        rows_tr = sem("rows_tr")
        rows_made = sem("rows_made")
        prep_made = sem("prep_made")
        consts = sem("consts")
        bc_mm = sem("bc_mm")
        bc_made = sem("bc_made")
        mt_in = sems("mt_in", 2)
        y_mm = sem("y_mm")
        y_scaled = sem("y_scaled")
        x2_made = sem("x2_made")
        h2_scaled = sem("h2_scaled")
        h2_made = sem("h2_made")
        h2_out = sems("h2_out", 2)
        h2_tr = sem("h2_tr")
        h2T_made = sem("h2T_made")
        lg_mm = sem("lg_mm")
        lg_made = sem("lg_made")
        mp_made = sem("mp_made")
        eid_made = sem("eid_made")
        wts_made = sem("wts_made")
        route = sem("route")
        exp_made = sem("exp_made")
        exp2_made = sem("exp2_made")
        m_made = sem("m_made")
        pos_mm = sem("pos_mm")
        mrun_made = sem("mrun_made")
        slot_step = sem("slot_step")
        slot_made = sem("slot_made")
        scat = sem("scat")
        cnt_mm = sem("cnt_mm")
        cnt_made = sem("cnt_made")
        lst_in = sem("lst_in")
        hg_zero = sem("hg_zero")
        idx_made = sem("idx_made")
        hg_in = sems("hg_in", HG)
        we_in = sems("we_in", RING)
        hg_tr = sem("hg_tr")
        hgT_a = sem("hgT_a")
        hgT_b = sem("hgT_b")
        gu_mm = sem("gu_mm")
        silu_made = sem("silu_made")
        act_made = sem("act_made")
        act_tr = sem("act_tr")
        actT_made = sem("actT_made")
        down_mm = sem("down_mm")
        ysb_made = sem("ysb_made")
        eo_out = sems("eo_out", 2)
        o_in = sem("o_in")
        o_gather = sem("o_gather")
        o_pe = sem("o_pe")
        o_act = sem("o_act")
        o_dve = sem("o_dve")
        o_out = sem("o_out")
        f1_made = sem("f1_made")
        f_made = sem("f_made")
        f_scaled = sem("f_scaled")
        fo_made = sem("fo_made")
        y_out = sems("y_out", 2)
        vec_in = sem("vec_in")
        passed = sem("passed")
        state_out = sem("state_out")
        pool_passed = sem("pool_passed")
        sp_tr = sem("sp_tr")
        vfs_in = sems("vfs_in", 2)
        small_in = sem("small_in")
        later_in = sem("later_in")
        c_silu = sem("c_silu")
        pre_tr = sem("pre_tr")
        pre_cp = sem("pre_cp")
        ada_in = sems("ada_in", 4)
        ada_mm = sem("ada_mm")
        mod_made = sem("mod_made")
        x_in = sems("x_in", 2)
        sum_made = sem("sum_made")
        sum_mean = sem("sum_mean")
        sum_root = sem("sum_root")
        x_normed = sem("x_normed")
        xT_made = sem("xT_made")
        h_scaled = sem("h_scaled")
        h_made = sem("h_made")
        ht_hi_made = sem("ht_hi_made")
        ht_lo_made = sem("ht_lo_made")
        hT_kept = sem("hT_kept")
        w_in_rows = sems("w_in_rows", 2)
        w_hi_k = sem("w_hi_k")
        w_lo_k = sem("w_lo_k")
        v_mm = sem("v_mm")
        v_gelu = sem("v_gelu")
        v_bn = sem("v_bn")
        sum2_made = sem("sum2_made")
        sum2_mean = sem("sum2_mean")
        sum2_root = sem("sum2_root")
        v_step = sem("v_step")
        v_made = sem("v_made")
        v_out = sems("v_out", 2)
        fc_in = sem("fc_in")
        ws_masked = sem("ws_masked")
        ws_tr = sem("ws_tr")
        ws_cp = sem("ws_cp")
        w_inn = sems("w_inn", 3)
        w_hi_made = sem("w_hi_made")
        w_lo_made = sem("w_lo_made")
        blk_mm = sem("blk_mm")
        p_cp = sem("p_cp")
        p_step = sem("p_step")
        p_done = sem("p_done")
        dS_made = sem("dS_made")
        tail_tr = sem("tail_tr")
        tail_cp = sem("tail_cp")
        u_made = sem("u_made")
        ta_made = sem("ta_made")
        tb_made = sem("tb_made")
        mix_mm = sem("mix_mm")
        yb_mm = sem("yb_mm")
        m0_made = sem("m0_made")
        m1_made = sem("m1_made")
        m2_made = sem("m2_made")
        yb1_made = sem("yb1_made")
        mg_made = sem("mg_made")
        mg_out = sems("mg_out", 2)
        vf_in = sems("vf_in", 2)
        wpl_in = sems("wpl_in", 2)
        smp_act = sem("smp_act")
        merged_s_made = sem("merged_s_made")
        st_out = sem("st_out")

        WCOL = {"p": 2 * AW, "u": 0, "ga": 2 * AW + BW, "gb": 2 * AW + BW + D}
        CH = 256
        CPM = CH // P
        NADA_V = 2 * D // CH
        NADA_F = NMOD // CPM - NADA_V
        VEC = {n: NMOD + KD * i for i, n in enumerate(
            ("pre_mix", "post_mix", "pre_ffn", "post_ffn", "pool_scale"))}
        NV = NMOD + 5 * KD
        SMP = {"u": 0, "ga": 1, "gb": 2, "mix": 3, "yb": 4}
        S_BANK, MOD_BANK = 6, 7
        REGION = {"u": 0, "ga": 2, "mix": 4, "gb": 0, "yb": 2}
        ONE, TWO = 1, 2
        LISTS = list_dram.rearrange("(s e) o -> s (e o)", e=NE)
        RC, SC = 16, 2
        LATER = 16 * 8
        X_IN = (16 * ((NQ + 1) // 2), 16 * (NQ // 2))
        ROWS_OUT = 16 * (NE // 2)

        def rows_of(q, looped):
            return NS if not looped and q == 0 else P

        def f_over(eng):
            eng.wait_ge(blk_mm, NG + 3 * HD)
            eng.wait_ge(yb_mm, HD + TWO)
            eng.wait_ge(mod_made, NADA_V + HD)
            eng.wait_ge(merged_s_made, 1)
            eng.wait_ge(mg_out[0], 16 * (HD // 2))
            eng.wait_ge(mg_out[1], 16 * (HD // 2))
            eng.wait_ge(st_out, 32)

        block = ctx.enter_context(nc.Block())

        @block.sync
        def _(sp):
            def ada_chunk(n, slot, ring):
                wait(sp, ada_mm, n - 3)
                sp.dma_start(ring[:, slot], w_ada_k[:, :, bass.ds(n * CH, CH)]).then_inc(ada_in[slot], 16)

            def x_tile(q, par, half, looped):
                wait(sp, x_normed, q - 1)
                if not looped and q == 0:
                    sp.dma_start(xbuf[0:NS, par, :], xs).then_inc(x_in[par], 16)
                else:
                    sp.dma_start(xbuf[:, par, :], xp[bass.ds(q - 1, 1)].rearrange("a p d -> p (a d)")
                                 ).then_inc(x_in[par], 16)

            def v_store(q, par, looped):
                wait(sp, v_made, q + 1)
                if not looped and q == 0:
                    sp.dma_start(chunk_v[0, :, 0, :], vg[0:NS, par, :]).then_inc(v_out[par], 16)
                else:
                    sp.dma_start(v_dram[bass.ds(q - 1, 1)].rearrange("a p d -> p (a d)"),
                                 vg[:, par, :]).then_inc(v_out[par], 16)

            for n in range(4):
                ada_chunk(n, n % 4, adaV)
            x_tile(0, 0, 0, False)
            x_tile(1, 1, 0, False)
            for n in range(4, NADA_V):
                ada_chunk(n, n % 4, adaV)
            for k in range(KD):
                wait(sp, w_lo_k, k - 1)
                sp.dma_start(wv_raw[:, k % 2, :], w_in_k[:, k, AW:2 * AW]).then_inc(w_in_rows[k % 2], 16)

            def step(q, par, half, looped):
                if looped or q < NQ:
                    x_tile(q, par, half, looped)
                if looped or q >= 3:
                    v_store(q - 3, 1 - par, looped)

            run_steps(sp, step, 2, NQ + 3, 4, 8)

            sp.wait_ge(v_mm, NQ)
            sp.wait_ge(hT_kept, 2 * NQ)
            sp.wait_ge(v_out[0], 16 * 5)
            sp.wait_ge(v_out[1], 16 * 4)
            sp.dma_start(bsb[:, :, :], b_spatial.to_broadcast([P, HD, P])).then_inc(fc_in, 16)
            sp.dma_start(ws[:, :, :], w_spatial[0].rearrange("h i j -> i h j")).then_inc(fc_in, 16)
            sp.dma_start(spr[:, :], state_pool[0].rearrange("b r c -> (b r) c")).then_inc(fc_in, 16)

            def load_block(n, slot, col):
                wait(sp, w_lo_made, n - 2)
                sp.dma_start(wraw[:, slot], w_in_k[:, :, col]).then_inc(w_inn[slot], 16)

            for g in range(NG):
                load_block(g, g % 3, bass.ds(WCOL["p"] + g * P, P))

            def f_step(q, par, half, looped):
                for j, part in enumerate(("u", "ga", "gb")):
                    load_block(q * 3 + (NG + j), (NG + j) % 3, bass.ds(q * P + WCOL[part], P))
                sp.wait_ge(mix_mm, q + 1)
                sp.dma_start(vf[:, par], v_dram[:, :, bass.ds(q * P, P)].rearrange("t p c -> p t c")
                             ).then_inc(vf_in[par], 16)
                sp.dma_start(vfs[:, par], chunk_v[0, :, 0, bass.ds(q * P, P)]).then_inc(vfs_in[par], 16)
                sp.wait_ge(yb_mm, q + 1)
                sp.dma_start(wpl[:, par], w_pool[0, bass.ds(half, 1), :, par * P:(par + 1) * P]
                             .rearrange("g c o -> c (g o)")).then_inc(wpl_in[par], 16)
                for a in range(2):
                    ada_chunk(q * 2 + (NADA_V + a), 2 * par + a, adaF)

            run_steps(sp, f_step, 0, HD, 0, HD - 2)
            sp.wait_ge(tail_cp, 1)
            sp.dma_start(pool_prompt[0, 0], ptok[:, :]).then_inc(st_out, 16)
            sp.dma_start(pool_sample[0, :, PST - 1, :], pstok[:, :]).then_inc(st_out, 16)

            f_over(sp)
            for k in range(KD):
                wait(sp, w_lo_k, KD + k - 1 if k >= 2 else 0)
                sp.dma_start(wo_raw[:, k % 2, :], w_out[0, k * P:(k + 1) * P, :]).then_inc(w_in_rows[k % 2], 16)

            def load_x(q, par, looped):
                wait(sp, x2_made, q - 1)
                if not looped and q == 0:
                    sp.dma_start(xw[0:NS, par, :], xs).then_inc(x_in[par], 16)
                else:
                    sp.dma_start(xw[:, par, :], xp[bass.ds(q - 1, 1)].rearrange("a p d -> p (a d)")
                                 ).then_inc(x_in[par], 16)

            def load_m(q, par, looped):
                wait(sp, ht_lo_made, q + (NQ - 1) if looped or q >= 2 else 0)
                sp.dma_start(mt[:, par], merged_dram[:, :, bass.ds((q - 1) * P, P)]
                             .rearrange("k p t -> p k t")).then_inc(mt_in[par], 16)

            def store_h2(q, par, looped):
                r = rows_of(q, looped)
                sp.wait_ge(h2_made, q + 1)
                dst = h2_dram[SEQ:TOK, :] if r == NS else (
                    h2_dram[0:SEQ, :].rearrange("(t p) d -> t p d", p=P)[bass.ds(q - 1, 1)]
                    .rearrange("t p d -> p (t d)"))
                sp.dma_start(dst, h2[0:r, par, :]).then_inc(h2_out[par], 16)

            def w_step(q, par, half, looped):
                if looped or q + 1 < NQ:
                    load_m(q + 1, 1 - par, looped)
                if looped or q >= 1:
                    store_h2(q - 1, 1 - par, looped or q > 1)
                if looped or q + 1 < NQ:
                    load_x(q + 1, 1 - par, looped)

            load_x(0, 0, False)
            run_steps(sp, w_step, 0, NQ + 1, 2, 8)

            sp.wait_ge(y_mm, NQ)
            sp.wait_ge(ht_lo_made, 2 * NQ)

            def load_expert(n, s, uses, looped):
                wait(sp, down_mm, n - (RING - 1))
                one = bass.ds(n, 1)
                sp.dma_start(wgu[s][:, 0], w_exp_gate[0, one].rearrange("a (p k) f -> p (a k) f", k=KD)
                             ).then_inc(we_in[s], 16)
                sp.dma_start(wgu[s][:, 1], w_exp_up[0, one].rearrange("a (p k) f -> p (a k) f", k=KD)
                             ).then_inc(we_in[s], 16)
                sp.dma_start(wd[s][:, :], w_exp_down[0, one].rearrange("a f d -> f (a d)")
                             ).then_inc(we_in[s], 16)

            load_expert(0, 0, 0, False)
            sp.wait_ge(scat, 32 * NQ)
            sp.dma_start(lst[:, :], LISTS[0:P, :]).then_inc(lst_in, 16)
            for n in range(1, RING):
                load_expert(n, n, 0, False)
            run_steps(sp, load_expert, RING, NE, RING, NE, RING)

            sp.wait_ge(down_mm, NE)
            sp.wait_ge(cnt_made, 2)
            for par in range(2):
                sp.wait_ge(eo_out[par], ROWS_OUT)
            fullest = sp.value_load(most_u[0:1, 0:1], min_val=0, max_val=TOK)
            with sp.If(fullest > P):
                with sp.Fori(1, NQ) as c:
                    with sp.Fori(0, NE) as x:
                        one = bass.ds(x, 1)
                        sp.dma_start(idx[0][:, :], LISTS[bass.ds(c * P, P), bass.ds(x * 2, 2)]).then_inc(o_in, 16)
                        sp.dma_start(wgu[0][:, 0], w_exp_gate[0, one].rearrange("a (p k) f -> p (a k) f", k=KD)
                                     ).then_inc(o_in, 16)
                        sp.dma_start(wgu[0][:, 1], w_exp_up[0, one].rearrange("a (p k) f -> p (a k) f", k=KD)
                                     ).then_inc(o_in, 16)
                        sp.dma_start(wd[0][:, :], w_exp_down[0, one].rearrange("a f d -> f (a d)")
                                     ).then_inc(o_in, 16)
                        wait_apart(sp, o_out, ((c - 1) * NE + x) * 16 + 16, passed)

            def load_y(q, par, half, looped):
                wait(sp, f_made, q - 1)
                r = rows_of(q, looped)
                if r == NS:
                    src = out_dram[2 * SEQ:2 * TOK, :].rearrange("(p k) d -> p (k d)", k=2)
                else:
                    src = out_dram[0:2 * SEQ, :].rearrange("(t p k) d -> t p (k d)", p=P, k=2)[
                        bass.ds(q - 1, 1)].rearrange("t p d -> p (t d)")
                sp.dma_start(yg[0:r, par].rearrange("p k d -> p (k d)"), src).then_inc(x_in[par], 16)

            load_y(0, 0, 0, False)
            load_y(1, 1, 0, False)

            def store_y(q, par, half, looped):
                if looped or q + 2 < NQ:
                    load_y(q + 2, par, half + 1, looped or True)
                sp.wait_ge(fo_made, q + 1)
                if not looped and q == 0:
                    sp.dma_start(y_sample.rearrange("b s d -> (b s) d"), fo[0:NS, par, :]).then_inc(y_out[par], 16)
                else:
                    sp.dma_start(y_prompt[0, bass.ds((q - 1) * P, P), :], fo[:, par, :]).then_inc(y_out[par], 16)

            run_steps(sp, store_y, 0, NQ, 1, NQ - 2)
            sp.wait_ge(y_out[0], 16 * 5)
            sp.wait_ge(y_out[1], 16 * 4)
            sp.wait_ge(st_out, 32)
            sp.wait_ge(state_out, 16)
            sp.wait_ge(v_out[0], 16 * 5)

        @block.gpsimd
        def _(pool):
            pool.memset(ident[:, :], 0.0).then_inc(consts, 1)
            pool.wait_ge(consts, 1)
            pool.affine_select(out=ident[:, :], in_=ident[:, :], compare_op=ALU.not_equal, fill=1.0,
                               base=0, pattern=[[-1, P]], channel_multiplier=1).then_inc(consts, 1)
            pool.memset(mhalf[:, :], -0.5)
            pool.iota(inv_n[:, :], pattern=[[1, 16]], base=1, channel_multiplier=0,
                      allow_small_or_imprecise_dtypes=True)
            pool.iota(iota8[:, :], pattern=[[1, 8]], base=0, channel_multiplier=0,
                      allow_small_or_imprecise_dtypes=True)
            pool.iota(tid[:, :], pattern=[[0, 1]], base=SEQ, channel_multiplier=1,
                      allow_small_or_imprecise_dtypes=True)
            pool.memset(sel[:, :], 0.0)
            pool.memset(upper[:, :], 1.0)
            pool.memset(ones[:, :], 1.0)
            pool.memset(mrun[:, :], 0.0)
            pool.memset(wr[:, :, :], 0.0)
            pool.memset(none_u[:, :], PAST_ALL)
            pool.memset(biasr[:, :], -3e38).then_inc(consts, 1)
            pool.wait_ge(consts, 3)
            pool.affine_select(out=sel[:, :], in_=sel[:, :], compare_op=ALU.not_equal, fill=1.0,
                               base=-NS, pattern=[[0, P]], channel_multiplier=1)
            pool.affine_select(out=upper[:, :], in_=upper[:, :], compare_op=ALU.is_gt, fill=0.0,
                               base=0, pattern=[[1, P]], channel_multiplier=-1).then_inc(consts, 1)

            def root(n, src, tmp, scale, made, tmp_made, out, out_made):
                wait_apart(pool, made, n + 1, pool_passed)
                pool.tensor_scalar(tmp, src, scale, EPS, ALU.mult, ALU.add).then_inc(tmp_made, 1)
                pool.wait_ge(tmp_made, n + 1)
                pool.tensor_tensor(out, tmp, mhalf[0:tmp.shape[0], :], ALU.pow).then_inc(out_made, 1)

            def x_root(q, par, looped):
                rows = NS if not looped and q == 0 else P
                root(q, ss[0:rows, par:par + 1], ms[0:rows, par:par + 1], 1.0 / D, sum_made, sum_mean,
                     rstd[0:rows, par:par + 1], sum_root)

            def v_root(q, looped):
                rows = NS if not looped and q == 0 else P
                root(q, mv[0:rows, 1:2], ve[0:rows, :], 1.0, sum2_made, sum2_mean, vr[0:rows, :], sum2_root)

            def keep_h(q, par, looped):
                wait(pool, ht_lo_made, q + 1)
                if not looped and q == 0:
                    for src, dst in ((ht_hi, hT_hi), (ht_lo, hT_lo)):
                        pool.tensor_copy(dst[:, :, SEQ:TOK], src[par][:, :, 0:NS].bitcast(F32)).then_inc(hT_kept, 1)
                else:
                    at = bass.ds((q - 1) * P, P)
                    for src, dst in ((ht_hi, hT_hi), (ht_lo, hT_lo)):
                        pool.tensor_copy(dst[:, :, at], src[par][:, :, :].bitcast(F32)).then_inc(hT_kept, 1)

            def step(q, par, half, looped):
                if looped or q + 1 < NQ:
                    x_root(q + 1, 1 - par, looped)
                if looped or 2 <= q:
                    if looped or q - 2 < NQ:
                        v_root(q - 2, looped)
                if looped or q < NQ:
                    keep_h(q, par, looped)

            x_root(0, 0, False)
            run_steps(pool, step, 0, NQ + 2, 4, 8)

            pool.wait_ge(fc_in, 48)
            pool.affine_select(out=ws[:, :, :], in_=ws[:, :, :], compare_op=ALU.is_ge, fill=0.0, base=0,
                               pattern=[[0, HD], [-1, P]], channel_multiplier=1).then_inc(ws_masked, 1)
            pool.dma_start(pool_sample[0, :, 0:PST - 1, :], state_pool[0, :, 1:PST, :]).then_inc(state_out, 16)
            def f_step(q, par, half, looped):
                pool.wait_ge(mg_made, q + 1)
                pool.dma_start(merged_dram[bass.ds(q, 1)].rearrange("a p t -> p (a t)"),
                               mg[:, par, :]).then_inc(mg_out[par], 16)

            run_steps(pool, f_step, 0, HD, 0, HD - 2)

            def y_root(q, par, looped):
                r = rows_of(q, looped)
                root(q + NQ, ss2[0:r, par:par + 1], ms2[0:r, par:par + 1], 1.0 / D, sum_made, sum_mean,
                     rs2[0:r, par:par + 1], sum_root)

            def x2_root(q, par, looped):
                r = rows_of(q, looped)
                c = slice(2 + par, 3 + par)
                root(q + NQ, ss2[0:r, c], ms2[0:r, c], 1.0 / D, sum2_made, sum2_mean, rs2[0:r, c], sum2_root)

            def scatter(q, looped):
                r = rows_of(q, looped)
                wait_apart(pool, slot_made, q + 1, pool_passed)
                for k in range(2):
                    pool.indirect_dma_start(list_dram, bass.IndirectOffsetOnAxis(lrow[k][0:r, :], 0),
                                            tidu[0:r, k, :], None).then_inc(scat, 16)

            def w_step(q, par, half, looped):
                if looped or 1 <= q <= NQ:
                    y_root(q - 1, 1 - par, looped or q > 1)
                    x2_root(q - 1, 1 - par, looped or q > 1)
                if looped or q >= 3:
                    scatter(q - 3, looped or q > 3)

            pool.wait_ge(later_in, LATER)
            run_steps(pool, w_step, 0, NQ + 3, 4, 8)

            pool.wait_ge(lg_mm, NQ)
            pool.wait_ge(h2_out[0], 16 * 5)
            pool.wait_ge(h2_out[1], 16 * 4)
            for t in hg:
                z = pool.memset(t[:, :], 0.0)
            z.then_inc(hg_zero, 1)
            pool.wait_ge(hg_zero, 1)
            pool.wait_ge(lst_in, 16)

            def gather(n, s, oct_):
                par = s % HG
                if not isinstance(n, int) or n >= HG:
                    wait_apart(pool, eo_out[s % 2], (n // 2 - (HG // 2 - 1)) * 16 if isinstance(n, int)
                               else oct_ * (16 * RING // 2) + 16 * (s // 2 - (HG // 2 - 1)), pool_passed)
                pool.tensor_copy(idx[par][:, :], lst[:, bass.ds(n, 1), :].rearrange("p a b -> p (a b)")
                                 ).then_inc(idx_made, 1)
                wait_apart_if(pool, hg_tr, n - (HG - 1), pool_passed)
                wait_apart(pool, idx_made, n + 1, pool_passed)
                pool.indirect_dma_start(hg[par][:, :], None, h2_dram,
                                        bass.IndirectOffsetOnAxis(idx[par][:, 0:1], 0),
                                        bounds_check=TOK - 1, oob_is_err=False).then_inc(hg_in[par], 16)

            def answer(n, s):
                wait_apart(pool, ysb_made, n + 1, pool_passed)
                pool.indirect_dma_start(out_dram, bass.IndirectOffsetOnAxis(idx[s % HG][:, 1:2], 0),
                                        ysb[:, s % 2, :], None,
                                        bounds_check=2 * TOK - 1, oob_is_err=False).then_inc(eo_out[s % 2], 16)

            def e_step(n, s, oct_, looped):
                if looped or n < NE:
                    gather(n, s, oct_)
                if looped or n >= 2:
                    answer(n - 2, s + RING - 2)

            run_steps(pool, e_step, 0, NE + 2, RING, NE, RING)

            pool.wait_ge(cnt_made, 2)
            for j in range(HG):
                pool.wait_ge(hg_in[j], 16 * (NE // HG))
            for par in range(2):
                pool.wait_ge(eo_out[par], ROWS_OUT)
            fullest = pool.value_load(most_u[0:1, 0:1], min_val=0, max_val=TOK)
            with pool.If(fullest > P):
                with pool.Fori(1, NQ) as c:
                    with pool.Fori(0, NE) as x:
                        m = (c - 1) * NE + x
                        wait_apart(pool, o_in, m * 64 + 64, pool_passed)
                        pool.indirect_dma_start(hg[0][:, :], None, h2_dram,
                                                bass.IndirectOffsetOnAxis(idx[0][:, 0:1], 0),
                                                bounds_check=TOK - 1, oob_is_err=False).then_inc(o_gather, 16)
                        wait_apart(pool, o_dve, m * 4 + 4, pool_passed)
                        pool.indirect_dma_start(out_dram, bass.IndirectOffsetOnAxis(idx[0][:, 1:2], 0),
                                                ysb[:, 0, :], None,
                                                bounds_check=2 * TOK - 1, oob_is_err=False).then_inc(o_out, 16)
                        wait_apart(pool, o_out, m * 16 + 16, pool_passed)

            def f_root(q, par, looped):
                r = rows_of(q, looped)
                root(q + 2 * NQ, ss[0:r, par:par + 1], ms[0:r, par:par + 1], 1.0 / D, sum_made, sum_mean,
                     rstd[0:r, par:par + 1], sum_root)

            run_steps(pool, lambda q, par, half, looped: f_root(q, par, looped), 0, NQ, 1, NQ)

        @block.scalar
        def _(act):
            act.dma_start(c9[0:NS, :], c_sample).then_inc(small_in, 16)
            act.dma_start(c9[NS:NC, :], c_prompt).then_inc(small_in, 16)
            act.dma_start(vecs[0:NMOD, :], b_ada.rearrange("o (m p) -> (o m) p", p=P)).then_inc(vec_in, 16)
            for n, g in (("pre_mix", g_pre_mix), ("post_mix", g_post_mix), ("pre_ffn", g_pre_ffn),
                         ("post_ffn", g_post_ffn), ("pool_scale", pool_scale)):
                act.dma_start(vecs[VEC[n]:VEC[n] + KD, :], g.rearrange("o (k p) -> (o k) p", p=P)
                              ).then_inc(vec_in, 16)
            act.wait_ge(consts, 3)
            act.dma_start(wr[:, :, 0:NGR], w_router_grp[0].rearrange("(p k) g -> p k g", k=KD)).then_inc(later_in, 16)
            act.dma_start(wr[:, :, 8:NL], w_router_exp[0].rearrange("(p k) g -> p k g", k=KD)).then_inc(later_in, 16)
            act.dma_start(biasr[:, 0:NGR], b_router_grp.to_broadcast([P, NGR])).then_inc(later_in, 16)
            act.dma_start(biasr[:, 8:NL], b_router_exp.to_broadcast([P, NE])).then_inc(later_in, 16)
            act.dma_start(list_dram.rearrange("(p n) o -> p (n o)", p=P), none_u[:, :]).then_inc(later_in, 16)
            act.dma_start(lng[:, :], ln_v_g.to_broadcast([P, AW])).then_inc(later_in, 16)
            act.dma_start(lnb[:, :], ln_v_b.to_broadcast([P, AW])).then_inc(later_in, 16)
            with nc.allow_non_contiguous_dma(reason="eight numbers, for eight partitions"):
                act.dma_start(w00[:, :], w_spatial[:, :, 0, 0].to_broadcast([NS, HD])).then_inc(later_in, 16)
            act.wait_ge(small_in, 32)
            act.activation(sc9[:, :], c9[:, :], ACT.Silu).then_inc(c_silu, 1)

            def x_norm(q, par, half, looped):
                rows = NS if not looped and q == 0 else P
                wait(act, x_in[par], half * 16 + 16)
                wait(act, xT_made, q)
                act.activation(xn[0:rows, :], xbuf[0:rows, par, :], ACT.Square,
                               accum_out=ss[0:rows, par:par + 1]).then_inc(sum_made, 1)
                wait(act, sum_root, q + 1)
                act.activation(xn[0:rows, :], xbuf[0:rows, par, :], ACT.Copy,
                               scale=rstd[0:rows, par:par + 1]).then_inc(x_normed, 1)

            def h_high(q, par, looped):
                cols = NS if not looped and q == 0 else P
                wait(act, h_made, q + 1)
                wait(act, v_mm, q - 1)
                wait(act, hT_kept, q * 2 - 2)
                act.activation(ht_hi[par][:, :, 0:cols], h[:, :, 0:cols], ACT.Copy).then_inc(ht_hi_made, 1)

            def v_gelu_of(q, par, half, looped):
                rows = NS if not looped and q == 0 else P
                wait(act, v_mm, q + 1)
                wait(act, v_out[par], half * 16)
                act.activation(vg[0:rows, par, :], banks(2 + 2 * par, 2)[0:rows, :], ACT.Gelu_apprx_tanh
                               ).then_inc(v_gelu, 1)

            x_norm(0, 0, 0, False)
            x_norm(1, 1, 0, False)
            for k in range(KD):
                act.wait_ge(w_in_rows[k % 2], 16 * (k // 2 + 1))
                act.activation(wv_hi[:, k, :], wv_raw[:, k % 2, :], ACT.Copy).then_inc(w_hi_k, 1)

            def step(q, par, half, looped):
                if looped or q >= 2:
                    v_gelu_of(q - 2, par, half - 1, looped)
                if looped or q < NQ:
                    h_high(q, par, looped)
                if looped or 1 <= q < NQ - 1:
                    x_norm(q + 1, 1 - par, half + par, looped)

            run_steps(act, step, 0, NQ + 2, 4, 8)

            def high(n, slot, count, hslot):
                act.wait_ge(w_inn[slot], count * 16 + 16)
                wait(act, blk_mm, n - 1)
                act.activation(w_hi[hslot][:, :, :], wraw[:, slot], ACT.Copy).then_inc(w_hi_made, 1)

            act.wait_ge(v_made, NQ)
            act.wait_ge(v_mm, NQ)
            for g in range(NG):
                high(g, g % 3, g // 3, g % 2)
                act.wait_ge(blk_mm, g + 1)
                wait(act, p_done, g - 1)
                act.activation(pT[g % 2][:, 16:16 + SEQ], banks(2 * (g % 2), 2), ACT.Copy).then_inc(p_cp, 1)

            def part_high(q, par, j):
                high(q * 3 + (NG + j), (NG + j) % 3, q + (NG + j) // 3, (NG + 3 * par + j) % 2)

            act.sem_inc(tb_made, ONE)
            part_high(0, 0, 0)

            def f_step(q, par, half, looped):
                part_high(q, par, 1)
                act.wait_ge(blk_mm, q * 3 + (NG + 1))
                act.wait_ge(m1_made, q + ONE)
                act.activation(u[:, :], banks(REGION["u"], 2), ACT.Gelu_apprx_tanh).then_inc(u_made, 1)
                part_high(q, par, 2)
                act.wait_ge(blk_mm, q * 3 + (NG + 2))
                act.wait_ge(m2_made, q + ONE)
                act.activation(ta[:, :], banks(REGION["ga"], 2), ACT.Tanh, scale=0.5).then_inc(ta_made, 1)
                if looped or q + 1 < HD:
                    part_high(q + 1, 1 - par, 0)
                act.wait_ge(blk_mm, q * 3 + (NG + 3))
                act.wait_ge(yb1_made, q + ONE)
                act.activation(tb[:, :], banks(REGION["gb"], 2), ACT.Tanh, scale=0.5).then_inc(tb_made, 1)

            run_steps(act, f_step, 0, HD, 0, HD - 2)

            def smp_ps(name):
                return PS[:, S_BANK, SMP[name] * KD * NS:(SMP[name] + 1) * KD * NS]

            act.wait_ge(yb_mm, HD + TWO)
            flat = smp[:, :, :, :].rearrange("p a k n -> p a (k n)")
            act.activation(flat[:, 0], smp_ps("u"), ACT.Gelu_apprx_tanh).then_inc(smp_act, 1)
            act.activation(flat[:, 1], smp_ps("ga"), ACT.Tanh, scale=0.5).then_inc(smp_act, 1)
            act.activation(flat[:, 2], smp_ps("gb"), ACT.Tanh, scale=0.5).then_inc(smp_act, 1)

            f_over(act)
            for k in range(KD):
                act.wait_ge(w_in_rows[k % 2], 16 * (KD // 2 + k // 2 + 1))
                act.activation(wo_hi[:, k, :], wo_raw[:, k % 2, :], ACT.Copy).then_inc(w_hi_k, 1)

            def m_high(q, par, half, looped):
                wait(act, y_mm, q - 1)
                if not looped and q == 0:
                    src, cols = mergedS[:, :, :], NS
                else:
                    act.wait_ge(mt_in[par], (half + par) * 16)
                    src, cols = mt[:, par], P
                act.activation(mt_hi[par][:, :, 0:cols], src, ACT.Copy).then_inc(ht_hi_made, 1)

            def y_square(q, par, looped):
                r = rows_of(q, looped)
                wait_apart(act, y_mm, q + 1, passed)
                act.activation(x2[0:r, bass.ds(q, 1), :].rearrange("p a d -> p (a d)"), banks(2 * par, 2)[0:r, :],
                               ACT.Square, accum_out=ss2[0:r, par:par + 1]).then_inc(sum_made, 1)

            def x2_square(q, par, half, looped):
                r = rows_of(q, looped)
                wait_apart_if(act, h2_out[par], half * 16, passed)
                wait_apart_if(act, h2_tr, q - 1, passed)
                wait_apart(act, x2_made, q + 1, passed)
                act.activation(h2[0:r, par, :], x2[0:r, bass.ds(q, 1), :].rearrange("p a d -> p (a d)"),
                               ACT.Square, accum_out=ss2[0:r, 2 + par:3 + par]).then_inc(sum2_made, 1)

            def h2_turned(q, par, looped):
                cols = rows_of(q, looped)
                act.wait_ge(h2_tr, q + 1)
                wait(act, lg_mm, q - 1)
                act.activation(h2T[:, par, :, 0:cols],
                               banks(4, 2)[:, 0:KD * cols].rearrange("p (k n) -> p k n", n=cols), ACT.Copy
                               ).then_inc(h2T_made, 1)

            def exps(q, looped):
                r = rows_of(q, looped)
                act.wait_ge(route, q * RC + 11)
                act.activation(exg[0:r, :], lg[0:r, 0:NGR], ACT.Exp, bias=ngm[0:r, :],
                               accum_out=se[0:r, :]).then_inc(exp_made, 1)
                act.activation(e12[0:r, :], dm[0:r, :], ACT.Exp).then_inc(exp2_made, 1)

            m_high(0, 0, 0, False)

            def w_step(q, par, half, looped):
                if looped or 1 <= q <= NQ:
                    y_square(q - 1, 1 - par, looped or q > 1)
                if looped or q >= 3:
                    exps(q - 3, looped or q > 3)
                if looped or 1 <= q <= NQ:
                    x2_square(q - 1, 1 - par, half - (1 - par), looped or q > 1)
                if looped or q + 1 < NQ:
                    m_high(q + 1, 1 - par, half + par, looped or True)
                if looped or 2 <= q <= NQ + 1:
                    h2_turned(q - 2, par, looped or q > 2)

            run_steps(act, w_step, 0, NQ + 3, 4, 8)

            act.wait_ge(lg_mm, NQ)

            def turned_b(n, s):
                par = s % 2
                act.wait_ge(hg_tr, n + 1)
                wait(act, gu_mm, n - 1)
                act.activation(hgT[par][:, 4:8, :].rearrange("p k n -> p (k n)"), PS[:, 1, :], ACT.Copy
                               ).then_inc(hgT_b, 1)

            def store_e(n, s, uses):
                par = s % 2
                act.wait_ge(down_mm, n + 1)
                wait(act, eo_out[par], uses * 16)
                act.activation(ysb[:, par, :], banks(5, 2), ACT.Copy).then_inc(ysb_made, 1)

            def e_step(n, s, oct_, looped):
                par = s % 2
                if looped or n < NE:
                    act.wait_ge(gu_mm, n + 1)
                    wait(act, act_made, n - 1)
                    act.activation(sil[:, par, :], PS[:, 2 + par, 0:FE], ACT.Silu).then_inc(silu_made, 1)
                if looped or n + 1 < NE:
                    turned_b(n + 1, s + 1)
                if looped or n >= 1:
                    store_e(n - 1, s + 1, oct_ * (RING // 2) + (s - 1) // 2)

            turned_b(0, 0)
            run_steps(act, e_step, 0, NE + 1, RING, NE - RING, RING)

            act.wait_ge(cnt_made, 2)
            fullest = act.value_load(most_u[0:1, 0:1], min_val=0, max_val=TOK)
            with act.If(fullest > P):
                with act.Fori(1, NQ) as c:
                    with act.Fori(0, NE) as x:
                        act.wait_ge(o_pe, ((c - 1) * NE + x) * 4 + 2)
                        act.activation(sil[:, 0, :], PS[:, 2, 0:FE], ACT.Silu).then_inc(o_act, 1)

            def f1_of(q, par, half, looped):
                r = rows_of(q, looped)
                wait_apart(act, x_in[par], half * 16 + (2 * X_IN[par] + 16), passed)
                wait_apart_if(act, f_made, q - 1, passed)
                act.activation(f1[0:r, par, :], yg[0:r, par, 0, :], ACT.Copy, scale=wts[0:r, bass.ds(q, 1), 0]
                               ).then_inc(f1_made, 1)

            f1_of(0, 0, 0, False)

            def end_step(q, par, half, looped):
                r = rows_of(q, looped)
                if looped or q + 1 < NQ:
                    f1_of(q + 1, 1 - par, half + par, looped or True)
                act.wait_ge(f_made, q + 1)
                act.activation(fj[0:r, :], ff[0:r, par, :], ACT.Square, accum_out=ss[0:r, par:par + 1]
                               ).then_inc(sum_made, 1)

            run_steps(act, end_step, 0, NQ, 2, 8)

        @block.vector
        def _(dve):
            dve.wait_ge(pre_tr, KD)
            dve.tensor_copy(cT[:, :, :].rearrange("p k n -> p (k n)"), PS[:, 6, 0:KD * NC]).then_inc(pre_cp, 1)
            dve.wait_ge(pre_tr, KD + 1)
            dve.tensor_copy(vecT[:, :], PS[:, 7, 0:NV]).then_inc(pre_cp, 1)

            def mod_chunks(n, many, bank):
                dve.wait_ge(ada_mm, n + many)
                rows = many * CPM
                at = bass.ds(n * CPM, rows)
                dve.tensor_tensor(modT[:, at, :],
                                  PS[:, bank, 0:rows * NC].rearrange("p (m n) -> p m n", n=NC),
                                  vecT[:, at].unsqueeze(2).to_broadcast([P, rows, NC]), ALU.add
                                  ).then_inc(mod_made, 1)

            dve.wait_ge(pre_cp, 2)
            for n in range(NADA_V):
                mod_chunks(n, 1, 2 + n % 4)
            dve.wait_ge(mod_made, NADA_V)
            dve.scalar_tensor_tensor(A1T[:, :, :], modT[:, KD:2 * KD, :], 1.0,
                                     vecT[:, VEC["pre_mix"]:VEC["pre_mix"] + KD].unsqueeze(2)
                                     .to_broadcast([P, KD, NC]), ALU.add, ALU.mult).then_inc(prep_made, 1)
            dve.tensor_scalar(psh[:, :], vecT[:, VEC["pool_scale"]:VEC["pool_scale"] + KD], 0.5, None,
                              ALU.mult).then_inc(prep_made, 1)
            dve.wait_ge(later_in, LATER)
            dve.wait_ge(consts, 2)
            dve.tensor_tensor(w00d[:, :, :], w00[:, :].unsqueeze(2).to_broadcast([NS, HD, NS]),
                              ident[0:NS, 0:NS].unsqueeze(1).to_broadcast([NS, HD, NS]), ALU.mult
                              ).then_inc(prep_made, 1)
            dve.reciprocal(invc[:, :], inv_n[:, :]).then_inc(prep_made, 1)
            for k in range(KD):
                dve.wait_ge(w_hi_k, k + 1)
                dve.tensor_tensor(wv_lo[:, k, :], wv_raw[:, k % 2, :], wv_hi[:, k, :].bitcast(F32),
                                  ALU.subtract).then_inc(w_lo_k, 1)
            dve.wait_ge(prep_made, 1)

            def h_of(q, par, looped):
                sample = not looped and q == 0
                cols = NS if sample else P
                sl = slice(0, NS) if sample else slice(PRM, PRM + 1)
                ps = banks(0, 2)[:, 0:KD * cols].rearrange("p (k n) -> p k n", n=cols)
                wait(dve, xT_made, q + 1)
                wait(dve, ht_lo_made, q)
                dve.tensor_tensor(h[:, :, 0:cols], ps, A1T[:, :, sl].to_broadcast([P, KD, cols]), ALU.mult
                                  ).then_inc(h_scaled, 1)
                dve.wait_ge(h_scaled, q + 1)
                dve.tensor_tensor(h[:, :, 0:cols], h[:, :, 0:cols],
                                  modT[:, 0:KD, sl].to_broadcast([P, KD, cols]), ALU.add
                                  ).then_inc(h_made, 1)

            def h_low(q, par, looped):
                cols = NS if not looped and q == 0 else P
                wait(dve, ht_hi_made, q + 1)
                dve.tensor_tensor(ht_lo[par][:, :, 0:cols], h[:, :, 0:cols],
                                  ht_hi[par][:, :, 0:cols].bitcast(F32), ALU.subtract).then_inc(ht_lo_made, 1)

            def v_stats(q, par, looped):
                rows = NS if not looped and q == 0 else P
                wait(dve, v_gelu, q + 1)
                for j in range(2):
                    b = dve.bn_stats(bn6[0:rows, j, :], vg[0:rows, par, j * 512:(j + 1) * 512])
                b.then_inc(v_bn, 1)
                wait_apart(dve, v_bn, q + 1, passed)
                dve.bn_aggr(mv[0:rows, :], bn6[0:rows, :, :].rearrange("p a b -> p (a b)")).then_inc(sum2_made, 1)

            def v_norm(q, par, looped):
                rows = NS if not looped and q == 0 else P
                t = vg[0:rows, par, :]
                wait(dve, sum2_root, q + 1)
                dve.tensor_scalar(t, t, mv[0:rows, 0:1], vr[0:rows, :], ALU.subtract, ALU.mult
                                  ).then_inc(v_step, 1)
                dve.wait_ge(v_step, q * 2 + 1)
                dve.tensor_tensor(t, t, lng[0:rows, :], ALU.mult).then_inc(v_step, 1)
                dve.wait_ge(v_step, q * 2 + 2)
                dve.tensor_tensor(t, t, lnb[0:rows, :], ALU.add).then_inc(v_made, 1)

            dve.wait_ge(later_in, LATER)

            def step(q, par, half, looped):
                if looped or q < NQ:
                    h_of(q, par, looped)
                if looped or q >= 2:
                    v_stats(q - 2, par, looped)
                if looped or q < NQ:
                    h_low(q, par, looped)
                if looped or q >= 2:
                    v_norm(q - 2, par, looped)

            run_steps(dve, step, 0, NQ + 2, 4, 8)

            dve.wait_ge(v_mm, NQ)
            dve.wait_ge(hT_kept, 2 * NQ)
            dve.wait_ge(v_out[0], 16 * 5)
            dve.wait_ge(v_out[1], 16 * 4)
            for t in (*pT,):
                z = dve.memset(t[:, 0:16], 0.0)
            z.then_inc(p_step, 1)
            dve.wait_ge(p_step, 1)

            def low(n, slot, hslot):
                dve.wait_ge(w_hi_made, n + 1)
                dve.tensor_tensor(w_lo[hslot][:, :, :], wraw[:, slot], w_hi[hslot][:, :, :].bitcast(F32),
                                  ALU.subtract).then_inc(w_lo_made, 1)

            done = 1

            def link(ins):
                nonlocal done
                ins.then_inc(p_step, 1)
                done += 1
                dve.wait_ge(p_step, done)

            def pool_group(g):
                w = 2 << g
                src = pT[g % 2]
                dve.wait_ge(p_cp, g + 1)
                dve.tensor_copy(ptail[:, g, :], src[:, 16 + SEQ - PST:16 + SEQ])
                at, wide = src, 1
                while wide < w:
                    out = pa if at is not pa else pb
                    low_ = 2 * wide - 1
                    link(dve.tensor_tensor(out[:, low_:], at[:, low_:],
                                           at[:, low_ - wide:16 + SEQ - wide], ALU.add))
                    at, wide = out, 2 * wide
                dst = dT[:, g, 0:SEQ]
                link(dve.scalar_tensor_tensor(dst, at[:, 16:], 1.0 / w, src[:, 16:], ALU.mult, ALU.subtract))
                link(dve.tensor_tensor(fix[:, 0:w], at[:, 16:16 + w], invc[:, 0:w], ALU.mult))
                dve.tensor_tensor(dT[:, g, 0:w], fix[:, 0:w], src[:, 16:16 + w], ALU.subtract
                                  ).then_inc(p_done, 1)

            low(0, 0, 0)
            dve.wait_ge(prep_made, 4)
            for g in range(NG):
                if g + 1 < NG:
                    low(g + 1, (g + 1) % 3, (g + 1) % 2)
                if g == 0:
                    dve.wait_ge(sp_tr, 1)
                    dve.tensor_copy(spT[:, :, :].rearrange("p g n -> p (g n)"),
                                    PS[:, 4, 0:NG * NS * PST])
                    dve.wait_ge(ws_tr, 1)
                    dve.tensor_copy(wsT[:, 0:4, :].rearrange("p h n -> p (h n)"), PS[:, 5, :])
                    dve.wait_ge(ws_tr, 2)
                    dve.tensor_copy(wsT[:, 4:8, :].rearrange("p h n -> p (h n)"), PS[:, 7, :]
                                    ).then_inc(ws_cp, 1)
                pool_group(g)
            link(dve.tensor_copy(psm[:, :, :].rearrange("p g n -> p (g n)"),
                                 PS[:, S_BANK, 5 * KD * NS:5 * KD * NS + NG * NS]))
            for g in range(NG):
                w = 2 << g
                link(dve.tensor_reduce(pws[:, g, :], spT[:, g, :].rearrange("p (n r) -> p n r", r=PST)
                                       [:, :, PST - (w - 1):PST], AX_X, ALU.add))
            link(dve.tensor_tensor(pws[:, :, :], pws[:, :, :], psm[:, :, :], ALU.add))
            for g in range(NG):
                d = dve.scalar_tensor_tensor(dT[:, g, SEQ:TOK], pws[:, g, :], 1.0 / (2 << g), psm[:, g, :],
                                             ALU.mult, ALU.subtract)
            d.then_inc(dS_made, 1)
            dve.wait_ge(tail_tr, 2)
            dve.tensor_copy(ptok[:, :], PS[0:PST, 4, :])
            dve.tensor_copy(pstok[:, :], PS[0:NS, 5, :]).then_inc(tail_cp, 1)

            def part_low(q, par, j):
                low(q * 3 + (NG + j), (NG + j) % 3, (NG + 3 * par + j) % 2)

            for s in (yb1_made, m0_made, m1_made, m2_made):
                dve.sem_inc(s, ONE)
            part_low(0, 0, 0)

            def f_step(q, par, half, looped):
                part_low(q, par, 1)
                part_low(q, par, 2)
                dve.wait_ge(mix_mm, q + (1 + TWO))
                dve.tensor_tensor(m0[:, :].rearrange("p (t i) -> p t i", i=P),
                                  banks(REGION["mix"], 2).rearrange("p (t i) -> p t i", i=P),
                                  bsb[:, bass.ds(q, 1), :].to_broadcast([P, NT, P]), ALU.add
                                  ).then_inc(m0_made, 1)
                dve.wait_ge(m0_made, q + (1 + ONE))
                dve.wait_ge(u_made, q + 1)
                dve.scalar_tensor_tensor(m0[:, :], m0[:, :], 0.5, u[:, :], ALU.mult, ALU.mult
                                         ).then_inc(m1_made, 1)
                dve.wait_ge(m1_made, q + (1 + ONE))
                dve.wait_ge(ta_made, q + 1)
                dve.scalar_tensor_tensor(m0[:, :], ta[:, :], 1.0, m0[:, :], ALU.add, ALU.mult
                                         ).then_inc(m2_made, 1)
                if looped or q + 1 < HD:
                    part_low(q + 1, 1 - par, 0)
                dve.wait_ge(tb_made, q + (1 + ONE))
                dve.wait_ge(yb_mm, q + (1 + TWO))
                dve.scalar_tensor_tensor(yb1[:, :], tb[:, :], 1.0, banks(REGION["yb"], 2), ALU.add, ALU.mult
                                         ).then_inc(yb1_made, 1)
                dve.wait_ge(yb1_made, q + (1 + ONE))
                dve.wait_ge(m2_made, q + (1 + ONE))
                wait(dve, mg_out[par], half * 16)
                dve.scalar_tensor_tensor(mg[:, par, :], yb1[:, :], psh[:, bass.ds(q, 1)], m0[:, :],
                                         ALU.mult, ALU.add).then_inc(mg_made, 1)
                mod_chunks(q * 2 + NADA_V, 2, MOD_BANK)

            run_steps(dve, f_step, 0, HD, 2, HD - 2)

            def smp_ps(name):
                return PS[:, S_BANK, SMP[name] * KD * NS:(SMP[name] + 1) * KD * NS].rearrange(
                    "p (k n) -> p k n", n=NS)

            dve.wait_ge(smp_act, 3)
            link(dve.tensor_tensor(smp[:, 3], smp_ps("mix"), bsb[:, :, 0:1].to_broadcast([P, KD, NS]),
                                       ALU.add))
            link(dve.scalar_tensor_tensor(smp[:, 3], smp[:, 3], 0.5, smp[:, 0], ALU.mult, ALU.mult))
            link(dve.scalar_tensor_tensor(smp[:, 3], smp[:, 1], 1.0, smp[:, 3], ALU.add, ALU.mult))
            link(dve.scalar_tensor_tensor(smp[:, 4], smp[:, 2], 1.0, smp_ps("yb"), ALU.add, ALU.mult))
            link(dve.tensor_tensor(smp[:, 4], smp[:, 4],
                                       psh[:, :].unsqueeze(2).to_broadcast([P, KD, NS]), ALU.mult))
            dve.tensor_tensor(mergedS[:, :, :], smp[:, 3], smp[:, 4], ALU.add).then_inc(merged_s_made, 1)

            lo, hi = KD, 2 * KD
            g_ = {n: vecT[:, VEC[n]:VEC[n] + KD].unsqueeze(2).to_broadcast([P, KD, NC])
                  for n in ("post_mix", "pre_ffn", "post_ffn")}
            dve.wait_ge(mod_made, NADA_V + HD)
            dve.tensor_tensor(rowsT[:, 0], modT[:, 2 * KD:3 * KD, :], g_["post_mix"], ALU.mult)
            dve.scalar_tensor_tensor(rowsT[:, 1], modT[:, 4 * KD:5 * KD, :], 1.0, g_["pre_ffn"], ALU.add, ALU.mult)
            dve.tensor_copy(rowsT[:, 2], modT[:, 3 * KD:4 * KD, :])
            dve.tensor_tensor(rowsT[:, 3], modT[:, 5 * KD:6 * KD, :], g_["post_ffn"], ALU.mult).then_inc(rowsT_made, 1)
            f_over(dve)
            for a in range(4):
                dve.wait_ge(rows_tr, a + 1)
                dve.tensor_copy(rws[:, a, :], banks(2 * a, 2)[0:NC, :]).then_inc(rows_made, 1)
            for a, t in enumerate((G1b, A2b, B2b, G2b)):
                dve.wait_ge(bc_mm, a + 1)
                if a in (1, 2):
                    dve.tensor_copy(t[:, :].rearrange("q (k p) -> q p k", k=KD),
                                    banks(2 * a, 2).rearrange("q (p k) -> q p k", k=KD)).then_inc(bc_made, 1)
                else:
                    dve.tensor_copy(t[:, :], banks(2 * a, 2)).then_inc(bc_made, 1)
            for k in range(KD):
                dve.wait_ge(w_hi_k, KD + k + 1)
                dve.tensor_tensor(wo_lo[:, k, :], wo_raw[:, k % 2, :], wo_hi[:, k, :].bitcast(F32),
                                  ALU.subtract).then_inc(w_lo_k, 1)

            def m_low(q, par, looped):
                if not looped and q == 0:
                    src, cols = mergedS[:, :, :], NS
                else:
                    src, cols = mt[:, par], P
                dve.wait_ge(ht_hi_made, q + (NQ + 1))
                dve.tensor_tensor(mt_lo[par][:, :, 0:cols], src, mt_hi[par][:, :, 0:cols].bitcast(F32),
                                  ALU.subtract).then_inc(ht_lo_made, 1)

            def turned(ap):
                return ap.rearrange("q (p k) -> q k p", k=KD)

            def straight(ap):
                return ap.rearrange("q (k p) -> q k p", k=KD)

            def x2_at(q, r):
                return x2[0:r, bass.ds(q, 1), :].rearrange("p a d -> p (a d)")

            def residual(q, par, half, looped):
                r = rows_of(q, looped)
                g1 = rws[0:NS, 0, :] if r == NS else G1b[:, :]
                dve.wait_ge(sum_root, q + (NQ + 1))
                dve.scalar_tensor_tensor(yt[0:r, :], banks(2 * par, 2)[0:r, :], rs2[0:r, par:par + 1], g1,
                                         ALU.mult, ALU.mult).then_inc(y_scaled, 1)
                dve.wait_ge(y_scaled, q + 1)
                dve.wait_ge(x_in[par], half * 16 + (X_IN[par] + 16))
                dve.tensor_tensor(x2_at(q, r), yt[0:r, :], xw[0:r, par, :], ALU.add).then_inc(x2_made, 1)

            def modulate(q, par, looped):
                r = rows_of(q, looped)
                if r == NS:
                    a2, b2 = turned(rws[0:NS, 1, :]), turned(rws[0:NS, 2, :])
                else:
                    a2, b2 = straight(A2b[:, :]), straight(B2b[:, :])
                out = straight(h2[0:r, par, :])
                dve.wait_ge(sum2_root, q + (NQ + 1))
                dve.scalar_tensor_tensor(out, turned(x2_at(q, r)), rs2[0:r, 2 + par:3 + par], a2,
                                         ALU.mult, ALU.mult).then_inc(h2_scaled, 1)
                dve.wait_ge(h2_scaled, q + 1)
                dve.tensor_tensor(out, out, b2, ALU.add).then_inc(h2_made, 1)

            def chain(sm, base):
                n = 0

                def link(ins):
                    nonlocal n
                    n += 1
                    ins.then_inc(sm, 1)
                    wait_apart(dve, sm, base + n, passed)
                    return n
                return link

            def route_of(q, looped):
                r = rows_of(q, looped)
                link = chain(route, q * RC)
                dve.wait_ge(lg_mm, q + 1)
                dve.tensor_tensor(lg[0:r, :], PS[0:r, 6, 0:NL], biasr[0:r, :], ALU.add).then_inc(lg_made, 1)
                wait_apart(dve, lg_made, q + 1, passed)
                link(dve.max(gtop[0:r, :], lg[0:r, 0:8]))
                link(dve.max_index(gix[0:r, :], gtop[0:r, :], lg[0:r, 0:8]))
                link(dve.tensor_copy(gid[0:r, :], gix[0:r, 0:1]))
                link(dve.tensor_scalar(ohg[0:r, :], iota8[0:r, 0:NGR], gid[0:r, :], None, ALU.is_equal))
                link(dve.tensor_tensor(t32[0:r, :].rearrange("p (g e) -> p g e", e=EPG),
                                       lg[0:r, 8:NL].rearrange("p (g e) -> p g e", e=EPG),
                                       ohg[0:r, :].unsqueeze(2).to_broadcast([r, NGR, EPG]), ALU.mult))
                link(dve.tensor_reduce(s8[0:r, :], t32[0:r, :].rearrange("p (g e) -> p e g", e=EPG), AX_X, ALU.add))
                link(dve.max(etop[0:r, :], s8[0:r, :]))
                link(dve.max_index(eix[0:r, :], etop[0:r, :], s8[0:r, :]))
                link(dve.tensor_copy(ei[0:r, :], eix[0:r, 0:2]))
                link(dve.tensor_scalar(ngm[0:r, :], gtop[0:r, 0:1], -1.0, None, ALU.mult))
                link(dve.tensor_tensor(dm[0:r, :], etop[0:r, 1:2], etop[0:r, 0:1], ALU.subtract))
                link(dve.tensor_tensor(oh12[0:r, :, :], iota8[0:r, :].unsqueeze(1).to_broadcast([r, 2, 8]),
                                       ei[0:r, :].unsqueeze(2).to_broadcast([r, 2, 8]), ALU.is_equal))
                for j in range(2):
                    x = dve.tensor_tensor(m12[0:r, j, :].rearrange("p (g e) -> p g e", e=EPG),
                                          ohg[0:r, :].unsqueeze(2).to_broadcast([r, NGR, EPG]),
                                          oh12[0:r, j, :].unsqueeze(1).to_broadcast([r, NGR, EPG]), ALU.mult)
                n = link(x)
                assert n == 13
                dve.tensor_tensor(mb[0:r, :], m12[0:r, 0, :], m12[0:r, 1, :], ALU.add).then_inc(m_made, 1)
                dve.scalar_tensor_tensor(eid[0:r, :], gid[0:r, :].to_broadcast([r, 2]), float(EPG), ei[0:r, :],
                                         ALU.mult, ALU.add).then_inc(eid_made, 1)

            def weights_of(q, looped):
                r = rows_of(q, looped)
                wait_apart(dve, exp2_made, q + 1, passed)
                dve.tensor_scalar(e1[0:r, :], e12[0:r, :], 1.0, None, ALU.add)
                dve.reciprocal(pg[0:r, :], se[0:r, :]).then_inc(route, 1)
                wait_apart(dve, route, q * RC + 14, passed)
                dve.reciprocal(rw[0:r, :], e1[0:r, :]).then_inc(route, 1)
                wait_apart(dve, route, q * RC + 15, passed)
                dve.tensor_tensor(wts[0:r, bass.ds(q, 1), 0], rw[0:r, :], pg[0:r, :], ALU.mult).then_inc(route, 1)
                wait_apart(dve, route, q * RC + 16, passed)
                dve.tensor_tensor(wts[0:r, bass.ds(q, 1), 1], wts[0:r, bass.ds(q, 1), 0], e12[0:r, :], ALU.mult
                                  ).then_inc(wts_made, 1)

            def slots_of(q, looped):
                r = rows_of(q, looped)
                wait_apart(dve, pos_mm, q + 1, passed)
                dve.tensor_tensor(mp[0:r, :, :], PS[0:r, 7, 0:NE].unsqueeze(1).to_broadcast([r, 2, NE]),
                                  m12[0:r, :, :], ALU.mult).then_inc(mp_made, 1)
                dve.wait_ge(eid_made, q + 1)
                dve.tensor_tensor(mrun[0:r, :], mrun[0:r, :], mb[0:r, :], ALU.add).then_inc(mrun_made, 1)
                wait_apart(dve, mp_made, q + 1, passed)
                wait_apart_if(dve, scat, q * 32, passed)
                dve.tensor_copy(tidu[0:r, :, 0], tid[0:r, :].to_broadcast([r, 2]))
                for j in range(2):
                    dve.tensor_scalar(tidu[0:r, j, 1:2], tid[0:r, :], 2.0, float(j), ALU.mult, ALU.add)
                dve.tensor_reduce(pos[0:r, :], mp[0:r, :, :], AX_X, ALU.add).then_inc(slot_step, 1)
                wait_apart(dve, slot_step, q * SC + 1, passed)
                for j in range(2):
                    z = dve.scalar_tensor_tensor(lrow[j][0:r, :], pos[0:r, j:j + 1], float(NE), eid[0:r, j:j + 1],
                                                 ALU.mult, ALU.add)
                z.then_inc(slot_made, 1)
                dve.tensor_scalar(tid[:, :], tid[:, :], float(-SEQ if r == NS else P), None, ALU.add
                                  ).then_inc(slot_step, 1)
                wait_apart(dve, slot_step, q * SC + 2, passed)

            m_low(0, 0, False)
            dve.wait_ge(later_in, LATER)

            def w_step(q, par, half, looped):
                if looped or q >= 3:
                    route_of(q - 3, looped or q > 3)
                if looped or 1 <= q <= NQ:
                    residual(q - 1, 1 - par, half - (1 - par), looped or q > 1)
                if looped or q >= 3:
                    weights_of(q - 3, looped or q > 3)
                if looped or 1 <= q <= NQ:
                    modulate(q - 1, 1 - par, looped or q > 1)
                if looped or q + 1 < NQ:
                    m_low(q + 1, 1 - par, looped or True)
                if looped or q >= 3:
                    slots_of(q - 3, looped or q > 3)

            run_steps(dve, w_step, 0, NQ + 3, 4, 8)
            dve.wait_ge(cnt_mm, 1)
            dve.tensor_reduce(most[:, :], PS[:, 7, 0:NE], AX_X, ALU.max).then_inc(cnt_made, 1)
            dve.wait_ge(cnt_made, 1)
            dve.tensor_copy(most_u[:, :], most[:, :]).then_inc(cnt_made, 1)

            def turned_a(n, s):
                par = s % 2
                dve.wait_ge(hg_tr, n + 1)
                wait(dve, gu_mm, n - 1)
                dve.tensor_copy(hgT[par][:, 0:4, :].rearrange("p k n -> p (k n)"), PS[:, 0, :]).then_inc(hgT_a, 1)

            def e_step(n, s, oct_, looped):
                par = s % 2
                dve.wait_ge(silu_made, n + 1)
                wait(dve, act_tr, n - 1)
                dve.tensor_tensor(actv[:, par, :], PS[:, 2 + par, FE:2 * FE], sil[:, par, :], ALU.mult
                                  ).then_inc(act_made, 1)
                if looped or n + 1 < NE:
                    turned_a(n + 1, s + 1)
                dve.wait_ge(act_tr, n + 1)
                wait(dve, down_mm, n - 1)
                dve.tensor_copy(actT[:, par, :], PS[:, 4, 0:P]).then_inc(actT_made, 1)

            turned_a(0, 0)
            run_steps(dve, e_step, 0, NE, RING, NE - RING, RING)

            fullest = dve.value_load(most_u[0:1, 0:1], min_val=0, max_val=TOK)
            with dve.If(fullest > P):
                with dve.Fori(1, NQ) as c:
                    with dve.Fori(0, NE) as x:
                        m = (c - 1) * NE + x
                        dve.wait_ge(o_pe, m * 4 + 1)
                        dve.tensor_copy(hgT[0][:, :, :].rearrange("p k n -> p (k n)"), banks(0, 2)
                                        ).then_inc(o_dve, 1)
                        dve.wait_ge(o_act, m + 1)
                        dve.tensor_tensor(actv[:, 0, :], PS[:, 2, FE:2 * FE], sil[:, 0, :], ALU.mult
                                          ).then_inc(o_dve, 1)
                        dve.wait_ge(o_pe, m * 4 + 3)
                        dve.tensor_copy(actT[:, 0, :], PS[:, 4, 0:P]).then_inc(o_dve, 1)
                        dve.wait_ge(o_pe, m * 4 + 4)
                        dve.tensor_copy(ysb[:, 0, :], banks(5, 2)).then_inc(o_dve, 1)

            def end_step(q, par, half, looped):
                r = rows_of(q, looped)
                g2 = rws[0:NS, 3, :] if r == NS else G2b[:, :]
                dve.wait_ge(f1_made, q + 1)
                dve.wait_ge(x_in[par], half * 16 + (2 * X_IN[par] + 16))
                wait(dve, f_scaled, q - 1)
                dve.scalar_tensor_tensor(ff[0:r, par, :], yg[0:r, par, 1, :], wts[0:r, bass.ds(q, 1), 1],
                                         f1[0:r, par, :], ALU.mult, ALU.add).then_inc(f_made, 1)
                dve.wait_ge(sum_root, q + (2 * NQ + 1))
                wait(dve, y_out[par], half * 16)
                dve.scalar_tensor_tensor(fo[0:r, par, :], ff[0:r, par, :], rstd[0:r, par:par + 1], g2,
                                         ALU.mult, ALU.mult).then_inc(f_scaled, 1)
                dve.wait_ge(f_scaled, q + 1)
                dve.tensor_tensor(fo[0:r, par, :], fo[0:r, par, :], x2_at(q, r), ALU.add).then_inc(fo_made, 1)

            run_steps(dve, end_step, 0, NQ, 2, 8)

        @block.tensor
        def _(pe):
            pe.wait_ge(consts, 2)
            pe.wait_ge(c_silu, 1)
            for k in range(KD):
                pe.transpose(PS[:, 6, k * NC:(k + 1) * NC], sc9[:, k * P:(k + 1) * P], ident[0:NC, 0:NC]
                             ).then_inc(pre_tr, 1)
            pe.wait_ge(vec_in, 16 * 6)
            pe.transpose(PS[:, 7, 0:NV], vecs[:, :], ident[0:NV, 0:NV]).then_inc(pre_tr, 1)

            def ada_chunk(slot, ring, uses, bank, col):
                pe.wait_ge(ada_in[slot], uses * 16 + 16)
                for m in range(CPM):
                    at = col + m * NC
                    for k in range(KD):
                        mm = pe.matmul(PS[:, bank, at:at + NC], ring[:, slot, k, m * P:(m + 1) * P],
                                       cT[:, k, :], start=(k == 0), stop=(k == KD - 1))
                mm.then_inc(ada_mm, 1)

            def x_turn(q, looped):
                rows = NS if not looped and q == 0 else P
                wait(pe, x_normed, q + 1)
                wait(pe, h_scaled, q)
                for k in range(KD):
                    mm = pe.transpose(banks(0, 2)[:, k * rows:(k + 1) * rows], xn[0:rows, k * P:(k + 1) * P],
                                      ident[0:rows, 0:rows])
                mm.then_inc(xT_made, 1)

            def v_of(q, par, looped):
                rows = NS if not looped and q == 0 else P
                wait(pe, ht_lo_made, q + 1)
                wait(pe, v_gelu, q - 1)
                for half in range(2):
                    cols = slice(half * 512, (half + 1) * 512)
                    out = PS[0:rows, 2 + 2 * par + half, :]
                    n = 0
                    for k in range(KD):
                        for a, b in ((ht_hi, wv_hi), (ht_hi, wv_lo), (ht_lo, wv_hi)):
                            mm = pe.matmul(out, a[par][:, k, 0:rows], b[:, k, cols], start=(n == 0),
                                           stop=(n == 3 * KD - 1))
                            n += 1
                mm.then_inc(v_mm, 1)

            pe.wait_ge(pre_cp, 1)
            for n in range(NADA_V):
                wait(pe, mod_made, n - 3)
                ada_chunk(n % 4, adaV, n // 4, 2 + n % 4, 0)
            x_turn(0, False)
            pe.wait_ge(w_lo_k, KD)

            def step(q, par, half, looped):
                if looped or q < NQ:
                    x_turn(q, looped)
                v_of(q - 1, 1 - par, looped)

            run_steps(pe, step, 1, NQ + 1, 2, 8)

            pe.wait_ge(fc_in, 48)
            pe.wait_ge(v_gelu, NQ)
            for g in range(NG):
                mm = pe.transpose(PS[:, 4, g * NS * PST:(g + 1) * NS * PST], spr[:, g * P:(g + 1) * P],
                                  ident[0:NS * PST, 0:NS * PST])
            mm.then_inc(sp_tr, 1)
            pe.wait_ge(ws_masked, 1)
            for b, bank in ((0, 5), (1, 7)):
                for j in range(4):
                    mm = pe.transpose(PS[:, bank, j * P:(j + 1) * P], ws[:, 4 * b + j, :], ident[:, :])
                mm.then_inc(ws_tr, 1)

            def project(n, hslot, region, smp_at):
                pe.wait_ge(w_lo_made, n + 1)
                for k in range(KD):
                    for j, (a, b) in enumerate(((w_hi, hT_hi), (w_hi, hT_lo), (w_lo, hT_hi))):
                        st, sp_ = (k == 0 and j == 0), (k == KD - 1 and j == 2)
                        for half in range(2):
                            pe.matmul(PS[:, region + half, :], a[hslot][:, k, :],
                                      b[:, k, half * 512:(half + 1) * 512], start=st, stop=sp_)
                        mm = pe.matmul(PS[:, S_BANK, smp_at], a[hslot][:, k, :], b[:, k, SEQ:TOK],
                                       start=st, stop=sp_)
                mm.then_inc(blk_mm, 1)

            pe.wait_ge(hT_kept, 2 * NQ)
            for g in range(NG):
                wait(pe, p_cp, g - 1)
                at = 5 * KD * NS + g * NS
                project(g, g % 2, 2 * (g % 2), slice(at, at + NS))
            pe.wait_ge(p_done, NG)
            pe.wait_ge(dS_made, 1)
            pe.wait_ge(ws_cp, 1)
            for g in range(NG):
                mm = pe.transpose(PS[0:PST, 4, g * P:(g + 1) * P], ptail[:, g, :], ident[:, :])
            mm.then_inc(tail_tr, 1)
            for g in range(NG):
                mm = pe.transpose(PS[0:NS, 5, g * P:(g + 1) * P], psm[:, g, :], ident[:, :])
            mm.then_inc(tail_tr, 1)
            pe.wait_ge(tail_cp, 1)
            pe.wait_ge(prep_made, 3)
            pe.sem_inc(mix_mm, TWO)
            pe.sem_inc(yb_mm, TWO)

            def part(q, par, j, name):
                project(q * 3 + (NG + j), (NG + 3 * par + j) % 2, REGION[name],
                        bass.ds(q * NS + SMP[name] * KD * NS, NS))

            def f_step(q, par, half, looped):
                pe.wait_ge(tb_made, q + ONE)
                part(q, par, 0, "u")
                pe.wait_ge(yb1_made, q + ONE)
                part(q, par, 1, "ga")
                pe.wait_ge(vf_in[par], half * 16 + 16)
                pe.wait_ge(vfs_in[par], half * 16 + 16)
                pe.wait_ge(m0_made, q + ONE)
                for t in range(NT):
                    pe.matmul(banks(REGION["mix"], 2)[:, t * P:(t + 1) * P], vf[:, par, t, :],
                              wsT[:, bass.ds(q, 1), :].rearrange("p a i -> p (a i)"), start=True, stop=True)
                pe.matmul(PS[:, S_BANK, bass.ds(q * NS + SMP["mix"] * KD * NS, NS)], vfs[:, par, :],
                          w00d[:, bass.ds(q, 1), :].rearrange("p a i -> p (a i)"), start=True, stop=True
                          ).then_inc(mix_mm, 1)
                pe.wait_ge(u_made, q + 1)
                part(q, par, 2, "gb")
                pe.wait_ge(wpl_in[par], half * 16 + 16)
                pe.wait_ge(ta_made, q + 1)
                for j in range(2):
                    pe.matmul(PS[:, REGION["yb"] + j, :], wpl[:, par, :],
                              dT[:, bass.ds(half, 1), j * 512:(j + 1) * 512].rearrange("p a n -> p (a n)"),
                              start=True, stop=True)
                pe.matmul(PS[:, S_BANK, bass.ds(q * NS + SMP["yb"] * KD * NS, NS)], wpl[:, par, :],
                          dT[:, bass.ds(half, 1), SEQ:TOK].rearrange("p a n -> p (a n)"),
                          start=True, stop=True).then_inc(yb_mm, 1)
                pe.wait_ge(mod_made, q + NADA_V)
                for a in range(2):
                    ada_chunk(2 * par + a, adaF, half + NADA_V // 4, MOD_BANK, a * CPM * NC)

            run_steps(pe, f_step, 0, HD, 0, HD - 2)

            pe.wait_ge(rowsT_made, 1)
            pe.wait_ge(consts, 4)
            pe.wait_ge(smp_act, 3)
            pe.wait_ge(merged_s_made, 1)
            for a in range(4):
                for k in range(KD):
                    mm = pe.transpose(banks(2 * a, 2)[0:NC, k * P:(k + 1) * P], rowsT[:, a, k, :], ident[:, :])
                mm.then_inc(rows_tr, 1)
            for a in range(4):
                pe.wait_ge(rows_made, a + 1)
                for half in range(2):
                    mm = pe.matmul(PS[:, 2 * a + half, :], sel[:, :], rws[:, a, half * 512:(half + 1) * 512],
                                   start=True, stop=True)
                mm.then_inc(bc_mm, 1)
            pe.wait_ge(bc_made, 4)

            def y_half(q, par, half, looped):
                r = rows_of(q, looped)
                n = 0
                for k in range(KD):
                    if half == 0 and not looped and q == 0:
                        pe.wait_ge(w_lo_k, KD + k + 1)
                    for a, b in ((mt_hi, wo_hi), (mt_hi, wo_lo), (mt_lo, wo_hi)):
                        mm = pe.matmul(PS[0:r, 2 * par + half, :], a[par][:, k, 0:r],
                                       b[:, k, half * 512:(half + 1) * 512], start=(n == 0), stop=(n == 3 * KD - 1))
                        n += 1
                return mm

            def h2_turn(q, par, looped):
                r = rows_of(q, looped)
                pe.wait_ge(h2_made, q + 1)
                wait(pe, h2T_made, q)
                for k in range(KD):
                    mm = pe.transpose(banks(4, 2)[:, k * r:(k + 1) * r], h2[0:r, par, k * P:(k + 1) * P],
                                      ident[0:r, 0:r])
                mm.then_inc(h2_tr, 1)

            def places(q, looped):
                r = rows_of(q, looped)
                first = not looped and q == 0
                pe.wait_ge(m_made, q + 1)
                wait(pe, mrun_made, q)
                wait(pe, mp_made, q)
                mm = pe.matmul(PS[0:r, 7, 0:NE], upper[0:r, 0:r], mb[0:r, :], start=True, stop=first)
                if not first:
                    mm = pe.matmul(PS[0:r, 7, 0:NE], ones[:, 0:r], mrun[:, :], start=False, stop=True)
                mm.then_inc(pos_mm, 1)

            def logits(q, par, looped):
                r = rows_of(q, looped)
                pe.wait_ge(h2T_made, q + 1)
                wait(pe, lg_made, q)
                for k in range(KD):
                    mm = pe.matmul(PS[0:r, 6, 0:NL], h2T[:, par, k, 0:r], wr[:, k, :], start=(k == 0),
                                   stop=(k == KD - 1))
                mm.then_inc(lg_mm, 1)

            pe.wait_ge(later_in, LATER)

            def w_step(q, par, half, looped):
                if looped or q < NQ:
                    pe.wait_ge(ht_lo_made, q + (NQ + 1))
                    wait(pe, y_scaled, q - 1)
                    y_half(q, par, 0, looped)
                if looped or 2 <= q <= NQ + 1:
                    h2_turn(q - 2, par, looped or q > 2)
                if looped or q >= 3:
                    places(q - 3, looped or q > 3)
                if looped or q < NQ:
                    y_half(q, par, 1, looped).then_inc(y_mm, 1)
                if looped or 2 <= q <= NQ + 1:
                    logits(q - 2, par, looped or q > 2)

            run_steps(pe, w_step, 0, NQ + 3, 4, 8)
            pe.wait_ge(mrun_made, NQ)
            pe.wait_ge(mp_made, NQ)
            pe.matmul(PS[:, 7, 0:NE], ones[:, :], mrun[:, :], start=True, stop=True).then_inc(cnt_mm, 1)

            def turn_in(n, s, uses):
                par = s % HG
                pe.wait_ge(hg_in[par], uses * 16 + 16)
                wait(pe, hgT_a, n)
                wait(pe, hgT_b, n)
                for k in range(KD):
                    mm = pe.transpose(banks(0, 2)[:, k * P:(k + 1) * P], hg[par][:, k * P:(k + 1) * P], ident[:, :])
                mm.then_inc(hg_tr, 1)

            def down(n, s):
                par, slot = s % 2, s % RING
                pe.wait_ge(actT_made, n + 1)
                wait(pe, ysb_made, n)
                for half in range(2):
                    mm = pe.matmul(PS[:, 5 + half, :], actT[:, par, :], wd[slot][:, half * 512:(half + 1) * 512],
                                   start=True, stop=True)
                mm.then_inc(down_mm, 1)

            def e_step(n, s, oct_, looped):
                par = s % 2
                if looped or n < NE:
                    pe.wait_ge(hgT_a, n + 1)
                    pe.wait_ge(hgT_b, n + 1)
                    pe.wait_ge(we_in[s], oct_ * 48 + 48)
                    wait(pe, act_made, n - 1)
                    for k in range(KD):
                        mm = pe.matmul(PS[:, 2 + par, 0:2 * FE], hgT[par][:, k, :], wgu[s][:, :, k, :],
                                       start=(k == 0), stop=(k == KD - 1))
                    mm.then_inc(gu_mm, 1)
                if looped or n + 1 < NE:
                    turn_in(n + 1, s + 1, oct_ * (RING // HG) + (s + 1) // HG)
                if looped or n >= 1:
                    down(n - 1, (s - 1) % RING)
                if looped or n < NE:
                    pe.wait_ge(act_made, n + 1)
                    wait(pe, actT_made, n)
                    pe.transpose(PS[:, 4, 0:P], actv[:, par, :], ident[:, :]).then_inc(act_tr, 1)

            turn_in(0, 0, 0)
            run_steps(pe, e_step, 0, NE + 1, RING, NE - RING, RING)

            pe.wait_ge(cnt_made, 2)
            pe.wait_ge(ysb_made, NE)
            fullest = pe.value_load(most_u[0:1, 0:1], min_val=0, max_val=TOK)
            with pe.If(fullest > P):
                with pe.Fori(1, NQ) as c:
                    with pe.Fori(0, NE) as x:
                        m = (c - 1) * NE + x
                        pe.wait_ge(o_gather, m * 16 + 16)
                        for k in range(KD):
                            mm = pe.transpose(banks(0, 2)[:, k * P:(k + 1) * P], hg[0][:, k * P:(k + 1) * P],
                                              ident[:, :])
                        mm.then_inc(o_pe, 1)
                        pe.wait_ge(o_dve, m * 4 + 1)
                        pe.wait_ge(o_in, m * 64 + 64)
                        for k in range(KD):
                            mm = pe.matmul(PS[:, 2, 0:2 * FE], hgT[0][:, k, :], wgu[0][:, :, k, :],
                                           start=(k == 0), stop=(k == KD - 1))
                        mm.then_inc(o_pe, 1)
                        pe.wait_ge(o_dve, m * 4 + 2)
                        pe.transpose(PS[:, 4, 0:P], actv[:, 0, :], ident[:, :]).then_inc(o_pe, 1)
                        pe.wait_ge(o_dve, m * 4 + 3)
                        for half in range(2):
                            mm = pe.matmul(PS[:, 5 + half, :], actT[:, 0, :], wd[0][:, half * 512:(half + 1) * 512],
                                           start=True, stop=True)
                        mm.then_inc(o_pe, 1)


_INS = ["x_prompt", "x_sample", "c_prompt", "c_sample", "state_pool", "w_ada", "b_ada", "g_pre_mix",
        "g_post_mix", "g_pre_ffn", "g_post_ffn", "w_in", "ln_v_g", "ln_v_b", "w_spatial", "b_spatial",
        "w_pool", "pool_scale", "w_out", "w_router_grp", "b_router_grp", "w_router_exp",
        "b_router_exp", "w_exp_gate", "w_exp_up", "w_exp_down"]


def kernel(**inputs):
    import numpy as _np
    import concourse.bacc as _bacc
    from concourse import mybir as _mybir
    from concourse.bass_utils import run_bass_kernel_spmd as _run

    nc = _bacc.Bacc("TRN2", target_bir_lowering=False, num_devices=1)
    arrays, args = {}, []
    for name in _INS:
        a = _np.ascontiguousarray(inputs[name])
        arrays[f"in_{name}_dram"] = a
        args.append(nc.dram_tensor(f"in_{name}_dram", a.shape, _mybir.dt.from_np(a.dtype), kind="ExternalInput").ap())
    x_prompt, x_sample, state_pool = inputs["x_prompt"], inputs["x_sample"], inputs["state_pool"]
    depth, samples, rows, width = state_pool.shape
    outs = [x_prompt.shape, x_sample.shape, (depth, x_prompt.shape[0], rows, width), state_pool.shape,
            (depth, samples, 1, x_prompt.shape[2])]
    for i, shape in enumerate(outs):
        args.append(nc.dram_tensor(f"out_{i}_dram", shape, _mybir.dt.float32, kind="ExternalOutput").ap())
    trunk_step(nc, *args)
    r = _run(nc, [arrays], core_ids=[0])
    return tuple(r.results[0][f"out_{i}_dram"] for i in range(len(outs)))
```

```python
from contextlib import ExitStack

import concourse.bass as bass
from concourse import mybir

F32 = mybir.dt.float32
F32R = mybir.dt.float32r
BF16 = mybir.dt.bfloat16
U32 = mybir.dt.uint32
ALU = mybir.AluOpType
ACT = mybir.ActivationFunctionType
AX_X = mybir.AxisListType.X

P = 128
EPS = 1e-6
PAST_ALL = 1 << 20


def wait(eng, sem, value):
    if isinstance(value, int) and value <= 0:
        return
    eng.wait_ge(sem, value)


def wait_apart(eng, sem, value, passed):
    eng.wait_ge(sem, value)
    eng.sem_inc(passed, 1)


def wait_apart_if(eng, sem, value, passed):
    if isinstance(value, int) and value <= 0:
        return
    wait_apart(eng, sem, value, passed)


def run_steps(eng, step, first, last, loop_from, loop_to, many=2):
    assert (loop_to - loop_from) % many == 0
    for q in range(first, loop_from):
        step(q, q % many, q // many, False)
    with eng.Fori(0, (loop_to - loop_from) // many) as i:
        for s in range(many):
            q0 = loop_from + s
            step(i * many + q0, q0 % many, i + q0 // many, True)
    for q in range(loop_to, last):
        step(q, q % many, q // many, False)


class Place:

    def __init__(self, nc, at, end):
        self.nc, self.at, self.end = nc, at, end

    def __call__(self, name, shape, dt):
        size = mybir.dt.size(dt)
        for n in shape[1:]:
            size *= n
        t = self.nc.alloc_sbuf_tensor_at(name, shape, dt, offset=self.at)
        self.at += (size + 31) // 32 * 32
        assert self.at <= self.end, (name, self.at, self.end)
        return t


def trunk_step(nc, x_prompt, x_sample, c_prompt, c_sample, state_pool, w_ada, b_ada, g_pre_mix,
               g_post_mix, g_pre_ffn, g_post_ffn, w_in, ln_v_g, ln_v_b, w_spatial, b_spatial, w_pool,
               pool_scale, w_out, w_router_grp, b_router_grp, w_router_exp, b_router_exp,
               w_exp_gate, w_exp_up, w_exp_down, y_prompt, y_sample, pool_prompt, pool_sample,
               chunk_v):
    _, SEQ, D = x_prompt.shape
    NS = x_sample.shape[0]
    KD = D // P
    NT = SEQ // P
    TOK = SEQ + NS
    NC = NS + 1
    PRM = NS
    AW = D
    BW = state_pool.shape[3]
    PST = state_pool.shape[2]
    NG = BW // P
    HD = w_spatial.shape[1]
    NMOD = w_ada.shape[2] // P
    NQ = NT + 1
    assert HD == KD == NT == 8 and NG == 4

    xp = x_prompt.rearrange("b (t p) d -> (b t) p d", p=P)
    xs = x_sample.rearrange("b s d -> (b s) d")
    w_in_k = w_in[0].rearrange("(k p) n -> p k n", p=P)
    w_ada_k = w_ada[0].rearrange("(k p) n -> p k n", p=P)

    v_dram = nc.dram_tensor("v_normed", [NT, P, AW], F32).ap()
    NE = w_exp_gate.shape[1]
    FE = w_exp_gate.shape[3]
    NGR = w_router_grp.shape[2]
    EPG = NE // NGR
    NL = 8 + NE
    SLOTS = NQ * P
    mod_dram = nc.dram_tensor("modulation", [NC, 4 * D], F32).ap()
    h2_dram = nc.dram_tensor("h2", [TOK, D], F32).ap()
    list_dram = nc.dram_tensor("token_lists", [SLOTS * NE, 2], U32).ap()
    out_dram = nc.dram_tensor("expert_outs", [2 * TOK, D], F32).ap()
    merged_dram = nc.dram_tensor("merged", [KD, P, TOK], F32).ap()

    with ExitStack() as ctx:
        def sem(name):
            return ctx.enter_context(nc.semaphore(name))

        def sems(name, n):
            return [sem(f"{name}{i}") for i in range(n)]

        CH = 256
        HG, IX = 4, 8
        BASE = (nc.sbuf_base + 31) // 32 * 32
        END = nc.sbuf_usable_end // 32 * 32
        keep = Place(nc, BASE, BASE + 10240)

        ident = keep("ident", [P, P], F32)
        vecT = keep("vecT", [P, 4 * KD], F32)
        cT = keep("cT", [P, KD, NC], F32)
        modT = keep("modT", [P, 2 * KD, NC], F32)
        A1T = keep("A1T", [P, KD, NC], F32)
        ss = keep("ss", [P, 2], F32)
        ms = keep("ms", [P, 2], F32)
        rstd = keep("rstd", [P, 2], F32)
        bn6 = keep("bn6", [P, 2, 6], F32)
        mv = keep("mv", [P, 2], F32)
        ve = keep("ve", [P, 1], F32)
        vr = keep("vr", [P, 1], F32)
        mhalf = keep("mhalf", [P, 1], F32)
        inv_n = keep("inv_n", [P, 16], F32)
        invc = keep("invc", [P, 16], F32)
        psh = keep("psh", [P, KD], F32)
        w00 = keep("w00", [NS, HD], F32)
        w00d = keep("w00d", [NS, HD, NS], F32)

        wr = keep("wr", [P, KD, NL], F32)
        biasr = keep("biasr", [P, NL], F32)
        iota8 = keep("iota8", [P, 8], F32)
        upper = keep("upper", [P, P], BF16)
        ones = keep("ones", [P, P], BF16)
        lg = keep("lg", [P, NL], F32)
        gtop = keep("gtop", [P, 8], F32)
        gix = keep("gix", [P, 8], U32)
        gid = keep("gid", [P, 1], F32)
        ohg = keep("ohg", [P, NGR], F32)
        t32 = keep("t32", [P, NE], F32)
        s8 = keep("s8", [P, 8], F32)
        etop = keep("etop", [P, 8], F32)
        eix = keep("eix", [P, 8], U32)
        ei = keep("ei", [P, 2], F32)
        oh12 = keep("oh12", [P, 2, 8], F32)
        m12 = keep("m12", [P, 2, NE], F32)
        mb = keep("mb", [P, NE], BF16)
        mrun = keep("mrun", [P, NE], BF16)
        ngm = keep("ngm", [P, 1], F32)
        exg = keep("exg", [P, NGR], F32)
        se = keep("se", [P, 1], F32)
        dm = keep("dm", [P, 1], F32)
        e12 = keep("e12", [P, 1], F32)
        pg = keep("pg", [P, 1], F32)
        e1 = keep("e1", [P, 1], F32)
        rw = keep("rw", [P, 1], F32)
        wts = keep("wts", [P, NQ, 2], F32)
        eid = keep("eid", [P, 2], F32)
        mp = keep("mp", [P, 2, NE], F32)
        pos = keep("pos", [P, 2], F32)
        lrow = [[keep(f"lrow{i}{j}", [P, 1], U32) for j in range(2)] for i in range(2)]
        tid = keep("tid", [P, 1], F32)
        tidu = keep("tidu", [P, 2, 2, 2], U32)
        lst = keep("lst", [P, NE, 2], U32)
        idx = [keep(f"idx{i}", [P, 2], U32) for i in range(IX)]
        most = keep("most", [P, 1], F32)
        most_u = keep("most_u", [P, 1], U32)
        ss2 = keep("ss2", [P, 4], F32)
        ms2 = keep("ms2", [P, 4], F32)
        rs2 = keep("rs2", [P, 4], F32)

        big = Place(nc, keep.end, END)
        hT_hi = big("hT_hi", [P, KD, TOK], F32R)
        lo_at = big.at
        hT_lo = big("hT_lo", [P, KD, TOK], F32R)
        early = Place(nc, lo_at, big.at)
        adaV = early("adaV", [P, 4, KD, CH], F32)

        v = Place(nc, big.at, END)
        wv_raw = v("wv_raw", [P, 2, AW], F32)
        xbuf = v("xbuf", [P, 2, D], F32)
        xn = v("xn", [P, D], F32)
        h = v("h", [P, KD, P], F32)
        ht_hi1 = v("ht_hi1", [P, KD, P], F32R)
        wv_hi = v("wv_hi", [P, KD, AW], F32R)
        wv_lo = v("wv_lo", [P, KD, AW], F32R)
        lng = v("lng", [P, AW], F32)
        lnb = v("lnb", [P, AW], F32)
        ht_hi = [v("ht_hi0", [P, KD, P], F32R), ht_hi1]
        ht_lo = [v(f"ht_lo{i}", [P, KD, P], F32R) for i in range(2)]
        vg = v("vg", [P, 2, AW], F32)
        early = Place(nc, keep.end, lo_at)
        c9 = early("c9", [NC, D], F32)
        sc9 = early("sc9", [NC, D], F32)
        vecs = early("vecs", [4 * KD, P], F32)
        rows0 = early("rows0", [NC, 2 * D], F32)
        none_u = early("none_u", [P, NQ * NE * 2], U32)

        f = Place(nc, big.at, END)
        wraw = f("wraw", [P, 3, KD, P], F32)
        w_hi = [f(f"w_hi{i}", [P, KD, P], F32R) for i in range(2)]
        w_lo = [f(f"w_lo{i}", [P, KD, P], F32R) for i in range(2)]
        ada_at = f.at
        adaF = f("adaF", [P, 4, KD, CH], F32)
        dT = f("dT", [P, NG, TOK], F32)
        bsb = f("bsb", [P, HD, P], F32)
        wsT = f("wsT", [P, HD, P], F32)
        pooling = Place(nc, f.at, f.at + 2 * 4128)
        ws = pooling("ws", [P, HD, P], F32)
        spr = pooling("spr", [NS * PST, BW], F32)
        spT = pooling("spT", [P, NG, NS * PST], F32)
        u = f("u", [P, TOK], F32)
        ta = f("ta", [P, TOK], F32)
        pooling = Place(nc, f.at, f.at + 5 * 4128)
        pT = [pooling(f"pT{i}", [P, 16 + TOK], F32) for i in range(2)]
        pa = pooling("pa", [P, 16 + SEQ], F32)
        pb = pooling("pb", [P, 16 + SEQ], F32)
        tb = f("tb", [P, TOK], F32)
        m0 = f("m0", [P, TOK], F32)
        yb1 = f("yb1", [P, TOK], F32)
        tails_at = Place(nc, f.at + 4 * TOK, f.at + 8 * TOK)
        ptok = tails_at("ptok", [PST, BW], F32)
        pstok = tails_at("pstok", [NS, BW], F32)
        mg = f("mg", [P, 2, TOK], F32)
        vf = f("vf", [P, 2, NT, P], F32)
        vfs = f("vfs", [NS, 2, P], F32)
        wpl = f("wpl", [P, 2, P], F32)
        ybs = f("ybs", [P, NS], F32)
        psm = f("psm", [P, NG, NS], F32)
        pws = f("pws", [P, NG, NS], F32)
        ptail = f("ptail", [P, NG, PST], F32)
        bias = f("bias", [NC, 2, 2 * CH], F32)
        rowbuf = f("rowbuf", [NC, 2, 2 * CH], F32)
        fix = f("fix", [P, 16], F32)
        w = Place(nc, keep.end, big.at)
        wo_hi = w("wo_hi", [P, KD, D], F32R)
        mt = w("mt", [P, 2, KD, P], F32)
        mt_hi = [w(f"mt_hi{i}", [P, KD, P], F32R) for i in range(2)]
        mt_lo = [w(f"mt_lo{i}", [P, KD, P], F32R) for i in range(2)]
        w = Place(nc, big.at, ada_at)
        rws = w("rws", [NC, 4, D], F32)
        G2b = w("G2b", [P, D], F32)
        xw_at = w.at
        xw = w("xw", [P, 2, D], F32)
        wo_raw = Place(nc, ada_at, END)("wo_raw", [P, KD, D], F32)
        w = Place(nc, ada_at, END)
        wo_lo = w("wo_lo", [P, KD, D], F32R)
        x2 = w("x2", [P, NQ, D], F32)
        moe_at = w.at
        G1b = w("G1b", [P, D], F32)
        A2b = w("A2b", [P, D], F32)
        B2b = w("B2b", [P, D], F32)
        yt = w("yt", [P, D], F32)
        h2 = w("h2buf", [P, 2, D], F32)
        g_post2 = Place(nc, w.at - 4 * D, w.at)("g_post2", [P, D], F32)
        gains = Place(nc, w.at, w.at + 8 * D)
        g_post1 = gains("g_post1", [P, D], F32)
        g_pre2 = gains("g_pre2", [P, D], F32)
        h2T = w("h2T", [P, 2, KD, P], F32)

        RING = 8
        first, second = Place(nc, keep.end, big.at), Place(nc, ada_at, ada_at + 4 * KD * D)
        wgu, wd = [], []
        for i in range(RING):
            e = first if i < 5 else second
            wgu.append(e(f"wgu{i}", [P, 2, KD, FE], F32))
            wd.append((e if i < RING - 1 else first)(f"wd{i}", [P, D], F32))
        e = Place(nc, xw_at, xw_at + 8 * D)
        hg = [e(f"hg{i}", [P, D], F32) for i in range(2)]
        e = Place(nc, moe_at, END)
        hg += [e(f"hg{i}", [P, D], F32) for i in range(2, HG)]
        hgT = [e(f"hgT{i}", [P, KD, P], F32) for i in range(2)]
        ysb = e("ysb", [P, 2, D], F32)
        sil = e("sil", [P, 2, P], F32)
        actT = e("actT", [P, 2, P], F32)
        e = Place(nc, keep.end, big.at)
        yg = e("yg", [P, 2, 2, D], F32)
        f1 = e("f1", [P, 2, D], F32)
        ff = e("ff", [P, 2, D], F32)
        fj = e("fj", [P, 2, D], F32)
        fo = e("fo", [P, 2, D], F32)

        PS = ctx.enter_context(nc.psum_tensor("PS", [P, 8, 512], F32))

        def banks(a, n):
            return PS[:, a:a + n, :].rearrange("p b n -> p (b n)")

        rows_in = sem("rows_in")
        more_rows_in = sem("more_rows_in")
        rows_made = sem("rows_made")
        mod_tr = sem("mod_tr")
        mod_out = sems("mod_out", 2)
        prep_made = sem("prep_made")
        consts = sem("consts")
        mt_in = sems("mt_in", 2)
        y_mm = sem("y_mm")
        y_scaled = sem("y_scaled")
        x2_made = sem("x2_made")
        h2_scaled = sem("h2_scaled")
        h2_made = sem("h2_made")
        h2_out = sems("h2_out", 2)
        h2_tr = sem("h2_tr")
        h2T_made = sem("h2T_made")
        lg_mm = sem("lg_mm")
        lg_made = sem("lg_made")
        mp_made = sem("mp_made")
        eid_made = sem("eid_made")
        wts_made = sem("wts_made")
        route = sem("route")
        exp_made = sem("exp_made")
        exp2_made = sem("exp2_made")
        m_made = sem("m_made")
        pos_mm = sem("pos_mm")
        mrun_made = sem("mrun_made")
        slot_step = sem("slot_step")
        slot_made = sem("slot_made")
        scat = sems("scat", 2)
        cnt_mm = sem("cnt_mm")
        cnt_made = sem("cnt_made")
        lst_in = sem("lst_in")
        hg_zero = sem("hg_zero")
        idx_made = sem("idx_made")
        hg_in = sems("hg_in", HG)
        we_in = sems("we_in", RING)
        hg_tr = sem("hg_tr")
        hgT_a = sem("hgT_a")
        hgT_b = sem("hgT_b")
        gu_mm = sem("gu_mm")
        silu_made = sem("silu_made")
        act_made = sem("act_made")
        down_mm = sem("down_mm")
        ysb_made = sem("ysb_made")
        eo_out = sems("eo_out", 2)
        o_in = sem("o_in")
        o_gather = sem("o_gather")
        o_pe = sem("o_pe")
        o_act = sem("o_act")
        o_dve = sem("o_dve")
        o_out = sem("o_out")
        f1_made = sem("f1_made")
        f_made = sem("f_made")
        f_scaled = sem("f_scaled")
        fo_made = sem("fo_made")
        y_out = sems("y_out", 2)
        vec_in = sem("vec_in")
        passed = sem("passed")
        state_out = sem("state_out")
        pool_passed = sem("pool_passed")
        vfs_in = sems("vfs_in", 2)
        small_in = sem("small_in")
        later_in = sem("later_in")
        c_silu = sem("c_silu")
        pre_tr = sem("pre_tr")
        pre_cp = sem("pre_cp")
        ada_in = sems("ada_in", 4)
        ada_mm = sem("ada_mm")
        mod_made = sem("mod_made")
        x_in = sems("x_in", 2)
        sum_made = sem("sum_made")
        sum_mean = sem("sum_mean")
        sum_root = sem("sum_root")
        x_normed = sem("x_normed")
        xT_made = sem("xT_made")
        h_scaled = sem("h_scaled")
        h_made = sem("h_made")
        ht_hi_made = sem("ht_hi_made")
        ht_lo_made = sem("ht_lo_made")
        hT_kept = sem("hT_kept")
        w_in_rows = sems("w_in_rows", 2)
        w_hi_k = sem("w_hi_k")
        w_lo_k = sem("w_lo_k")
        v_mm = sem("v_mm")
        v_gelu = sem("v_gelu")
        v_bn = sem("v_bn")
        sum2_made = sem("sum2_made")
        sum2_mean = sem("sum2_mean")
        sum2_root = sem("sum2_root")
        v_step = sem("v_step")
        v_made = sem("v_made")
        v_out = sems("v_out", 2)
        fc_in = sem("fc_in")
        ws_masked = sem("ws_masked")
        ws_tr = sem("ws_tr")
        ws_cp = sem("ws_cp")
        w_inn = sems("w_inn", 3)
        w_hi_made = sem("w_hi_made")
        w_lo_made = sem("w_lo_made")
        blk_mm = sem("blk_mm")
        p_cp = sem("p_cp")
        p_step = sem("p_step")
        p_done = sem("p_done")
        dS_made = sem("dS_made")
        tail_tr = sem("tail_tr")
        spare_read = sem("spare_read")
        tail_cp = sem("tail_cp")
        u_made = sem("u_made")
        ta_made = sem("ta_made")
        tb_made = sem("tb_made")
        mix_mm = sem("mix_mm")
        yb_mm = sem("yb_mm")
        m0_made = sem("m0_made")
        m1_made = sem("m1_made")
        m2_made = sem("m2_made")
        yb1_made = sem("yb1_made")
        mg_made = sem("mg_made")
        mg_out = sems("mg_out", 2)
        vf_in = sems("vf_in", 2)
        wpl_in = sems("wpl_in", 2)
        st_out = sem("st_out")

        WCOL = {"p": 2 * AW, "u": 0, "ga": 2 * AW + BW, "gb": 2 * AW + BW + D}
        CPM = CH // P
        NADA_V = 2 * D // CH
        NADA_F = NMOD // CPM - NADA_V
        VEC = {"pre_mix": 2 * KD, "pool_scale": 3 * KD}
        NV = 4 * KD
        R_G1, R_B2, R_A2, R_G2 = range(4)
        THIRD = TOK // 3
        assert 3 * THIRD == TOK and THIRD >= 256
        REGION = (5, 2)
        MIX = 0
        SMIX_AT, SYB_AT = THIRD, THIRD + NS
        LISTS = list_dram.rearrange("(s e) o -> s (e o)", e=NE)
        RC, SC = 16, 2
        LATER = 16 * 8
        X_IN = (16 * ((NQ + 1) // 2), 16 * (NQ // 2))
        ROWS_OUT = 16 * (NE // 2)

        def rows_of(q, looped):
            return NS if not looped and q == 0 else P

        def thirds(r):
            return PS[:, REGION[r]:REGION[r] + 3, 0:THIRD]

        def in_thirds(ap):
            return ap.rearrange("p (b n) -> p b n", n=THIRD)

        def v_over(eng):
            eng.wait_ge(v_mm, NQ)
            eng.wait_ge(hT_kept, 2 * NQ)
            eng.wait_ge(v_out[0], 16 * 5)
            eng.wait_ge(v_out[1], 16 * 4)

        def f_over(eng):
            eng.wait_ge(blk_mm, NG + 3 * HD)
            eng.wait_ge(yb_mm, HD)
            eng.wait_ge(mod_out[0], 16 * (HD // 2))
            eng.wait_ge(mod_out[1], 16 * (HD // 2))
            eng.wait_ge(mg_out[0], 16 * (HD // 2))
            eng.wait_ge(mg_out[1], 16 * (HD // 2))
            eng.wait_ge(st_out, 32)

        block = ctx.enter_context(nc.Block())

        @block.sync
        def _(sp):
            def ada_chunk(n, slot, ring):
                wait(sp, ada_mm, n - 3)
                sp.dma_start(ring[:, slot], w_ada_k[:, :, bass.ds(n * CH, CH)]).then_inc(ada_in[slot], 16)

            def x_tile(q, par, half, looped):
                wait(sp, x_normed, q - 1)
                if not looped and q == 0:
                    sp.dma_start(xbuf[0:NS, par, :], xs).then_inc(x_in[par], 16)
                else:
                    sp.dma_start(xbuf[:, par, :], xp[bass.ds(q - 1, 1)].rearrange("a p d -> p (a d)")
                                 ).then_inc(x_in[par], 16)

            def v_store(q, par, looped):
                wait(sp, v_made, q + 1)
                if not looped and q == 0:
                    sp.dma_start(chunk_v[0, :, 0, :], vg[0:NS, par, :]).then_inc(v_out[par], 16)
                else:
                    sp.dma_start(v_dram[bass.ds(q - 1, 1)].rearrange("a p d -> p (a d)"),
                                 vg[:, par, :]).then_inc(v_out[par], 16)

            sp.dma_start(c9[0:NS, :], c_sample).then_inc(small_in, 16)
            sp.dma_start(c9[NS:NC, :], c_prompt).then_inc(small_in, 16)
            for n in range(4):
                ada_chunk(n, n % 4, adaV)
            x_tile(0, 0, 0, False)
            x_tile(1, 1, 0, False)
            for k in range(KD):
                wait(sp, w_lo_k, k - 1)
                sp.dma_start(wv_raw[:, k % 2, :], w_in_k[:, k, AW:2 * AW]).then_inc(w_in_rows[k % 2], 16)
                if k % 2:
                    ada_chunk(4 + k // 2, k // 2, adaV)

            def step(q, par, half, looped):
                if looped or q < NQ:
                    x_tile(q, par, half, looped)
                if looped or q >= 3:
                    v_store(q - 3, 1 - par, looped)

            def load_block(n, slot, col):
                wait(sp, w_lo_made, n - 2)
                sp.dma_start(wraw[:, slot], w_in_k[:, :, col]).then_inc(w_inn[slot], 16)

            run_steps(sp, step, 2, NQ + 1, 4, 8)
            sp.wait_ge(w_lo_k, KD)
            sp.wait_ge(sum_root, NQ)
            sp.wait_ge(x_normed, NQ)
            for g in range(3):
                load_block(g, g, bass.ds(WCOL["p"] + g * P, P))
            for q in range(NQ + 1, NQ + 3):
                step(q, q % 2, q // 2, False)

            v_over(sp)
            sp.dma_start(spr[:, :], state_pool[0].rearrange("b r c -> (b r) c")).then_inc(fc_in, 16)
            sp.dma_start(ws[:, :, :], w_spatial[0].rearrange("h i j -> i h j")).then_inc(fc_in, 16)
            sp.dma_start(bsb[:, :, :], b_spatial.to_broadcast([P, HD, P])).then_inc(fc_in, 16)
            load_block(3, 0, bass.ds(WCOL["p"] + 3 * P, P))

            def f_part(q, j, part):
                load_block(q * 3 + (NG + j), (NG + j) % 3, bass.ds(q * P + WCOL[part], P))

            def f_step(q, par, half, looped):
                f_part(q, 0, "u")
                wait(sp, blk_mm, q * 3 + (NG - 4) if looped or q >= 2 else 0)
                sp.dma_start(vfs[:, par], chunk_v[0, :, 0, bass.ds(q * P, P)]).then_inc(vfs_in[par], 16)
                wait(sp, yb_mm, q - 1)
                sp.dma_start(wpl[:, par], w_pool[0, bass.ds(half, 1), :, par * P:(par + 1) * P]
                             .rearrange("g c o -> c (g o)")).then_inc(wpl_in[par], 16)
                wait(sp, mod_made, q + (NADA_V - 1) if looped or q >= 2 else 0)
                sp.dma_start(bias[:, par], b_ada[:, bass.ds(q * 2 * CH + 2 * D, 2 * CH)].to_broadcast([NC, 2 * CH])
                             ).then_inc(wpl_in[par], 16)
                for a in range(2):
                    ada_chunk(q * 2 + (NADA_V + a), 2 * par + a, adaF)
                f_part(q, 1, "ga")
                wait(sp, mix_mm, q - 1)
                sp.dma_start(vf[:, par], v_dram[:, :, bass.ds(q * P, P)].rearrange("t p c -> p t c")
                             ).then_inc(vf_in[par], 16)
                f_part(q, 2, "gb")

            f_step(0, 0, 0, False)
            sp.wait_ge(tail_cp, 1)
            sp.dma_start(pool_prompt[0, 0], ptok[:, :]).then_inc(st_out, 16)
            sp.dma_start(pool_sample[0, :, PST - 1, :], pstok[:, :]).then_inc(st_out, 16)
            run_steps(sp, f_step, 1, HD, 2, HD)

            sp.wait_ge(ada_mm, NADA_V + NADA_F)
            for a in range(2):
                k = a * KD // 2
                sp.dma_start(wo_raw[:, k:k + KD // 2, :], w_out[0].rearrange("(k p) n -> p k n", p=P)[
                    :, k:k + KD // 2, :]).then_inc(w_in_rows[a], 16)
            f_over(sp)

            def load_x(q, par, looped):
                wait(sp, x2_made, q - 1)
                if not looped and q == 0:
                    sp.dma_start(xw[0:NS, par, :], xs).then_inc(x_in[par], 16)
                else:
                    sp.dma_start(xw[:, par, :], xp[bass.ds(q - 1, 1)].rearrange("a p d -> p (a d)")
                                 ).then_inc(x_in[par], 16)

            def load_m(q, par, looped):
                wait(sp, ht_lo_made, q + (NQ - 1) if looped or q >= 2 else 0)
                if not looped and q == 0:
                    with nc.allow_non_contiguous_dma(reason="the samples' eight columns"):
                        sp.dma_start(mt[:, par, :, 0:NS], merged_dram[:, :, SEQ:TOK]
                                     .rearrange("k p t -> p k t")).then_inc(mt_in[par], 16)
                else:
                    sp.dma_start(mt[:, par], merged_dram[:, :, bass.ds((q - 1) * P, P)]
                                 .rearrange("k p t -> p k t")).then_inc(mt_in[par], 16)

            def store_h2(q, par, looped):
                r = rows_of(q, looped)
                sp.wait_ge(h2_made, q + 1)
                dst = h2_dram[SEQ:TOK, :] if r == NS else (
                    h2_dram[0:SEQ, :].rearrange("(t p) d -> t p d", p=P)[bass.ds(q - 1, 1)]
                    .rearrange("t p d -> p (t d)"))
                sp.dma_start(dst, h2[0:r, par, :]).then_inc(h2_out[par], 16)

            def w_step(q, par, half, looped):
                if looped or q + 1 < NQ:
                    load_m(q + 1, 1 - par, looped)
                if looped or q >= 1:
                    store_h2(q - 1, 1 - par, looped or q > 1)
                if looped or q + 1 < NQ:
                    load_x(q + 1, 1 - par, looped)

            load_m(0, 0, False)
            load_x(0, 0, False)
            run_steps(sp, w_step, 0, NQ + 1, 2, 8)

            sp.wait_ge(y_mm, NQ)
            sp.wait_ge(ht_lo_made, 2 * NQ)

            def load_expert(n, s, uses, looped):
                wait(sp, down_mm, n - (RING - 1))
                one = bass.ds(n, 1)
                sp.dma_start(wgu[s][:, 0], w_exp_gate[0, one].rearrange("a (p k) f -> p (a k) f", k=KD)
                             ).then_inc(we_in[s], 16)
                sp.dma_start(wgu[s][:, 1], w_exp_up[0, one].rearrange("a (p k) f -> p (a k) f", k=KD)
                             ).then_inc(we_in[s], 16)
                sp.dma_start(wd[s][:, :], w_exp_down[0, one].rearrange("a f d -> f (a d)")
                             ).then_inc(we_in[s], 16)

            FIRST = RING // 2
            for n in range(FIRST):
                load_expert(n, n, 0, False)
            sp.wait_ge(hg_in[1], 16)
            for n in range(FIRST, RING):
                load_expert(n, n, 0, False)
            run_steps(sp, load_expert, RING, NE, RING, NE, RING)

            sp.wait_ge(down_mm, NE)
            sp.wait_ge(cnt_made, 2)
            for par in range(2):
                sp.wait_ge(eo_out[par], ROWS_OUT)
            fullest = sp.value_load(most_u[0:1, 0:1], min_val=0, max_val=TOK)
            with sp.If(fullest > P):
                with sp.Fori(1, NQ) as c:
                    with sp.Fori(0, NE) as x:
                        one = bass.ds(x, 1)
                        sp.dma_start(idx[0][:, :], LISTS[bass.ds(c * P, P), bass.ds(x * 2, 2)]).then_inc(o_in, 16)
                        sp.dma_start(wgu[0][:, 0], w_exp_gate[0, one].rearrange("a (p k) f -> p (a k) f", k=KD)
                                     ).then_inc(o_in, 16)
                        sp.dma_start(wgu[0][:, 1], w_exp_up[0, one].rearrange("a (p k) f -> p (a k) f", k=KD)
                                     ).then_inc(o_in, 16)
                        sp.dma_start(wd[0][:, :], w_exp_down[0, one].rearrange("a f d -> f (a d)")
                                     ).then_inc(o_in, 16)
                        wait_apart(sp, o_out, ((c - 1) * NE + x) * 16 + 16, passed)

            def load_y(q, par, half, looped):
                wait(sp, f_made, q - 1)
                r = rows_of(q, looped)
                if r == NS:
                    src = out_dram[2 * SEQ:2 * TOK, :].rearrange("(p k) d -> p (k d)", k=2)
                else:
                    src = out_dram[0:2 * SEQ, :].rearrange("(t p k) d -> t p (k d)", p=P, k=2)[
                        bass.ds(q - 1, 1)].rearrange("t p d -> p (t d)")
                sp.dma_start(yg[0:r, par].rearrange("p k d -> p (k d)"), src).then_inc(x_in[par], 16)

            load_y(0, 0, 0, False)
            load_y(1, 1, 0, False)

            def store_y(q, par, half, looped):
                if looped or q + 2 < NQ:
                    load_y(q + 2, par, half + 1, looped or True)
                sp.wait_ge(fo_made, q + 1)
                if not looped and q == 0:
                    sp.dma_start(y_sample.rearrange("b s d -> (b s) d"), fo[0:NS, par, :]).then_inc(y_out[par], 16)
                else:
                    sp.dma_start(y_prompt[0, bass.ds((q - 1) * P, P), :], fo[:, par, :]).then_inc(y_out[par], 16)

            run_steps(sp, store_y, 0, NQ, 1, NQ - 2)
            sp.wait_ge(y_out[0], 16 * 5)
            sp.wait_ge(y_out[1], 16 * 4)
            sp.wait_ge(st_out, 32)
            sp.wait_ge(state_out, 16)
            sp.wait_ge(v_out[0], 16 * 5)

        @block.gpsimd
        def _(pool):
            pool.memset(ident[:, :], 0.0).then_inc(consts, 1)
            pool.wait_ge(consts, 1)
            pool.affine_select(out=ident[:, :], in_=ident[:, :], compare_op=ALU.not_equal, fill=1.0,
                               base=0, pattern=[[-1, P]], channel_multiplier=1).then_inc(consts, 1)
            pool.memset(mhalf[:, :], -0.5)
            pool.iota(inv_n[:, :], pattern=[[1, 16]], base=1, channel_multiplier=0,
                      allow_small_or_imprecise_dtypes=True)
            pool.iota(iota8[:, :], pattern=[[1, 8]], base=0, channel_multiplier=0,
                      allow_small_or_imprecise_dtypes=True)
            pool.iota(tid[:, :], pattern=[[0, 1]], base=SEQ, channel_multiplier=1,
                      allow_small_or_imprecise_dtypes=True)
            pool.memset(upper[:, :], 1.0)
            pool.memset(ones[:, :], 1.0)
            pool.memset(mrun[:, :], 0.0)
            pool.memset(wr[:, :, :], 0.0)
            pool.memset(none_u[:, :], PAST_ALL)
            pool.memset(biasr[:, :], -3e38).then_inc(consts, 1)
            pool.wait_ge(consts, 3)
            pool.affine_select(out=upper[:, :], in_=upper[:, :], compare_op=ALU.is_gt, fill=0.0,
                               base=0, pattern=[[1, P]], channel_multiplier=-1).then_inc(consts, 1)

            def root(n, src, tmp, scale, made, tmp_made, out, out_made):
                wait_apart(pool, made, n + 1, pool_passed)
                pool.tensor_scalar(tmp, src, scale, EPS, ALU.mult, ALU.add).then_inc(tmp_made, 1)
                pool.wait_ge(tmp_made, n + 1)
                pool.tensor_tensor(out, tmp, mhalf[0:tmp.shape[0], :], ALU.pow).then_inc(out_made, 1)

            def x_root(q, par, looped):
                rows = NS if not looped and q == 0 else P
                root(q, ss[0:rows, par:par + 1], ms[0:rows, par:par + 1], 1.0 / D, sum_made, sum_mean,
                     rstd[0:rows, par:par + 1], sum_root)

            def v_root(q, looped):
                rows = NS if not looped and q == 0 else P
                root(q, mv[0:rows, 1:2], ve[0:rows, :], 1.0, sum2_made, sum2_mean, vr[0:rows, :], sum2_root)

            def keep_h(q, par, looped):
                wait(pool, ht_lo_made, q + 1)
                if not looped and q == 0:
                    for src, dst in ((ht_hi, hT_hi), (ht_lo, hT_lo)):
                        pool.tensor_copy(dst[:, :, SEQ:TOK], src[par][:, :, 0:NS].bitcast(F32)).then_inc(hT_kept, 1)
                else:
                    at = bass.ds((q - 1) * P, P)
                    for src, dst in ((ht_hi, hT_hi), (ht_lo, hT_lo)):
                        pool.tensor_copy(dst[:, :, at], src[par][:, :, :].bitcast(F32)).then_inc(hT_kept, 1)

            def step(q, par, half, looped):
                if looped or q + 1 < NQ:
                    x_root(q + 1, 1 - par, looped)
                if looped or 2 <= q:
                    if looped or q - 2 < NQ:
                        v_root(q - 2, looped)
                if looped or q < NQ:
                    keep_h(q, par, looped)

            pool.wait_ge(later_in, LATER)
            x_root(0, 0, False)
            run_steps(pool, step, 0, NQ + 2, 4, 8)

            pool.wait_ge(fc_in, 48)
            pool.affine_select(out=ws[:, :, :], in_=ws[:, :, :], compare_op=ALU.is_ge, fill=0.0, base=0,
                               pattern=[[0, HD], [-1, P]], channel_multiplier=1).then_inc(ws_masked, 1)
            pool.dma_start(pool_sample[0, :, 0:PST - 1, :], state_pool[0, :, 1:PST, :]).then_inc(state_out, 16)
            def f_step(q, par, half, looped):
                wait_apart(pool, mod_made, q + (NADA_V + 1), pool_passed)
                pool.dma_start(mod_dram[:, bass.ds(q * 2 * CH, 2 * CH)], rowbuf[:, par, :]).then_inc(mod_out[par], 16)
                wait_apart(pool, mg_made, q + 1, pool_passed)
                pool.dma_start(merged_dram[bass.ds(q, 1)].rearrange("a p t -> p (a t)"),
                               mg[:, par, :]).then_inc(mg_out[par], 16)

            run_steps(pool, f_step, 0, HD, 0, HD - 2)

            def y_root(q, par, looped):
                r = rows_of(q, looped)
                root(q + NQ, ss2[0:r, par:par + 1], ms2[0:r, par:par + 1], 1.0 / D, sum_made, sum_mean,
                     rs2[0:r, par:par + 1], sum_root)

            def x2_root(q, par, looped):
                r = rows_of(q, looped)
                c = slice(2 + par, 3 + par)
                root(q + NQ, ss2[0:r, c], ms2[0:r, c], 1.0 / D, sum2_made, sum2_mean, rs2[0:r, c], sum2_root)

            def scatter(q, par, looped):
                r = rows_of(q, looped)
                wait_apart(pool, slot_made, q + 1, pool_passed)
                for k in range(2):
                    pool.indirect_dma_start(list_dram, bass.IndirectOffsetOnAxis(lrow[par][k][0:r, :], 0),
                                            tidu[0:r, par, k, :], None).then_inc(scat[par], 16)

            def w_step(q, par, half, looped):
                if looped or 1 <= q <= NQ:
                    y_root(q - 1, 1 - par, looped or q > 1)
                    x2_root(q - 1, 1 - par, looped or q > 1)
                if looped or q >= 3:
                    scatter(q - 3, 1 - par, looped or q > 3)

            pool.wait_ge(later_in, LATER)
            run_steps(pool, w_step, 0, NQ + 1, 4, 8)
            pool.wait_ge(x2_made, NQ)
            pool.wait_ge(h2_scaled, NQ)
            for t in hg:
                pool.memset(t[:, :], 0.0).then_inc(hg_zero, 1)
            for q in range(NQ + 1, NQ + 3):
                w_step(q, q % 2, q // 2, False)
            pool.wait_ge(hg_zero, HG)

            pool.wait_ge(h2_out[0], 16 * 5)
            pool.wait_ge(h2_out[1], 16 * 4)
            pool.wait_ge(scat[0], 32 * 5)
            pool.wait_ge(scat[1], 32 * 4)
            pool.dma_start(lst[:, :, :].rearrange("p n o -> p (n o)"), LISTS[0:P, :]).then_inc(lst_in, 16)
            pool.wait_ge(lst_in, 16)

            def gather(n, s, oct_):
                wait_apart_if(pool, eo_out[s % 2], oct_ * (16 * RING // 2) + 16 * (s // 2 - (IX // 2 - 1)), pool_passed)
                pool.tensor_copy(idx[s % IX][:, :], lst[:, bass.ds(n, 1), :].rearrange("p a b -> p (a b)")
                                 ).then_inc(idx_made, 1)
                wait_apart_if(pool, hg_tr, n - (HG - 1), pool_passed)
                wait_apart(pool, idx_made, n + 1, pool_passed)
                pool.indirect_dma_start(hg[s % HG][:, :], None, h2_dram,
                                        bass.IndirectOffsetOnAxis(idx[s % IX][:, 0:1], 0),
                                        bounds_check=TOK - 1, oob_is_err=False).then_inc(hg_in[s % HG], 16)

            def answer(n, s):
                wait_apart(pool, ysb_made, n + 1, pool_passed)
                pool.indirect_dma_start(out_dram, bass.IndirectOffsetOnAxis(idx[s % IX][:, 1:2], 0),
                                        ysb[:, s % 2, :], None,
                                        bounds_check=2 * TOK - 1, oob_is_err=False).then_inc(eo_out[s % 2], 16)

            LAG = 4

            def e_step(n, s, oct_, looped):
                if looped or n < NE:
                    gather(n, s, oct_)
                if looped or n >= LAG:
                    answer(n - LAG, s + RING - LAG)

            run_steps(pool, e_step, 0, NE + LAG, RING, NE, RING)

            pool.wait_ge(cnt_made, 2)
            for j in range(HG):
                pool.wait_ge(hg_in[j], 16 * (NE // HG))
            for par in range(2):
                pool.wait_ge(eo_out[par], ROWS_OUT)
            fullest = pool.value_load(most_u[0:1, 0:1], min_val=0, max_val=TOK)
            with pool.If(fullest > P):
                with pool.Fori(1, NQ) as c:
                    with pool.Fori(0, NE) as x:
                        m = (c - 1) * NE + x
                        wait_apart(pool, o_in, m * 64 + 64, pool_passed)
                        pool.indirect_dma_start(hg[0][:, :], None, h2_dram,
                                                bass.IndirectOffsetOnAxis(idx[0][:, 0:1], 0),
                                                bounds_check=TOK - 1, oob_is_err=False).then_inc(o_gather, 16)
                        wait_apart(pool, o_dve, m * 3 + 3, pool_passed)
                        pool.indirect_dma_start(out_dram, bass.IndirectOffsetOnAxis(idx[0][:, 1:2], 0),
                                                ysb[:, 0, :], None,
                                                bounds_check=2 * TOK - 1, oob_is_err=False).then_inc(o_out, 16)
                        wait_apart(pool, o_out, m * 16 + 16, pool_passed)

            def f_root(q, par, looped):
                r = rows_of(q, looped)
                root(q + 2 * NQ, ss[0:r, par:par + 1], ms[0:r, par:par + 1], 1.0 / D, sum_made, sum_mean,
                     rstd[0:r, par:par + 1], sum_root)

            run_steps(pool, lambda q, par, half, looped: f_root(q, par, looped), 0, NQ, 1, NQ)

        @block.scalar
        def _(act):
            act.dma_start(vecs[0:2 * KD, :], b_ada[:, 0:2 * D].rearrange("o (m p) -> (o m) p", p=P)).then_inc(vec_in, 16)
            for n, g in (("pre_mix", g_pre_mix), ("pool_scale", pool_scale)):
                act.dma_start(vecs[VEC[n]:VEC[n] + KD, :], g.rearrange("o (k p) -> (o k) p", p=P)
                              ).then_inc(vec_in, 16)
            act.wait_ge(consts, 3)
            act.dma_start(wr[:, :, 0:NGR], w_router_grp[0].rearrange("(p k) g -> p k g", k=KD)).then_inc(later_in, 16)
            act.dma_start(wr[:, :, 8:NL], w_router_exp[0].rearrange("(p k) g -> p k g", k=KD)).then_inc(later_in, 16)
            act.dma_start(biasr[:, 0:NGR], b_router_grp.to_broadcast([P, NGR])).then_inc(later_in, 16)
            act.dma_start(biasr[:, 8:NL], b_router_exp.to_broadcast([P, NE])).then_inc(later_in, 16)
            act.dma_start(list_dram.rearrange("(p n) o -> p (n o)", p=P), none_u[:, :]).then_inc(later_in, 16)
            act.dma_start(lng[:, :], ln_v_g.to_broadcast([P, AW])).then_inc(later_in, 16)
            act.dma_start(lnb[:, :], ln_v_b.to_broadcast([P, AW])).then_inc(later_in, 16)
            with nc.allow_non_contiguous_dma(reason="eight numbers, for eight partitions"):
                act.dma_start(w00[:, :], w_spatial[:, :, 0, 0].to_broadcast([NS, HD])).then_inc(later_in, 16)
            act.wait_ge(small_in, 32)
            act.activation(sc9[:, :], c9[:, :], ACT.Silu).then_inc(c_silu, 1)

            def x_norm(q, par, half, looped):
                rows = NS if not looped and q == 0 else P
                wait(act, x_in[par], half * 16 + 16)
                wait(act, xT_made, q)
                act.activation(xn[0:rows, :], xbuf[0:rows, par, :], ACT.Square,
                               accum_out=ss[0:rows, par:par + 1]).then_inc(sum_made, 1)
                wait(act, sum_root, q + 1)
                act.activation(xn[0:rows, :], xbuf[0:rows, par, :], ACT.Copy,
                               scale=rstd[0:rows, par:par + 1]).then_inc(x_normed, 1)

            def h_high(q, par, looped):
                cols = NS if not looped and q == 0 else P
                wait(act, h_made, q + 1)
                wait(act, v_mm, q - 1)
                wait(act, hT_kept, q * 2 - 2)
                act.activation(ht_hi[par][:, :, 0:cols], h[:, :, 0:cols], ACT.Copy).then_inc(ht_hi_made, 1)

            def v_gelu_of(q, par, half, looped):
                rows = NS if not looped and q == 0 else P
                wait(act, v_mm, q + 1)
                wait(act, v_out[par], half * 16)
                act.activation(vg[0:rows, par, :], banks(2 + 2 * par, 2)[0:rows, :], ACT.Gelu_apprx_tanh
                               ).then_inc(v_gelu, 1)

            x_norm(0, 0, 0, False)
            for k in range(KD):
                act.wait_ge(w_in_rows[k % 2], 16 * (k // 2 + 1))
                act.activation(wv_hi[:, k, :], wv_raw[:, k % 2, :], ACT.Copy).then_inc(w_hi_k, 1)
            x_norm(1, 1, 0, False)

            def step(q, par, half, looped):
                if looped or q >= 2:
                    v_gelu_of(q - 2, par, half - 1, looped)
                if looped or q < NQ:
                    h_high(q, par, looped)
                if looped or 1 <= q < NQ - 1:
                    x_norm(q + 1, 1 - par, half + par, looped)

            def high(n, slot, count, hslot):
                act.wait_ge(w_inn[slot], count * 16 + 16)
                wait(act, blk_mm, n - 1)
                act.activation(w_hi[hslot][:, :, :], wraw[:, slot], ACT.Copy).then_inc(w_hi_made, 1)

            run_steps(act, step, 0, NQ + 1, 4, 8)
            high(0, 0, 0, 0)
            act.wait_ge(xT_made, NQ)
            high(1, 1, 0, 1)
            step(NQ + 1, (NQ + 1) % 2, (NQ + 1) // 2, False)

            def part_high(q, par, j):
                high(q * 3 + (NG + j), (NG + j) % 3, q + (NG + j) // 3, (par + j) % 2)

            v_over(act)
            for g in range(NG):
                act.wait_ge(blk_mm, g + 1)
                wait(act, p_done, g - 1)
                act.activation(in_thirds(pT[g % 2][:, 16:16 + TOK]), thirds(g % 2), ACT.Copy).then_inc(p_cp, 1)
                if g + 2 < NG:
                    high(g + 2, (g + 2) % 3, (g + 2) // 3, g % 2)
                else:
                    part_high(0, 0, g + 2 - NG)
            act.wait_ge(dS_made, 1)

            def f_step(q, par, half, looped):
                act.wait_ge(blk_mm, q * 3 + (NG + 1))
                wait(act, m1_made, q)
                act.activation(in_thirds(u[:, :]), thirds(par), ACT.Gelu_apprx_tanh).then_inc(u_made, 1)
                part_high(q, par, 2)
                act.wait_ge(blk_mm, q * 3 + (NG + 2))
                wait(act, m2_made, q)
                act.wait_ge(spare_read, q + 1)
                act.activation(in_thirds(ta[:, :]), thirds(1 - par), ACT.Tanh, scale=0.5).then_inc(ta_made, 1)
                if looped or q + 1 < HD:
                    part_high(q + 1, 1 - par, 0)
                act.wait_ge(blk_mm, q * 3 + (NG + 3))
                wait(act, yb1_made, q)
                act.activation(in_thirds(tb[:, :]), thirds(par), ACT.Tanh, scale=0.5).then_inc(tb_made, 1)
                if looped or q + 1 < HD:
                    part_high(q + 1, 1 - par, 1)

            run_steps(act, f_step, 0, HD, 2, HD - 2)

            act.wait_ge(blk_mm, NG + 3 * HD)
            for k in range(KD):
                act.wait_ge(w_in_rows[k // (KD // 2)], 16 * (KD // 2 + 1))
                act.activation(wo_hi[:, k, :], wo_raw[:, k, :], ACT.Copy).then_inc(w_hi_k, 1)
            f_over(act)
            act.dma_start(rws[0:NS].rearrange("p a d -> p (a d)"), mod_dram[0:NS, :]).then_inc(rows_in, 16)
            act.dma_start(g_post1[:, :], g_post_mix.to_broadcast([P, D])).then_inc(rows_in, 16)
            act.dma_start(g_pre2[:, :], g_pre_ffn.to_broadcast([P, D])).then_inc(rows_in, 16)
            for t, a in ((G1b, R_G1), (A2b, R_A2), (B2b, R_B2), (G2b, R_G2)):
                act.dma_start(t[:, :], mod_dram[PRM:NC, a * D:(a + 1) * D].to_broadcast([P, D])
                              ).then_inc(more_rows_in, 16)
            act.dma_start(g_post2[:, :], g_post_ffn.to_broadcast([P, D])).then_inc(more_rows_in, 16)

            def m_high(q, par, half, looped):
                wait(act, y_mm, q - 1)
                cols = rows_of(q, looped)
                act.wait_ge(mt_in[par], half * 16 + 16)
                act.activation(mt_hi[par][:, :, 0:cols], mt[:, par, :, 0:cols], ACT.Copy).then_inc(ht_hi_made, 1)

            def y_square(q, par, looped):
                r = rows_of(q, looped)
                wait_apart(act, y_mm, q + 1, passed)
                act.activation(x2[0:r, bass.ds(q, 1), :].rearrange("p a d -> p (a d)"), banks(2 * par, 2)[0:r, :],
                               ACT.Square, accum_out=ss2[0:r, par:par + 1]).then_inc(sum_made, 1)

            def x2_square(q, par, half, looped):
                r = rows_of(q, looped)
                wait_apart_if(act, h2_out[par], half * 16, passed)
                wait_apart_if(act, h2_tr, q - 1, passed)
                wait_apart(act, x2_made, q + 1, passed)
                act.activation(h2[0:r, par, :], x2[0:r, bass.ds(q, 1), :].rearrange("p a d -> p (a d)"),
                               ACT.Square, accum_out=ss2[0:r, 2 + par:3 + par]).then_inc(sum2_made, 1)

            def h2_turned(q, par, looped):
                cols = rows_of(q, looped)
                act.wait_ge(h2_tr, q + 1)
                wait(act, lg_mm, q - 1)
                act.activation(h2T[:, par, :, 0:cols],
                               banks(4, 2)[:, 0:KD * cols].rearrange("p (k n) -> p k n", n=cols), ACT.Copy
                               ).then_inc(h2T_made, 1)

            def exps(q, looped):
                r = rows_of(q, looped)
                act.wait_ge(route, q * RC + 11)
                act.activation(exg[0:r, :], lg[0:r, 0:NGR], ACT.Exp, bias=ngm[0:r, :],
                               accum_out=se[0:r, :]).then_inc(exp_made, 1)
                act.activation(e12[0:r, :], dm[0:r, :], ACT.Exp).then_inc(exp2_made, 1)

            m_high(0, 0, 0, False)

            def w_step(q, par, half, looped):
                if looped or 1 <= q <= NQ:
                    y_square(q - 1, 1 - par, looped or q > 1)
                if looped or q >= 3:
                    exps(q - 3, looped or q > 3)
                if looped or 1 <= q <= NQ:
                    x2_square(q - 1, 1 - par, half - (1 - par), looped or q > 1)
                if looped or q + 1 < NQ:
                    m_high(q + 1, 1 - par, half + par, looped or True)
                if looped or 2 <= q <= NQ + 1:
                    h2_turned(q - 2, par, looped or q > 2)

            run_steps(act, w_step, 0, NQ + 3, 4, 8)

            act.wait_ge(lg_mm, NQ)

            def turned_b(n, s):
                par = s % 2
                act.wait_ge(hg_tr, n + 1)
                wait(act, gu_mm, n - 1)
                act.activation(hgT[par][:, 4:8, :].rearrange("p k n -> p (k n)"), PS[:, 1, :], ACT.Copy
                               ).then_inc(hgT_b, 1)

            def store_e(n, s, uses):
                par = s % 2
                act.wait_ge(down_mm, n + 1)
                wait(act, eo_out[par], uses * 16)
                act.activation(ysb[:, par, :], banks(5, 2), ACT.Copy).then_inc(ysb_made, 1)

            def e_step(n, s, oct_, looped):
                par = s % 2
                if looped or n + 1 < NE:
                    turned_b(n + 1, s + 1)
                if looped or n < NE:
                    act.wait_ge(gu_mm, n + 1)
                    wait(act, act_made, n - 1)
                    act.activation(sil[:, par, :], PS[:, 2 + par, 0:P], ACT.Silu).then_inc(silu_made, 1)
                if looped or n >= 1:
                    store_e(n - 1, s + 1, oct_ * (RING // 2) + (s - 1) // 2)

            turned_b(0, 0)
            run_steps(act, e_step, 0, NE + 1, RING, NE - RING, RING)

            act.wait_ge(cnt_made, 2)
            fullest = act.value_load(most_u[0:1, 0:1], min_val=0, max_val=TOK)
            with act.If(fullest > P):
                with act.Fori(1, NQ) as c:
                    with act.Fori(0, NE) as x:
                        act.wait_ge(o_pe, ((c - 1) * NE + x) * 3 + 2)
                        act.activation(sil[:, 0, :], PS[:, 2, 0:P], ACT.Silu).then_inc(o_act, 1)

            def f1_of(q, par, half, looped):
                r = rows_of(q, looped)
                wait_apart(act, x_in[par], half * 16 + (2 * X_IN[par] + 16), passed)
                wait_apart_if(act, f_made, q - 1, passed)
                act.activation(f1[0:r, par, :], yg[0:r, par, 0, :], ACT.Copy, scale=wts[0:r, bass.ds(q, 1), 0]
                               ).then_inc(f1_made, 1)

            f1_of(0, 0, 0, False)

            def end_step(q, par, half, looped):
                r = rows_of(q, looped)
                if looped or q + 1 < NQ:
                    f1_of(q + 1, 1 - par, half + par, looped or True)
                act.wait_ge(f_made, q + 1)
                act.activation(fj[0:r, par, :], ff[0:r, par, :], ACT.Square, accum_out=ss[0:r, par:par + 1]
                               ).then_inc(sum_made, 1)

            run_steps(act, end_step, 0, NQ, 2, 8)

        @block.vector
        def _(dve):
            dve.wait_ge(pre_tr, KD)
            dve.tensor_copy(cT[:, :, :].rearrange("p k n -> p (k n)"), PS[:, 6, 0:KD * NC]).then_inc(pre_cp, 1)
            dve.wait_ge(pre_tr, KD + 1)
            dve.tensor_copy(vecT[:, :], PS[:, 7, 0:NV]).then_inc(pre_cp, 1)

            dve.wait_ge(pre_cp, 2)
            for k in range(KD):
                dve.wait_ge(w_hi_k, k + 1)
                dve.tensor_tensor(wv_lo[:, k, :], wv_raw[:, k % 2, :], wv_hi[:, k, :].bitcast(F32),
                                  ALU.subtract).then_inc(w_lo_k, 1)
                dve.wait_ge(ada_mm, k + 1)
                dve.tensor_copy(rows0[:, k * CH:(k + 1) * CH], PS[0:NC, 2 + k % 4, 0:CH]).then_inc(mod_made, 1)
            dve.wait_ge(mod_tr, NADA_V)
            dve.tensor_tensor(modT[:, :, :], PS[:, 6, 0:2 * KD * NC].rearrange("p (m n) -> p m n", n=NC),
                              vecT[:, 0:2 * KD].unsqueeze(2).to_broadcast([P, 2 * KD, NC]), ALU.add
                              ).then_inc(prep_made, 1)
            dve.wait_ge(prep_made, 1)
            dve.scalar_tensor_tensor(A1T[:, :, :], modT[:, KD:2 * KD, :], 1.0,
                                     vecT[:, VEC["pre_mix"]:VEC["pre_mix"] + KD].unsqueeze(2)
                                     .to_broadcast([P, KD, NC]), ALU.add, ALU.mult).then_inc(prep_made, 1)
            dve.tensor_scalar(psh[:, :], vecT[:, VEC["pool_scale"]:VEC["pool_scale"] + KD], 0.5, None,
                              ALU.mult).then_inc(prep_made, 1)
            dve.wait_ge(later_in, LATER)
            dve.wait_ge(consts, 2)
            dve.tensor_tensor(w00d[:, :, :], w00[:, :].unsqueeze(2).to_broadcast([NS, HD, NS]),
                              ident[0:NS, 0:NS].unsqueeze(1).to_broadcast([NS, HD, NS]), ALU.mult
                              ).then_inc(prep_made, 1)
            dve.reciprocal(invc[:, :], inv_n[:, :]).then_inc(prep_made, 1)
            dve.wait_ge(prep_made, 2)

            def h_of(q, par, looped):
                sample = not looped and q == 0
                cols = NS if sample else P
                sl = slice(0, NS) if sample else slice(PRM, PRM + 1)
                ps = banks(0, 2)[:, 0:KD * cols].rearrange("p (k n) -> p k n", n=cols)
                wait(dve, xT_made, q + 1)
                wait(dve, ht_lo_made, q)
                dve.tensor_tensor(h[:, :, 0:cols], ps, A1T[:, :, sl].to_broadcast([P, KD, cols]), ALU.mult
                                  ).then_inc(h_scaled, 1)
                dve.wait_ge(h_scaled, q + 1)
                dve.tensor_tensor(h[:, :, 0:cols], h[:, :, 0:cols],
                                  modT[:, 0:KD, sl].to_broadcast([P, KD, cols]), ALU.add
                                  ).then_inc(h_made, 1)

            def h_low(q, par, looped):
                cols = NS if not looped and q == 0 else P
                wait(dve, ht_hi_made, q + 1)
                dve.tensor_tensor(ht_lo[par][:, :, 0:cols], h[:, :, 0:cols],
                                  ht_hi[par][:, :, 0:cols].bitcast(F32), ALU.subtract).then_inc(ht_lo_made, 1)

            def v_stats(q, par, looped):
                rows = NS if not looped and q == 0 else P
                wait(dve, v_gelu, q + 1)
                for j in range(2):
                    b = dve.bn_stats(bn6[0:rows, j, :], vg[0:rows, par, j * 512:(j + 1) * 512])
                b.then_inc(v_bn, 1)
                wait_apart(dve, v_bn, q + 1, passed)
                dve.bn_aggr(mv[0:rows, :], bn6[0:rows, :, :].rearrange("p a b -> p (a b)")).then_inc(sum2_made, 1)

            def v_norm(q, par, looped):
                rows = NS if not looped and q == 0 else P
                t = vg[0:rows, par, :]
                wait(dve, sum2_root, q + 1)
                dve.tensor_scalar(t, t, mv[0:rows, 0:1], vr[0:rows, :], ALU.subtract, ALU.mult
                                  ).then_inc(v_step, 1)
                dve.wait_ge(v_step, q * 2 + 1)
                dve.tensor_tensor(t, t, lng[0:rows, :], ALU.mult).then_inc(v_step, 1)
                dve.wait_ge(v_step, q * 2 + 2)
                dve.tensor_tensor(t, t, lnb[0:rows, :], ALU.add).then_inc(v_made, 1)

            dve.wait_ge(later_in, LATER)

            def step(q, par, half, looped):
                if looped or q < NQ:
                    h_of(q, par, looped)
                if looped or q >= 2:
                    v_stats(q - 2, par, looped)
                if looped or q < NQ:
                    h_low(q, par, looped)
                if looped or q >= 2:
                    v_norm(q - 2, par, looped)

            run_steps(dve, step, 0, NQ + 1, 4, 8)

            def low(n, slot, hslot):
                dve.wait_ge(w_hi_made, n + 1)
                dve.tensor_tensor(w_lo[hslot][:, :, :], wraw[:, slot], w_hi[hslot][:, :, :].bitcast(F32),
                                  ALU.subtract).then_inc(w_lo_made, 1)

            low(0, 0, 0)
            dve.wait_ge(v_mm, NQ - 1)
            dve.wait_ge(hT_kept, 2 * NQ - 2)
            low(1, 1, 1)
            step(NQ + 1, (NQ + 1) % 2, (NQ + 1) // 2, False)
            v_over(dve)
            for t in pT:
                z = dve.memset(t[:, 0:16], 0.0)
            z.then_inc(p_step, 1)
            dve.wait_ge(p_step, 1)

            done = 1

            def link(ins):
                nonlocal done
                ins.then_inc(p_step, 1)
                done += 1
                dve.wait_ge(p_step, done)

            def pool_group(g):
                w = 2 << g
                src = pT[g % 2]
                dve.wait_ge(p_cp, g + 1)
                dve.tensor_copy(ptail[:, g, :], src[:, 16 + SEQ - PST:16 + SEQ])
                dve.tensor_copy(psm[:, g, :], src[:, 16 + SEQ:16 + TOK])
                at, wide = src, 1
                while wide < w:
                    out = pa if at is not pa else pb
                    low_ = 2 * wide - 1
                    link(dve.tensor_tensor(out[:, low_:16 + SEQ], at[:, low_:16 + SEQ],
                                           at[:, low_ - wide:16 + SEQ - wide], ALU.add))
                    at, wide = out, 2 * wide
                dst = dT[:, g, 0:SEQ]
                link(dve.scalar_tensor_tensor(dst, at[:, 16:16 + SEQ], 1.0 / w, src[:, 16:16 + SEQ], ALU.mult, ALU.subtract))
                link(dve.tensor_tensor(fix[:, 0:w], at[:, 16:16 + w], invc[:, 0:w], ALU.mult))
                dve.tensor_tensor(dT[:, g, 0:w], fix[:, 0:w], src[:, 16:16 + w], ALU.subtract
                                  ).then_inc(p_done, 1)

            dve.wait_ge(prep_made, 5)

            def part_low(q, par, j):
                low(q * 3 + (NG + j), (NG + j) % 3, (par + j) % 2)

            def flat(ap):
                return ap.rearrange("p h n -> p (h n)")

            for g in range(NG):
                if g + 2 < NG:
                    low(g + 2, (g + 2) % 3, g % 2)
                else:
                    part_low(0, 0, g + 2 - NG)
                pool_group(g)
                if g == 1:
                    dve.wait_ge(ws_tr, 1)
                    dve.tensor_copy(flat(spT[:, :, :]), PS[:, MIX, 0:NG * NS * PST]).then_inc(ws_cp, 1)
                    dve.wait_ge(ws_tr, 2)
                    dve.tensor_copy(flat(wsT[:, 4:8, :]), PS[:, MIX + 1, :]).then_inc(ws_cp, 1)
                if g == 2:
                    dve.wait_ge(ws_tr, 3)
                    dve.tensor_copy(flat(wsT[:, 0:4, :]), PS[:, MIX, :]).then_inc(ws_cp, 1)
            for g in range(NG):
                w = 2 << g
                link(dve.tensor_reduce(pws[:, g, :], spT[:, g, :].rearrange("p (n r) -> p n r", r=PST)
                                       [:, :, PST - (w - 1):PST], AX_X, ALU.add))
            link(dve.tensor_tensor(pws[:, :, :], pws[:, :, :], psm[:, :, :], ALU.add))
            for g in range(NG):
                d = dve.scalar_tensor_tensor(dT[:, g, SEQ:TOK], pws[:, g, :], 1.0 / (2 << g), psm[:, g, :],
                                             ALU.mult, ALU.subtract)
            d.then_inc(dS_made, 1)
            dve.wait_ge(tail_tr, 1)
            dve.tensor_copy(ptok[:, :], PS[0:PST, MIX, :])
            dve.tensor_copy(pstok[:, :], PS[0:NS, MIX + 1, :]).then_inc(tail_cp, 1)

            def f_step(q, par, half, looped):
                part_low(q, par, 2)
                wait(dve, mod_out[par], half * 16)
                dve.wait_ge(wpl_in[par], half * 32 + 32)
                dve.wait_ge(ada_mm, q * 2 + (NADA_V + 2))
                dve.tensor_tensor(rowbuf[:, par, :], PS[0:NC, MIX, :], bias[:, par, :], ALU.add).then_inc(mod_made, 1)
                bank = REGION[1 - par]
                dve.wait_ge(blk_mm, q * 3 + (NG + 2))
                wait(dve, mg_made, q)
                dve.tensor_scalar(m0[:, SEQ:TOK], PS[:, bank, SMIX_AT:SMIX_AT + NS],
                                  bsb[:, bass.ds(q, 1), 0:1].rearrange("p a n -> p (a n)"), None, ALU.add)
                dve.tensor_copy(ybs[:, :], PS[:, bank, SYB_AT:SYB_AT + NS]).then_inc(spare_read, 1)
                dve.wait_ge(mix_mm, q + 1)
                dve.tensor_tensor(m0[:, 0:SEQ].rearrange("p (t i) -> p t i", i=P),
                                  banks(MIX, 2).rearrange("p (t i) -> p t i", i=P),
                                  bsb[:, bass.ds(q, 1), :].to_broadcast([P, NT, P]), ALU.add
                                  ).then_inc(m0_made, 1)
                dve.wait_ge(m0_made, q + 1)
                dve.wait_ge(u_made, q + 1)
                dve.scalar_tensor_tensor(m0[:, :], m0[:, :], 0.5, u[:, :], ALU.mult, ALU.mult
                                         ).then_inc(m1_made, 1)
                dve.wait_ge(m1_made, q + 1)
                dve.wait_ge(ta_made, q + 1)
                dve.scalar_tensor_tensor(m0[:, :], ta[:, :], 1.0, m0[:, :], ALU.add, ALU.mult
                                         ).then_inc(m2_made, 1)
                if looped or q + 1 < HD:
                    part_low(q + 1, 1 - par, 0)
                dve.wait_ge(tb_made, q + 1)
                dve.scalar_tensor_tensor(yb1[:, SEQ:TOK], tb[:, SEQ:TOK], 1.0, ybs[:, :], ALU.add, ALU.mult)
                dve.wait_ge(yb_mm, q + 1)
                dve.scalar_tensor_tensor(yb1[:, 0:SEQ], tb[:, 0:SEQ], 1.0, banks(MIX, 2), ALU.add, ALU.mult
                                         ).then_inc(yb1_made, 1)
                if looped or q + 1 < HD:
                    part_low(q + 1, 1 - par, 1)
                dve.wait_ge(yb1_made, q + 1)
                dve.wait_ge(m2_made, q + 1)
                wait(dve, mg_out[par], half * 16)
                if not looped and q == 1:
                    dve.wait_ge(st_out, 32)
                dve.scalar_tensor_tensor(mg[:, par, :], yb1[:, :], psh[:, bass.ds(q, 1)], m0[:, :],
                                         ALU.mult, ALU.add).then_inc(mg_made, 1)

            run_steps(dve, f_step, 0, HD, 2, HD - 2)

            for k in range(KD):
                dve.wait_ge(w_hi_k, KD + k + 1)
                dve.tensor_tensor(wo_lo[:, k, :], wo_raw[:, k, :], wo_hi[:, k, :].bitcast(F32),
                                  ALU.subtract).then_inc(w_lo_k, 1)
            f_over(dve)

            def m_low(q, par, looped):
                cols = rows_of(q, looped)
                dve.wait_ge(ht_hi_made, q + (NQ + 1))
                dve.tensor_tensor(mt_lo[par][:, :, 0:cols], mt[:, par, :, 0:cols], mt_hi[par][:, :, 0:cols].bitcast(F32),
                                  ALU.subtract).then_inc(ht_lo_made, 1)

            def turned(ap):
                return ap.rearrange("q (p k) -> q k p", k=KD)

            def straight(ap):
                return ap.rearrange("q (k p) -> q k p", k=KD)

            def x2_at(q, r):
                return x2[0:r, bass.ds(q, 1), :].rearrange("p a d -> p (a d)")

            def residual(q, par, half, looped):
                r = rows_of(q, looped)
                g1 = rws[0:NS, R_G1, :] if r == NS else G1b[:, :]
                dve.wait_ge(sum_root, q + (NQ + 1))
                dve.scalar_tensor_tensor(yt[0:r, :], banks(2 * par, 2)[0:r, :], rs2[0:r, par:par + 1], g1,
                                         ALU.mult, ALU.mult).then_inc(y_scaled, 1)
                dve.wait_ge(y_scaled, q + 1)
                dve.wait_ge(x_in[par], half * 16 + (X_IN[par] + 16))
                dve.tensor_tensor(x2_at(q, r), yt[0:r, :], xw[0:r, par, :], ALU.add).then_inc(x2_made, 1)

            def modulate(q, par, looped):
                r = rows_of(q, looped)
                if r == NS:
                    a2, b2 = turned(rws[0:NS, R_A2, :]), turned(rws[0:NS, R_B2, :])
                else:
                    a2, b2 = turned(A2b[:, :]), turned(B2b[:, :])
                out = straight(h2[0:r, par, :])
                dve.wait_ge(sum2_root, q + (NQ + 1))
                dve.scalar_tensor_tensor(out, turned(x2_at(q, r)), rs2[0:r, 2 + par:3 + par], a2,
                                         ALU.mult, ALU.mult).then_inc(h2_scaled, 1)
                dve.wait_ge(h2_scaled, q + 1)
                dve.tensor_tensor(out, out, b2, ALU.add).then_inc(h2_made, 1)

            def chain(sm, base):
                n = 0

                def link(ins):
                    nonlocal n
                    n += 1
                    ins.then_inc(sm, 1)
                    wait_apart(dve, sm, base + n, passed)
                    return n
                return link

            def route_of(q, looped):
                r = rows_of(q, looped)
                link = chain(route, q * RC)
                dve.wait_ge(lg_mm, q + 1)
                dve.tensor_tensor(lg[0:r, :], PS[0:r, 6, 0:NL], biasr[0:r, :], ALU.add).then_inc(lg_made, 1)
                wait_apart(dve, lg_made, q + 1, passed)
                link(dve.max(gtop[0:r, :], lg[0:r, 0:8]))
                link(dve.max_index(gix[0:r, :], gtop[0:r, :], lg[0:r, 0:8]))
                link(dve.tensor_copy(gid[0:r, :], gix[0:r, 0:1]))
                link(dve.tensor_scalar(ohg[0:r, :], iota8[0:r, 0:NGR], gid[0:r, :], None, ALU.is_equal))
                link(dve.tensor_tensor(t32[0:r, :].rearrange("p (g e) -> p g e", e=EPG),
                                       lg[0:r, 8:NL].rearrange("p (g e) -> p g e", e=EPG),
                                       ohg[0:r, :].unsqueeze(2).to_broadcast([r, NGR, EPG]), ALU.mult))
                link(dve.tensor_reduce(s8[0:r, :], t32[0:r, :].rearrange("p (g e) -> p e g", e=EPG), AX_X, ALU.add))
                link(dve.max(etop[0:r, :], s8[0:r, :]))
                link(dve.max_index(eix[0:r, :], etop[0:r, :], s8[0:r, :]))
                link(dve.tensor_copy(ei[0:r, :], eix[0:r, 0:2]))
                link(dve.tensor_scalar(ngm[0:r, :], gtop[0:r, 0:1], -1.0, None, ALU.mult))
                link(dve.tensor_tensor(dm[0:r, :], etop[0:r, 1:2], etop[0:r, 0:1], ALU.subtract))
                link(dve.tensor_tensor(oh12[0:r, :, :], iota8[0:r, :].unsqueeze(1).to_broadcast([r, 2, 8]),
                                       ei[0:r, :].unsqueeze(2).to_broadcast([r, 2, 8]), ALU.is_equal))
                for j in range(2):
                    x = dve.tensor_tensor(m12[0:r, j, :].rearrange("p (g e) -> p g e", e=EPG),
                                          ohg[0:r, :].unsqueeze(2).to_broadcast([r, NGR, EPG]),
                                          oh12[0:r, j, :].unsqueeze(1).to_broadcast([r, NGR, EPG]), ALU.mult)
                n = link(x)
                assert n == 13
                dve.tensor_tensor(mb[0:r, :], m12[0:r, 0, :], m12[0:r, 1, :], ALU.add).then_inc(m_made, 1)
                dve.scalar_tensor_tensor(eid[0:r, :], gid[0:r, :].to_broadcast([r, 2]), float(EPG), ei[0:r, :],
                                         ALU.mult, ALU.add).then_inc(eid_made, 1)

            def weights_of(q, looped):
                r = rows_of(q, looped)
                wait_apart(dve, exp2_made, q + 1, passed)
                dve.tensor_scalar(e1[0:r, :], e12[0:r, :], 1.0, None, ALU.add)
                dve.reciprocal(pg[0:r, :], se[0:r, :]).then_inc(route, 1)
                wait_apart(dve, route, q * RC + 14, passed)
                dve.reciprocal(rw[0:r, :], e1[0:r, :]).then_inc(route, 1)
                wait_apart(dve, route, q * RC + 15, passed)
                dve.tensor_tensor(wts[0:r, bass.ds(q, 1), 0], rw[0:r, :], pg[0:r, :], ALU.mult).then_inc(route, 1)
                wait_apart(dve, route, q * RC + 16, passed)
                dve.tensor_tensor(wts[0:r, bass.ds(q, 1), 1], wts[0:r, bass.ds(q, 1), 0], e12[0:r, :], ALU.mult
                                  ).then_inc(wts_made, 1)

            def slots_of(q, par, half, looped):
                r = rows_of(q, looped)
                wait_apart(dve, pos_mm, q + 1, passed)
                dve.tensor_tensor(mp[0:r, :, :], PS[0:r, 7, 0:NE].unsqueeze(1).to_broadcast([r, 2, NE]),
                                  m12[0:r, :, :], ALU.mult).then_inc(mp_made, 1)
                dve.wait_ge(eid_made, q + 1)
                dve.tensor_tensor(mrun[0:r, :], mrun[0:r, :], mb[0:r, :], ALU.add).then_inc(mrun_made, 1)
                wait_apart(dve, mp_made, q + 1, passed)
                wait_apart_if(dve, scat[par], half * 32, passed)
                dve.tensor_copy(tidu[0:r, par, :, 0], tid[0:r, :].to_broadcast([r, 2]))
                for j in range(2):
                    dve.tensor_scalar(tidu[0:r, par, j, 1:2], tid[0:r, :], 2.0, float(j), ALU.mult, ALU.add)
                dve.tensor_reduce(pos[0:r, :], mp[0:r, :, :], AX_X, ALU.add).then_inc(slot_step, 1)
                wait_apart(dve, slot_step, q * SC + 1, passed)
                for j in range(2):
                    z = dve.scalar_tensor_tensor(lrow[par][j][0:r, :], pos[0:r, j:j + 1], float(NE), eid[0:r, j:j + 1],
                                                 ALU.mult, ALU.add)
                z.then_inc(slot_made, 1)
                dve.tensor_scalar(tid[:, :], tid[:, :], float(-SEQ if r == NS else P), None, ALU.add
                                  ).then_inc(slot_step, 1)
                wait_apart(dve, slot_step, q * SC + 2, passed)

            m_low(0, 0, False)
            dve.wait_ge(rows_in, 16 * 3)
            dve.tensor_tensor(rws[0:NS, R_G1], rws[0:NS, R_G1], g_post1[0:NS, :], ALU.mult).then_inc(rows_made, 1)
            dve.scalar_tensor_tensor(rws[0:NS, R_A2], rws[0:NS, R_A2], 1.0, g_pre2[0:NS, :], ALU.add, ALU.mult
                                     ).then_inc(rows_made, 1)
            dve.wait_ge(more_rows_in, 16 * 5)
            dve.tensor_tensor(G1b[:, :], G1b[:, :], g_post1[:, :], ALU.mult).then_inc(rows_made, 1)
            dve.scalar_tensor_tensor(A2b[:, :], A2b[:, :], 1.0, g_pre2[:, :], ALU.add, ALU.mult).then_inc(rows_made, 1)
            dve.tensor_tensor(G2b[:, :], G2b[:, :], g_post2[:, :], ALU.mult).then_inc(rows_made, 1)
            dve.tensor_tensor(rws[0:NS, R_G2], rws[0:NS, R_G2], g_post2[0:NS, :], ALU.mult).then_inc(rows_made, 1)
            dve.wait_ge(rows_made, 6)
            dve.wait_ge(later_in, LATER)

            def w_step(q, par, half, looped):
                if looped or q >= 3:
                    route_of(q - 3, looped or q > 3)
                if looped or 1 <= q <= NQ:
                    residual(q - 1, 1 - par, half - (1 - par), looped or q > 1)
                if looped or q >= 3:
                    weights_of(q - 3, looped or q > 3)
                if looped or 1 <= q <= NQ:
                    modulate(q - 1, 1 - par, looped or q > 1)
                if looped or q + 1 < NQ:
                    m_low(q + 1, 1 - par, looped or True)
                if looped or q >= 3:
                    slots_of(q - 3, 1 - par, half + par - 2, looped or q > 3)

            run_steps(dve, w_step, 0, NQ + 3, 4, 8)
            dve.wait_ge(cnt_mm, 1)
            dve.tensor_reduce(most[:, :], PS[:, 7, 0:NE], AX_X, ALU.max).then_inc(cnt_made, 1)
            dve.wait_ge(cnt_made, 1)
            dve.tensor_copy(most_u[:, :], most[:, :]).then_inc(cnt_made, 1)

            def turned_a(n, s):
                par = s % 2
                dve.wait_ge(hg_tr, n + 1)
                wait(dve, gu_mm, n - 1)
                dve.tensor_copy(hgT[par][:, 0:4, :].rearrange("p k n -> p (k n)"), PS[:, 0, :]).then_inc(hgT_a, 1)

            def e_step(n, s, oct_, looped):
                par = s % 2
                if looped or n + 1 < NE:
                    turned_a(n + 1, s + 1)
                dve.wait_ge(silu_made, n + 1)
                wait(dve, down_mm, n - 1)
                dve.tensor_tensor(actT[:, par, :], PS[:, 2 + par, P:2 * P], sil[:, par, :], ALU.mult
                                  ).then_inc(act_made, 1)

            turned_a(0, 0)
            run_steps(dve, e_step, 0, NE, RING, NE - RING, RING)

            fullest = dve.value_load(most_u[0:1, 0:1], min_val=0, max_val=TOK)
            with dve.If(fullest > P):
                with dve.Fori(1, NQ) as c:
                    with dve.Fori(0, NE) as x:
                        m = (c - 1) * NE + x
                        dve.wait_ge(o_pe, m * 3 + 1)
                        dve.tensor_copy(hgT[0][:, :, :].rearrange("p k n -> p (k n)"), banks(0, 2)
                                        ).then_inc(o_dve, 1)
                        dve.wait_ge(o_act, m + 1)
                        dve.tensor_tensor(actT[:, 0, :], PS[:, 2, P:2 * P], sil[:, 0, :], ALU.mult
                                          ).then_inc(o_dve, 1)
                        dve.wait_ge(o_pe, m * 3 + 3)
                        dve.tensor_copy(ysb[:, 0, :], banks(5, 2)).then_inc(o_dve, 1)

            def sum_of(q, par, half, looped):
                r = rows_of(q, looped)
                dve.wait_ge(f1_made, q + 1)
                dve.wait_ge(x_in[par], half * 16 + (2 * X_IN[par] + 16))
                wait(dve, f_scaled, q - 1)
                dve.scalar_tensor_tensor(ff[0:r, par, :], yg[0:r, par, 1, :], wts[0:r, bass.ds(q, 1), 1],
                                         f1[0:r, par, :], ALU.mult, ALU.add).then_inc(f_made, 1)

            def end_step(q, par, half, looped):
                r = rows_of(q, looped)
                g2 = rws[0:NS, R_G2, :] if r == NS else G2b[:, :]
                if looped or q + 1 < NQ:
                    sum_of(q + 1, 1 - par, half + par, looped or True)
                dve.wait_ge(sum_root, q + (2 * NQ + 1))
                wait(dve, y_out[par], half * 16)
                dve.scalar_tensor_tensor(fo[0:r, par, :], ff[0:r, par, :], rstd[0:r, par:par + 1], g2,
                                         ALU.mult, ALU.mult).then_inc(f_scaled, 1)
                dve.wait_ge(f_scaled, q + 1)
                dve.tensor_tensor(fo[0:r, par, :], fo[0:r, par, :], x2_at(q, r), ALU.add).then_inc(fo_made, 1)

            sum_of(0, 0, 0, False)
            run_steps(dve, end_step, 0, NQ, 2, 8)

        @block.tensor
        def _(pe):
            pe.wait_ge(consts, 2)
            pe.wait_ge(c_silu, 1)
            for k in range(KD):
                pe.transpose(PS[:, 6, k * NC:(k + 1) * NC], sc9[:, k * P:(k + 1) * P], ident[0:NC, 0:NC]
                             ).then_inc(pre_tr, 1)
            pe.wait_ge(vec_in, 16 * 3)
            pe.transpose(PS[:, 7, 0:NV], vecs[:, :], ident[0:NV, 0:NV]).then_inc(pre_tr, 1)

            def ada_chunk(slot, ring, uses, bank, col):
                pe.wait_ge(ada_in[slot], uses * 16 + 16)
                for k in range(KD):
                    mm = pe.matmul(PS[0:NC, bank, col:col + CH], cT[:, k, :], ring[:, slot, k, :],
                                   start=(k == 0), stop=(k == KD - 1))
                mm.then_inc(ada_mm, 1)

            def turn_rows(n):
                pe.wait_ge(mod_made, n + 1)
                for m in range(n * CPM, (n + 1) * CPM):
                    mm = pe.transpose(PS[:, 6, m * NC:(m + 1) * NC], rows0[:, m * P:(m + 1) * P], ident[0:NC, 0:NC])
                mm.then_inc(mod_tr, 1)

            def x_turn(q, looped):
                rows = NS if not looped and q == 0 else P
                wait(pe, x_normed, q + 1)
                wait(pe, h_scaled, q)
                for k in range(KD):
                    mm = pe.transpose(banks(0, 2)[:, k * rows:(k + 1) * rows], xn[0:rows, k * P:(k + 1) * P],
                                      ident[0:rows, 0:rows])
                mm.then_inc(xT_made, 1)

            def v_of(q, par, looped):
                rows = NS if not looped and q == 0 else P
                wait(pe, ht_lo_made, q + 1)
                wait(pe, v_gelu, q - 1)
                for half in range(2):
                    cols = slice(half * 512, (half + 1) * 512)
                    out = PS[0:rows, 2 + 2 * par + half, :]
                    n = 0
                    for k in range(KD):
                        for a, b in ((ht_hi, wv_hi), (ht_hi, wv_lo), (ht_lo, wv_hi)):
                            mm = pe.matmul(out, a[par][:, k, 0:rows], b[:, k, cols], start=(n == 0),
                                           stop=(n == 3 * KD - 1))
                            n += 1
                mm.then_inc(v_mm, 1)

            pe.wait_ge(pre_cp, 1)
            for n in range(NADA_V):
                wait(pe, mod_made, n - 3)
                ada_chunk(n % 4, adaV, n // 4, 2 + n % 4, 0)
                if n:
                    turn_rows(n - 1)
            turn_rows(NADA_V - 1)
            x_turn(0, False)
            pe.wait_ge(w_lo_k, KD)

            def step(q, par, half, looped):
                if looped or q < NQ:
                    x_turn(q, looped)
                v_of(q - 1, 1 - par, looped)

            run_steps(pe, step, 1, NQ + 1, 2, 8)

            def project(n, hslot, region):
                pe.wait_ge(w_lo_made, n + 1)
                for k in range(KD):
                    for j, (a, b) in enumerate(((w_hi, hT_hi), (w_hi, hT_lo), (w_lo, hT_hi))):
                        for t in range(3):
                            mm = pe.matmul(PS[:, REGION[region] + t, 0:THIRD], a[hslot][:, k, :],
                                           b[:, k, t * THIRD:(t + 1) * THIRD], start=(k == 0 and j == 0),
                                           stop=(k == KD - 1 and j == 2))
                mm.then_inc(blk_mm, 1)

            pe.wait_ge(prep_made, 4)
            pe.wait_ge(hT_kept, 2 * NQ)
            pe.wait_ge(v_gelu, NQ - 1)
            project(0, 0, 0)
            pe.wait_ge(v_gelu, NQ)
            project(1, 1, 1)
            pe.wait_ge(fc_in, 48)
            for g in range(NG):
                mm = pe.transpose(PS[:, MIX, g * NS * PST:(g + 1) * NS * PST], spr[:, g * P:(g + 1) * P],
                                  ident[0:NS * PST, 0:NS * PST])
            mm.then_inc(ws_tr, 1)

            def turn_maps(first, bank):
                for j in range(4):
                    mm = pe.transpose(PS[:, bank, j * P:(j + 1) * P], ws[:, first + j, :], ident[:, :])
                mm.then_inc(ws_tr, 1)

            pe.wait_ge(ws_masked, 1)
            turn_maps(4, MIX + 1)
            pe.wait_ge(p_cp, 1)
            project(2, 0, 0)
            pe.wait_ge(ws_cp, 1)
            turn_maps(0, MIX)
            pe.wait_ge(p_cp, 2)
            project(3, 1, 1)

            def part(q, par, j):
                project(q * 3 + (NG + j), (par + j) % 2, (par + j) % 2)

            def tails():
                pe.wait_ge(dS_made, 1)
                pe.wait_ge(ws_cp, 3)
                for g in range(NG):
                    pe.transpose(PS[0:PST, MIX, g * P:(g + 1) * P], ptail[:, g, :], ident[:, :])
                for g in range(NG):
                    mm = pe.transpose(PS[0:NS, MIX + 1, g * P:(g + 1) * P], psm[:, g, :], ident[:, :])
                mm.then_inc(tail_tr, 1)

            def f_step(q, par, half, looped):
                first = not looped and q == 0
                if first:
                    pe.wait_ge(p_cp, NG - 1)
                else:
                    pe.wait_ge(ta_made, q)
                part(q, par, 0)
                if first:
                    tails()
                    pe.wait_ge(tail_cp, 1)
                else:
                    pe.wait_ge(yb1_made, q)
                for a in range(2):
                    ada_chunk(2 * par + a, adaF, half + NADA_V // 4, MIX, a * CH)
                if first:
                    pe.wait_ge(p_cp, NG)
                else:
                    pe.wait_ge(tb_made, q)
                bank = REGION[1 - par]
                pe.wait_ge(vfs_in[par], half * 16 + 16)
                pe.matmul(PS[:, bank, SMIX_AT:SMIX_AT + NS], vfs[:, par, :],
                          w00d[:, bass.ds(q, 1), :].rearrange("p a i -> p (a i)"), start=True, stop=True)
                pe.wait_ge(wpl_in[par], half * 32 + 32)
                pe.matmul(PS[:, bank, SYB_AT:SYB_AT + NS], wpl[:, par, :],
                          dT[:, bass.ds(half, 1), SEQ:TOK].rearrange("p a n -> p (a n)"), start=True, stop=True)
                part(q, par, 1)
                pe.wait_ge(vf_in[par], half * 16 + 16)
                pe.wait_ge(mod_made, q + (NADA_V + 1))
                for t in range(NT):
                    mm = pe.matmul(banks(MIX, 2)[:, t * P:(t + 1) * P], vf[:, par, t, :],
                                   wsT[:, bass.ds(q, 1), :].rearrange("p a i -> p (a i)"), start=True, stop=True)
                mm.then_inc(mix_mm, 1)
                pe.wait_ge(u_made, q + 1)
                part(q, par, 2)
                pe.wait_ge(m0_made, q + 1)
                for j in range(2):
                    mm = pe.matmul(PS[:, MIX + j, :], wpl[:, par, :],
                                   dT[:, bass.ds(half, 1), j * 512:(j + 1) * 512].rearrange("p a n -> p (a n)"),
                                   start=True, stop=True)
                mm.then_inc(yb_mm, 1)

            run_steps(pe, f_step, 0, HD, 2, HD)

            pe.wait_ge(consts, 4)
            pe.wait_ge(tb_made, HD)
            pe.wait_ge(yb1_made, HD)
            def y_half(q, par, half, looped):
                r = rows_of(q, looped)
                n = 0
                for k in range(KD):
                    if half == 0 and not looped and q == 0:
                        pe.wait_ge(w_lo_k, KD + k + 1)
                    for a, b in ((mt_hi, wo_hi), (mt_hi, wo_lo), (mt_lo, wo_hi)):
                        mm = pe.matmul(PS[0:r, 2 * par + half, :], a[par][:, k, 0:r],
                                       b[:, k, half * 512:(half + 1) * 512], start=(n == 0), stop=(n == 3 * KD - 1))
                        n += 1
                return mm

            def h2_turn(q, par, looped):
                r = rows_of(q, looped)
                pe.wait_ge(h2_made, q + 1)
                wait(pe, h2T_made, q)
                for k in range(KD):
                    mm = pe.transpose(banks(4, 2)[:, k * r:(k + 1) * r], h2[0:r, par, k * P:(k + 1) * P],
                                      ident[0:r, 0:r])
                mm.then_inc(h2_tr, 1)

            def places(q, looped):
                r = rows_of(q, looped)
                first = not looped and q == 0
                pe.wait_ge(m_made, q + 1)
                wait(pe, mrun_made, q)
                wait(pe, mp_made, q)
                mm = pe.matmul(PS[0:r, 7, 0:NE], upper[0:r, 0:r], mb[0:r, :], start=True, stop=first)
                if not first:
                    mm = pe.matmul(PS[0:r, 7, 0:NE], ones[:, 0:r], mrun[:, :], start=False, stop=True)
                mm.then_inc(pos_mm, 1)

            def logits(q, par, looped):
                r = rows_of(q, looped)
                pe.wait_ge(h2T_made, q + 1)
                wait(pe, lg_made, q)
                for k in range(KD):
                    mm = pe.matmul(PS[0:r, 6, 0:NL], h2T[:, par, k, 0:r], wr[:, k, :], start=(k == 0),
                                   stop=(k == KD - 1))
                mm.then_inc(lg_mm, 1)

            pe.wait_ge(later_in, LATER)

            def w_step(q, par, half, looped):
                if looped or q < NQ:
                    pe.wait_ge(ht_lo_made, q + (NQ + 1))
                    wait(pe, y_scaled, q - 1)
                    y_half(q, par, 0, looped)
                if looped or 2 <= q <= NQ + 1:
                    h2_turn(q - 2, par, looped or q > 2)
                if looped or q >= 3:
                    places(q - 3, looped or q > 3)
                if looped or q < NQ:
                    y_half(q, par, 1, looped).then_inc(y_mm, 1)
                if looped or 2 <= q <= NQ + 1:
                    logits(q - 2, par, looped or q > 2)

            run_steps(pe, w_step, 0, NQ + 3, 4, 8)
            pe.wait_ge(mrun_made, NQ)
            pe.wait_ge(mp_made, NQ)
            pe.matmul(PS[:, 7, 0:NE], ones[:, :], mrun[:, :], start=True, stop=True).then_inc(cnt_mm, 1)

            def turn_in(n, s, uses):
                par = s % HG
                pe.wait_ge(hg_in[par], uses * 16 + 16)
                wait(pe, hgT_a, n)
                wait(pe, hgT_b, n)
                for k in range(KD):
                    mm = pe.transpose(banks(0, 2)[:, k * P:(k + 1) * P], hg[par][:, k * P:(k + 1) * P], ident[:, :])
                mm.then_inc(hg_tr, 1)

            def gate_up(hgt, wgu_, bank):
                for j in range(2):
                    for k in range(KD):
                        mm = pe.matmul(PS[:, bank, j * P:(j + 1) * P], wgu_[:, j, k, :], hgt[:, k, :],
                                       start=(k == 0), stop=(k == KD - 1))
                return mm

            def down(n, s):
                par, slot = s % 2, s % RING
                pe.wait_ge(act_made, n + 1)
                wait(pe, ysb_made, n)
                for half in range(2):
                    mm = pe.matmul(PS[:, 5 + half, :], actT[:, par, :], wd[slot][:, half * 512:(half + 1) * 512],
                                   start=True, stop=True)
                mm.then_inc(down_mm, 1)

            def e_step(n, s, oct_, looped):
                par = s % 2
                if looped or n < NE:
                    pe.wait_ge(hgT_a, n + 1)
                    pe.wait_ge(hgT_b, n + 1)
                    pe.wait_ge(we_in[s], oct_ * 48 + 48)
                    wait(pe, act_made, n - 1)
                    gate_up(hgT[par], wgu[s], 2 + par).then_inc(gu_mm, 1)
                if looped or n + 1 < NE:
                    turn_in(n + 1, s + 1, oct_ * (RING // HG) + (s + 1) // HG)
                if looped or n >= 1:
                    down(n - 1, (s - 1) % RING)

            turn_in(0, 0, 0)
            run_steps(pe, e_step, 0, NE + 1, RING, NE - RING, RING)

            pe.wait_ge(cnt_made, 2)
            pe.wait_ge(ysb_made, NE)
            fullest = pe.value_load(most_u[0:1, 0:1], min_val=0, max_val=TOK)
            with pe.If(fullest > P):
                with pe.Fori(1, NQ) as c:
                    with pe.Fori(0, NE) as x:
                        m = (c - 1) * NE + x
                        pe.wait_ge(o_gather, m * 16 + 16)
                        for k in range(KD):
                            mm = pe.transpose(banks(0, 2)[:, k * P:(k + 1) * P], hg[0][:, k * P:(k + 1) * P],
                                              ident[:, :])
                        mm.then_inc(o_pe, 1)
                        pe.wait_ge(o_dve, m * 3 + 1)
                        pe.wait_ge(o_in, m * 64 + 64)
                        gate_up(hgT[0], wgu[0], 2).then_inc(o_pe, 1)
                        pe.wait_ge(o_dve, m * 3 + 2)
                        for half in range(2):
                            mm = pe.matmul(PS[:, 5 + half, :], actT[:, 0, :], wd[0][:, half * 512:(half + 1) * 512],
                                           start=True, stop=True)
                        mm.then_inc(o_pe, 1)


_INS = ["x_prompt", "x_sample", "c_prompt", "c_sample", "state_pool", "w_ada", "b_ada", "g_pre_mix",
        "g_post_mix", "g_pre_ffn", "g_post_ffn", "w_in", "ln_v_g", "ln_v_b", "w_spatial", "b_spatial",
        "w_pool", "pool_scale", "w_out", "w_router_grp", "b_router_grp", "w_router_exp",
        "b_router_exp", "w_exp_gate", "w_exp_up", "w_exp_down"]


def kernel(**inputs):
    import numpy as _np
    import concourse.bacc as _bacc
    from concourse import mybir as _mybir
    from concourse.bass_utils import run_bass_kernel_spmd as _run

    nc = _bacc.Bacc("TRN2", target_bir_lowering=False, num_devices=1)
    arrays, args = {}, []
    for name in _INS:
        a = _np.ascontiguousarray(inputs[name])
        arrays[f"in_{name}_dram"] = a
        args.append(nc.dram_tensor(f"in_{name}_dram", a.shape, _mybir.dt.from_np(a.dtype), kind="ExternalInput").ap())
    x_prompt, x_sample, state_pool = inputs["x_prompt"], inputs["x_sample"], inputs["state_pool"]
    depth, samples, rows, width = state_pool.shape
    outs = [x_prompt.shape, x_sample.shape, (depth, x_prompt.shape[0], rows, width), state_pool.shape,
            (depth, samples, 1, x_prompt.shape[2])]
    for i, shape in enumerate(outs):
        args.append(nc.dram_tensor(f"out_{i}_dram", shape, _mybir.dt.float32, kind="ExternalOutput").ap())
    trunk_step(nc, *args)
    r = _run(nc, [arrays], core_ids=[0])
    return tuple(r.results[0][f"out_{i}_dram"] for i in range(len(outs)))
```

```python
from contextlib import ExitStack

import concourse.bass as bass
from concourse import mybir

F32 = mybir.dt.float32
F32R = mybir.dt.float32r
BF16 = mybir.dt.bfloat16
U32 = mybir.dt.uint32
ALU = mybir.AluOpType
ACT = mybir.ActivationFunctionType
AX_X = mybir.AxisListType.X

P = 128
EPS = 1e-6
PAST_ALL = 1 << 20


def wait(eng, sem, value):
    if isinstance(value, int) and value <= 0:
        return
    eng.wait_ge(sem, value)


def wait_apart(eng, sem, value, passed):
    eng.wait_ge(sem, value)
    eng.sem_inc(passed, 1)


def wait_apart_if(eng, sem, value, passed):
    if isinstance(value, int) and value <= 0:
        return
    wait_apart(eng, sem, value, passed)


def run_steps(eng, step, first, last, loop_from, loop_to, many=2):
    assert (loop_to - loop_from) % many == 0
    for q in range(first, loop_from):
        step(q, q % many, q // many, False)
    with eng.Fori(0, (loop_to - loop_from) // many) as i:
        for s in range(many):
            q0 = loop_from + s
            step(i * many + q0, q0 % many, i + q0 // many, True)
    for q in range(loop_to, last):
        step(q, q % many, q // many, False)


class Place:

    def __init__(self, nc, at, end):
        self.nc, self.at, self.end = nc, at, end

    def __call__(self, name, shape, dt):
        size = mybir.dt.size(dt)
        for n in shape[1:]:
            size *= n
        t = self.nc.alloc_sbuf_tensor_at(name, shape, dt, offset=self.at)
        self.at += (size + 31) // 32 * 32
        assert self.at <= self.end, (name, self.at, self.end)
        return t


def trunk_step(nc, x_prompt, x_sample, c_prompt, c_sample, state_pool, w_ada, b_ada, g_pre_mix,
               g_post_mix, g_pre_ffn, g_post_ffn, w_in, ln_v_g, ln_v_b, w_spatial, b_spatial, w_pool,
               pool_scale, w_out, w_router_grp, b_router_grp, w_router_exp, b_router_exp,
               w_exp_gate, w_exp_up, w_exp_down, y_prompt, y_sample, pool_prompt, pool_sample,
               chunk_v):
    _, SEQ, D = x_prompt.shape
    NS = x_sample.shape[0]
    KD = D // P
    NT = SEQ // P
    TOK = SEQ + NS
    NC = NS + 1
    PRM = NS
    AW = D
    BW = state_pool.shape[3]
    PST = state_pool.shape[2]
    NG = BW // P
    HD = w_spatial.shape[1]
    NMOD = w_ada.shape[2] // P
    NQ = NT + 1
    assert HD == KD == NT == 8 and NG == 4

    xp = x_prompt.rearrange("b (t p) d -> (b t) p d", p=P)
    xs = x_sample.rearrange("b s d -> (b s) d")
    w_in_k = w_in[0].rearrange("(k p) n -> p k n", p=P)
    w_ada_k = w_ada[0].rearrange("(k p) n -> p k n", p=P)

    v_dram = nc.dram_tensor("v_normed", [NT, P, AW], F32).ap()
    NE = w_exp_gate.shape[1]
    FE = w_exp_gate.shape[3]
    NGR = w_router_grp.shape[2]
    EPG = NE // NGR
    NL = 8 + NE
    SLOTS = NQ * P
    mod_dram = nc.dram_tensor("modulation", [NC, 4 * D], F32).ap()
    h2_dram = nc.dram_tensor("h2", [TOK, D], F32).ap()
    list_dram = nc.dram_tensor("token_lists", [SLOTS * NE, 2], U32).ap()
    out_dram = nc.dram_tensor("expert_outs", [2 * TOK, D], F32).ap()
    merged_dram = nc.dram_tensor("merged", [KD, P, TOK], F32).ap()

    with ExitStack() as ctx:
        def sem(name):
            return ctx.enter_context(nc.semaphore(name))

        def sems(name, n):
            return [sem(f"{name}{i}") for i in range(n)]

        CH = 256
        CLO = 32
        HG, IX = 4, 8
        BASE = (nc.sbuf_base + 31) // 32 * 32
        END = nc.sbuf_usable_end // 32 * 32
        keep = Place(nc, BASE, BASE + 11264)

        ident = keep("ident", [P, P], F32)
        vecT = keep("vecT", [P, 4 * KD], F32)
        cT = keep("cT", [P, KD, NC], F32)
        c_split = keep("c_split", [P, KD, CLO + NC], F32R)
        c_high = keep("c_high", [P, KD, CLO + NC], F32R)
        modT = keep("modT", [P, 2 * KD, NC], F32)
        A1T = keep("A1T", [P, KD, NC], F32)
        ss = keep("ss", [P, 2], F32)
        ms = keep("ms", [P, 2], F32)
        rstd = keep("rstd", [P, 2], F32)
        bn6 = keep("bn6", [P, 2, 6], F32)
        mv = keep("mv", [P, 2], F32)
        ve = keep("ve", [P, 1], F32)
        vr = keep("vr", [P, 1], F32)
        mhalf = keep("mhalf", [P, 1], F32)
        inv_n = keep("inv_n", [P, 16], F32)
        invc = keep("invc", [P, 16], F32)
        psh = keep("psh", [P, KD], F32)
        w00 = keep("w00", [NS, HD], F32)
        mS = keep("mS", [P, KD, NS], F32)
        w00d = keep("w00d", [NS, HD, NS], F32)

        wr = keep("wr", [P, KD, NL], F32)
        biasr = keep("biasr", [P, NL], F32)
        iota8 = keep("iota8", [P, 8], F32)
        upper = keep("upper", [P, P], BF16)
        ones = keep("ones", [P, P], BF16)
        lg = keep("lg", [P, NL], F32)
        gtop = keep("gtop", [P, 8], F32)
        gix = keep("gix", [P, 8], U32)
        gid = keep("gid", [P, 1], F32)
        ohg = keep("ohg", [P, NGR], F32)
        t32 = keep("t32", [P, NE], F32)
        s8 = keep("s8", [P, 8], F32)
        etop = keep("etop", [P, 8], F32)
        eix = keep("eix", [P, 8], U32)
        ei = keep("ei", [P, 2], F32)
        oh12 = keep("oh12", [P, 2, 8], F32)
        m12 = keep("m12", [P, 2, NE], F32)
        mb = keep("mb", [P, NE], BF16)
        mrun = keep("mrun", [P, NE], BF16)
        ngm = keep("ngm", [P, 1], F32)
        exg = keep("exg", [P, NGR], F32)
        se = keep("se", [P, 1], F32)
        dm = keep("dm", [P, 1], F32)
        e12 = keep("e12", [P, 1], F32)
        pg = keep("pg", [P, 1], F32)
        e1 = keep("e1", [P, 1], F32)
        rw = keep("rw", [P, 1], F32)
        wts = keep("wts", [P, NQ, 2], F32)
        eid = keep("eid", [P, 2], F32)
        mp = keep("mp", [P, 2, NE], F32)
        pos = keep("pos", [P, 2], F32)
        lrow = [[keep(f"lrow{i}{j}", [P, 1], U32) for j in range(2)] for i in range(2)]
        tid = keep("tid", [P, 1], F32)
        tidu = keep("tidu", [P, 2, 2, 2], U32)
        lst = keep("lst", [P, NE, 2], U32)
        idx = [keep(f"idx{i}", [P, 2], U32) for i in range(IX)]
        most = keep("most", [P, 1], F32)
        most_u = keep("most_u", [P, 1], U32)
        ss2 = keep("ss2", [P, 4], F32)
        ms2 = keep("ms2", [P, 4], F32)
        rs2 = keep("rs2", [P, 4], F32)

        keep.end = keep.at
        big = Place(nc, keep.end, END)
        hT_hi = big("hT_hi", [P, KD, TOK], F32R)
        lo_at = big.at
        hT_lo = big("hT_lo", [P, KD, TOK], F32R)
        early = Place(nc, lo_at, big.at)
        adaV = early("adaV", [P, 4, KD, CH], F32)

        v = Place(nc, big.at, END)
        v.at += 2 * 4 * KD * P
        xbuf = v("xbuf", [P, 2, D], F32)
        xn = v("xn", [P, D], F32)
        h = v("h", [P, KD, P], F32)
        ht_hi1 = v("ht_hi1", [P, KD, P], F32R)
        wv_hi = v("wv_hi", [P, KD, AW], F32R)
        wv_raw = Place(nc, v.at, END)("wv_raw", [P, KD, AW], F32)
        wv_lo = v("wv_lo", [P, KD, AW], F32R)
        lng = v("lng", [P, AW], F32)
        lnb = v("lnb", [P, AW], F32)
        ht_hi = [v("ht_hi0", [P, KD, P], F32R), ht_hi1]
        ht_lo = [v(f"ht_lo{i}", [P, KD, P], F32R) for i in range(2)]
        vg = v("vg", [P, 2, AW], F32)
        none_u = v("none_u", [P, NQ * NE * 2], U32)
        early = Place(nc, keep.end, lo_at)
        c9 = early("c9", [NC, D], F32)
        sc9 = early("sc9", [NC, D], F32)
        vecs = early("vecs", [4 * KD, P], F32)
        rows0 = early("rows0", [NC, 2 * D], F32)

        f = Place(nc, big.at, END)
        wraw = f("wraw", [P, 3, KD, P], F32)
        w_hi = [f(f"w_hi{i}", [P, KD, P], F32R) for i in range(2)]
        w_lo = [f(f"w_lo{i}", [P, KD, P], F32R) for i in range(2)]
        ada_at = f.at
        ada_raw = [f(f"ada_raw{i}", [P, KD, CH], F32) for i in range(2)]
        ada_lo = [Place(nc, ada_at + i * 4 * KD * CH, f.at)(f"ada_lo{i}", [P, KD, CH], F32R) for i in range(2)]
        ada_hi = [f(f"ada_hi{i}", [P, KD, CH], F32R) for i in range(2)]
        dT = f("dT", [P, NG, TOK], F32)
        bsb = f("bsb", [P, HD, P], F32)
        wsT = f("wsT", [P, HD, P], F32)
        pooling = Place(nc, f.at, f.at + 2 * 4128)
        ws = pooling("ws", [P, HD, P], F32)
        spr = pooling("spr", [NS * PST, BW], F32)
        spT = pooling("spT", [P, NG, NS * PST], F32)
        u = f("u", [P, TOK], F32)
        ta = f("ta", [P, TOK], F32)
        pooling = Place(nc, f.at, f.at + 5 * 4128)
        pT = [pooling(f"pT{i}", [P, 16 + TOK], F32) for i in range(2)]
        pa = pooling("pa", [P, 16 + SEQ], F32)
        pb = pooling("pb", [P, 16 + SEQ], F32)
        tb = f("tb", [P, TOK], F32)
        m0 = f("m0", [P, TOK], F32)
        yb1 = f("yb1", [P, TOK], F32)
        tails_at = Place(nc, f.at + 4 * TOK, f.at + 8 * TOK)
        ptok = tails_at("ptok", [PST, BW], F32)
        pstok = tails_at("pstok", [NS, BW], F32)
        mg = f("mg", [P, 2, TOK], F32)
        vf = f("vf", [P, 2, NT, P], F32)
        vfs = f("vfs", [NS, 2, P], F32)
        wpl = f("wpl", [P, 2, P], F32)
        ybs = f("ybs", [P, NS], F32)
        psm = f("psm", [P, NG, NS], F32)
        pws = f("pws", [P, NG, NS], F32)
        ptail = f("ptail", [P, NG, PST], F32)
        bias = f("bias", [NC, 2, 2 * CH], F32)
        rowbuf = f("rowbuf", [NC, 2, 2 * CH], F32)
        clo_rows = f("clo_rows", [NC, 2 * CH], F32)
        fix = f("fix", [P, 16], F32)
        w = Place(nc, keep.end, big.at)
        wo_hi = w("wo_hi", [P, KD, D], F32R)
        mt_at = w.at
        mt = w("mt", [P, 2, KD, P], F32)
        mt_lo = [Place(nc, mt_at + i * 4 * KD * P, w.at)(f"mt_lo{i}", [P, KD, P], F32R) for i in range(2)]
        mt_hi = [w(f"mt_hi{i}", [P, KD, P], F32R) for i in range(2)]
        spare_at = w.at
        w = Place(nc, big.at, ada_at)
        rws = w("rws", [NC, 4, D], F32)
        G2b = w("G2b", [P, D], F32)
        xw_at = w.at
        xw = w("xw", [P, 2, D], F32)
        wo_raw = Place(nc, ada_at, END)("wo_raw", [P, KD, D], F32)
        w = Place(nc, ada_at, END)
        wo_lo = w("wo_lo", [P, KD, D], F32R)
        x2 = w("x2", [P, NQ, D], F32)
        moe_at = w.at
        G1b = w("G1b", [P, D], F32)
        A2b = w("A2b", [P, D], F32)
        B2b = w("B2b", [P, D], F32)
        h2 = w("h2buf", [P, 2, D], F32)
        gains = Place(nc, w.at, w.at + 8 * D)
        g_post1 = gains("g_post1", [P, D], F32)
        g_pre2 = gains("g_pre2", [P, D], F32)
        h2T = w("h2T", [P, 2, KD, P], F32)
        wd0, wd2 = [w(f"wd{i}", [P, D], F32) for i in (0, 2)]

        RING = 8
        spare = Place(nc, spare_at, big.at)
        first, second = Place(nc, keep.end, keep.end + 4 * KD * D), Place(nc, ada_at, ada_at + 4 * KD * D)
        wgu, wd = [], []
        for i in range(RING):
            at = spare if i in (0, 2) else Place(nc, big.at, big.at + 12 * D) if i == 1 else first if i < 6 else second
            wgu.append(at(f"wgu{i}", [P, 2, KD, FE], F32))
            wd.append(wd0 if i == 0 else wd2 if i == 2 else (second if i == 5 else at)(f"wd{i}", [P, D], F32))
        e = Place(nc, xw_at, xw_at + 8 * D)
        hg = [e(f"hg{i}", [P, D], F32) for i in range(2)]
        e = Place(nc, moe_at, END)
        hg += [e(f"hg{i}", [P, D], F32) for i in range(2, HG)]
        hgT = [e(f"hgT{i}", [P, KD, P], F32) for i in range(2)]
        ysb = e("ysb", [P, 2, D], F32)
        sil = e("sil", [P, 2, P], F32)
        actT = e("actT", [P, 2, P], F32)
        g_post2 = Place(nc, spare_at - 8 * D, spare_at)("g_post2", [P, D], F32)
        e = Place(nc, keep.end, big.at)
        yg = e("yg", [P, 4, 2, D], F32)
        f1 = e("f1", [P, 2, D], F32)
        ff = e("ff", [P, 2, D], F32)
        fj = e("fj", [P, 2, D], F32)
        fo = e("fo", [P, 2, D], F32)

        PS = ctx.enter_context(nc.psum_tensor("PS", [P, 8, 512], F32))

        def banks(a, n):
            return PS[:, a:a + n, :].rearrange("p b n -> p (b n)")

        rows_in = sem("rows_in")
        more_rows_in = sem("more_rows_in")
        rows_made = sem("rows_made")
        mod_tr = sem("mod_tr")
        c_hi_made = sem("c_hi_made")
        c_lo_made = sem("c_lo_made")
        ada_hi_made = sem("ada_hi_made")
        ada_lo_made = sem("ada_lo_made")
        clo_read = sem("clo_read")
        mod_part = sem("mod_part")
        mod_out = sems("mod_out", 2)
        prep_made = sem("prep_made")
        consts = sem("consts")
        mt_in = sems("mt_in", 2)
        y_mm = sem("y_mm")
        y_scaled = sem("y_scaled")
        x2_made = sem("x2_made")
        h2_scaled = sem("h2_scaled")
        h2_made = sem("h2_made")
        h2_out = sems("h2_out", 2)
        h2_tr = sem("h2_tr")
        h2T_made = sem("h2T_made")
        lg_mm = sem("lg_mm")
        lg_made = sem("lg_made")
        mp_made = sem("mp_made")
        eid_made = sem("eid_made")
        wts_made = sem("wts_made")
        route = sem("route")
        mS_made = sem("mS_made")
        exp_made = sem("exp_made")
        m_made = sem("m_made")
        pos_mm = sem("pos_mm")
        mrun_made = sem("mrun_made")
        slot_step = sem("slot_step")
        slot_made = sem("slot_made")
        scat = sems("scat", 2)
        cnt_mm = sem("cnt_mm")
        cnt_made = sem("cnt_made")
        lst_in = sem("lst_in")
        hg_zero = sem("hg_zero")
        idx_made = sem("idx_made")
        hg_in = sems("hg_in", HG)
        we_in = sems("we_in", RING)
        hg_tr = sem("hg_tr")
        hgT_a = sem("hgT_a")
        hgT_b = sem("hgT_b")
        gu_mm = sem("gu_mm")
        silu_made = sem("silu_made")
        act_made = sem("act_made")
        down_mm = sem("down_mm")
        ysb_made = sem("ysb_made")
        eo_out = sems("eo_out", 2)
        o_in = sem("o_in")
        o_gather = sem("o_gather")
        o_pe = sem("o_pe")
        o_act = sem("o_act")
        o_dve = sem("o_dve")
        o_out = sem("o_out")
        f1_made = sem("f1_made")
        f_made = sem("f_made")
        f_scaled = sem("f_scaled")
        fo_made = sem("fo_made")
        y_out = sems("y_out", 2)
        vec_in = sem("vec_in")
        passed = sem("passed")
        pool_passed = sem("pool_passed")
        vfs_in = sems("vfs_in", 2)
        small_in = sem("small_in")
        later_in = sem("later_in")
        c_silu = sem("c_silu")
        pre_tr = sem("pre_tr")
        pre_cp = sem("pre_cp")
        ada_in = sems("ada_in", 4)
        ada_mm = sem("ada_mm")
        mod_made = sem("mod_made")
        x_in = sems("x_in", 2)
        sum_made = sem("sum_made")
        sum_mean = sem("sum_mean")
        sum_root = sem("sum_root")
        x_normed = sem("x_normed")
        xT_made = sem("xT_made")
        h_scaled = sem("h_scaled")
        h_made = sem("h_made")
        ht_hi_made = sem("ht_hi_made")
        ht_lo_made = sem("ht_lo_made")
        hT_kept = sem("hT_kept")
        w_in_rows = sems("w_in_rows", 2)
        w_hi_k = sem("w_hi_k")
        w_lo_k = sem("w_lo_k")
        v_mm = sem("v_mm")
        v_gelu = sem("v_gelu")
        v_bn = sem("v_bn")
        sum2_made = sem("sum2_made")
        sum2_mean = sem("sum2_mean")
        sum2_root = sem("sum2_root")
        v_step = sem("v_step")
        v_made = sem("v_made")
        v_out = sems("v_out", 2)
        fc_in = sem("fc_in")
        ws_masked = sem("ws_masked")
        ws_tr = sem("ws_tr")
        ws_cp = sem("ws_cp")
        w_inn = sems("w_inn", 3)
        w_hi_made = sem("w_hi_made")
        w_lo_made = sem("w_lo_made")
        blk_mm = sem("blk_mm")
        p_cp = sem("p_cp")
        p_step = sem("p_step")
        p_done = sem("p_done")
        dS_made = sem("dS_made")
        tail_tr = sem("tail_tr")
        spare_read = sem("spare_read")
        tail_cp = sem("tail_cp")
        u_made = sem("u_made")
        ta_made = sem("ta_made")
        tb_made = sem("tb_made")
        mix_mm = sem("mix_mm")
        yb_mm = sem("yb_mm")
        m0_made = sem("m0_made")
        m1_made = sem("m1_made")
        m2_made = sem("m2_made")
        yb1_made = sem("yb1_made")
        mg_made = sem("mg_made")
        mg_out = sems("mg_out", 2)
        vf_in = sems("vf_in", 2)
        wpl_in = sems("wpl_in", 2)
        st_out = sem("st_out")

        WCOL = {"p": 2 * AW, "u": 0, "ga": 2 * AW + BW, "gb": 2 * AW + BW + D}
        CPM = CH // P
        NADA_V = 2 * D // CH
        NADA_F = NMOD // CPM - NADA_V
        VEC = {"pre_mix": 2 * KD, "pool_scale": 3 * KD}
        NV = 4 * KD
        R_G1, R_B2, R_A2, R_G2 = range(4)
        X_IN = (16 * ((NQ + 1) // 2), 16 * (NQ // 2))
        SCAT_IN = (0, 16)
        Y_IN = ((x_in[0], 2 * X_IN[0]), (x_in[1], 2 * X_IN[1]), (mt_in[0], X_IN[1]), (mt_in[1], X_IN[1]))
        THIRD = TOK // 3
        assert 3 * THIRD == TOK and THIRD >= 256
        REGION = (5, 2)
        MIX = 0
        SMIX_AT, SYB_AT = THIRD, THIRD + NS
        LISTS = list_dram.rearrange("(s e) o -> s (e o)", e=NE)
        RC, SC = 12, 2
        LATER = 16 * 8
        ADA_IN = 16 * NADA_V // 4
        ROWS_OUT = 16 * (NE // 2)

        def rows_of(q, looped):
            return NS if not looped and q == 0 else P

        def thirds(r):
            return PS[:, REGION[r]:REGION[r] + 3, 0:THIRD]

        def in_thirds(ap):
            return ap.rearrange("p (b n) -> p b n", n=THIRD)

        def v_over(eng):
            eng.wait_ge(v_mm, NQ)
            eng.wait_ge(hT_kept, 2 * NQ)
            eng.wait_ge(v_out[0], 16 * 5)
            eng.wait_ge(v_out[1], 16 * 4)

        def f_over(eng):
            eng.wait_ge(blk_mm, NG + 3 * HD)
            eng.wait_ge(yb_mm, HD)
            eng.wait_ge(mod_out[0], 16 * (HD // 2))
            eng.wait_ge(mod_out[1], 16 * (HD // 2))
            eng.wait_ge(mg_out[0], 16 * (HD // 2))
            eng.wait_ge(mg_out[1], 16 * (HD // 2))
            eng.wait_ge(st_out, 32)

        block = ctx.enter_context(nc.Block())

        @block.sync
        def _(sp):
            def ada_chunk(n, slot, ring):
                wait(sp, ada_mm, n - 3)
                sp.dma_start(ring[:, slot], w_ada_k[:, :, bass.ds(n * CH, CH)]).then_inc(ada_in[slot], 16)

            def x_tile(q, par, half, looped):
                wait(sp, x_normed, q - 1)
                if not looped and q == 0:
                    sp.dma_start(xbuf[0:NS, par, :], xs).then_inc(x_in[par], 16)
                else:
                    sp.dma_start(xbuf[:, par, :], xp[bass.ds(q - 1, 1)].rearrange("a p d -> p (a d)")
                                 ).then_inc(x_in[par], 16)

            def v_store(q, par, looped):
                wait(sp, v_made, q + 1)
                if not looped and q == 0:
                    sp.dma_start(chunk_v[0, :, 0, :], vg[0:NS, par, :]).then_inc(v_out[par], 16)
                else:
                    sp.dma_start(v_dram[bass.ds(q - 1, 1)].rearrange("a p d -> p (a d)"),
                                 vg[:, par, :]).then_inc(v_out[par], 16)

            sp.dma_start(c9[0:NS, :], c_sample).then_inc(small_in, 16)
            sp.dma_start(c9[NS:NC, :], c_prompt).then_inc(small_in, 16)
            for n in range(4):
                ada_chunk(n, n % 4, adaV)
            x_tile(0, 0, 0, False)
            x_tile(1, 1, 0, False)

            def wv_half(a):
                k = a * KD // 2
                sp.dma_start(wv_raw[:, k:k + KD // 2, :], w_in_k[:, k:k + KD // 2, AW:2 * AW]
                             ).then_inc(w_in_rows[a], 16)

            wv_half(0)
            for n in range(4, NADA_V):
                ada_chunk(n, n % 4, adaV)
            wv_half(1)

            def step(q, par, half, looped):
                if looped or q < NQ:
                    x_tile(q, par, half, looped)
                if looped or q >= 3:
                    v_store(q - 3, 1 - par, looped)

            def load_block(n, slot, col):
                wait(sp, w_lo_made, n - 2)
                sp.dma_start(wraw[:, slot], w_in_k[:, :, col]).then_inc(w_inn[slot], 16)

            run_steps(sp, step, 2, NQ + 1, 4, 8)
            sp.wait_ge(sum_root, NQ)
            sp.wait_ge(x_normed, NQ)
            for g in range(3):
                load_block(g, g, bass.ds(WCOL["p"] + g * P, P))
            for q in range(NQ + 1, NQ + 3):
                step(q, q % 2, q // 2, False)

            v_over(sp)
            sp.dma_start(spr[:, :], state_pool[0].rearrange("b r c -> (b r) c")).then_inc(fc_in, 16)
            sp.dma_start(ws[:, :, :], w_spatial[0].rearrange("h i j -> i h j")).then_inc(fc_in, 16)
            sp.dma_start(bsb[:, :, :], b_spatial.to_broadcast([P, HD, P])).then_inc(fc_in, 16)
            load_block(3, 0, bass.ds(WCOL["p"] + 3 * P, P))

            def ada_load(q):
                for a in range(2):
                    sp.wait_ge(ada_mm, q * 2 + (NADA_V - 1 + a))
                    sp.dma_start(ada_raw[a][:, :, :], w_ada_k[:, :, bass.ds((q * 2 + (NADA_V + a)) * CH, CH)]
                                 ).then_inc(ada_in[a], 16)

            ada_load(0)

            def f_part(q, j, part):
                load_block(q * 3 + (NG + j), (NG + j) % 3, bass.ds(q * P + WCOL[part], P))

            def f_step(q, par, half, looped):
                f_part(q, 0, "u")
                wait(sp, blk_mm, q * 3 + (NG - 4) if looped or q >= 2 else 0)
                sp.dma_start(vfs[:, par], chunk_v[0, :, 0, bass.ds(q * P, P)]).then_inc(vfs_in[par], 16)
                wait(sp, yb_mm, q - 1)
                sp.dma_start(wpl[:, par], w_pool[0, bass.ds(half, 1), :, par * P:(par + 1) * P]
                             .rearrange("g c o -> c (g o)")).then_inc(wpl_in[par], 16)
                wait(sp, mod_made, q + (NADA_V - 1) if looped or q >= 2 else 0)
                sp.dma_start(bias[:, par], b_ada[:, bass.ds(q * 2 * CH + 2 * D, 2 * CH)].to_broadcast([NC, 2 * CH])
                             ).then_inc(wpl_in[par], 16)
                if looped or q > 0:
                    ada_load(q)
                f_part(q, 1, "ga")
                wait(sp, mix_mm, q - 1)
                sp.dma_start(vf[:, par], v_dram[:, :, bass.ds(q * P, P)].rearrange("t p c -> p t c")
                             ).then_inc(vf_in[par], 16)
                f_part(q, 2, "gb")

            f_step(0, 0, 0, False)
            sp.wait_ge(tail_cp, 1)
            sp.dma_start(pool_prompt[0, 0], ptok[:, :]).then_inc(st_out, 16)
            sp.dma_start(pool_sample[0, :, PST - 1, :], pstok[:, :]).then_inc(st_out, 16)
            run_steps(sp, f_step, 1, HD, 2, HD)

            sp.wait_ge(ada_mm, NADA_V + NADA_F)
            for a in range(2):
                k = a * KD // 2
                sp.dma_start(wo_raw[:, k:k + KD // 2, :], w_out[0].rearrange("(k p) n -> p k n", p=P)[
                    :, k:k + KD // 2, :]).then_inc(w_in_rows[a], 16)
            f_over(sp)

            def load_x(q, par, looped):
                wait(sp, x2_made, q - 1)
                if not looped and q == 0:
                    sp.dma_start(xw[0:NS, par, :], xs).then_inc(x_in[par], 16)
                else:
                    sp.dma_start(xw[:, par, :], xp[bass.ds(q - 1, 1)].rearrange("a p d -> p (a d)")
                                 ).then_inc(x_in[par], 16)

            def load_m(q, par, looped):
                wait(sp, y_mm, q - 1)
                sp.dma_start(mt[:, par], merged_dram[:, :, bass.ds((q - 1) * P, P)]
                             .rearrange("k p t -> p k t")).then_inc(mt_in[par], 16)

            def store_h2(q, par, looped):
                r = rows_of(q, looped)
                sp.wait_ge(h2_made, q + 1)
                dst = h2_dram[SEQ:TOK, :] if r == NS else (
                    h2_dram[0:SEQ, :].rearrange("(t p) d -> t p d", p=P)[bass.ds(q - 1, 1)]
                    .rearrange("t p d -> p (t d)"))
                sp.dma_start(dst, h2[0:r, par, :]).then_inc(h2_out[par], 16)

            def w_step(q, par, half, looped):
                if looped or q + 1 < NQ:
                    load_m(q + 1, 1 - par, looped)
                if not looped and q in (2, 3):
                    load_expert(6 - 2 * q)
                if not looped and q == NQ - 1:
                    load_expert(1)
                if looped or q >= 1:
                    store_h2(q - 1, 1 - par, looped or q > 1)
                if looped or q + 1 < NQ:
                    load_x(q + 1, 1 - par, looped)

            def load_gate_up(n, s):
                wait(sp, gu_mm, n - (RING - 1))
                one = bass.ds(n, 1)
                sp.dma_start(wgu[s][:, 0], w_exp_gate[0, one].rearrange("a (p k) f -> p (a k) f", k=KD)
                             ).then_inc(we_in[s], 16)
                sp.dma_start(wgu[s][:, 1], w_exp_up[0, one].rearrange("a (p k) f -> p (a k) f", k=KD)
                             ).then_inc(we_in[s], 16)

            def load_down(n, s):
                wait(sp, down_mm, n - (RING - 1))
                sp.dma_start(wd[s][:, :], w_exp_down[0, bass.ds(n, 1)].rearrange("a f d -> f (a d)")
                             ).then_inc(we_in[s], 16)

            def load_expert(n):
                load_gate_up(n, n)
                load_down(n, n)

            load_x(0, 0, False)
            run_steps(sp, w_step, 0, NQ + 1, 4, 8)

            sp.wait_ge(y_mm, NQ)
            sp.wait_ge(ht_lo_made, 2 * NQ)

            for n in range(3, 6):
                load_expert(n)
            sp.wait_ge(lst_in, 16)
            load_gate_up(6, 6)
            sp.wait_ge(hg_in[0], 16)
            load_down(6, 6)
            load_gate_up(RING - 1, RING - 1)
            load_gate_up(RING, 0)
            load_down(RING - 1, RING - 1)

            def load_step(n, s, uses, looped):
                if looped or n + 1 < NE:
                    load_gate_up(n + 1, (s + 1) % RING)
                load_down(n, s)

            run_steps(sp, load_step, RING, NE, RING, NE - RING, RING)

            sp.wait_ge(down_mm, NE)
            sp.wait_ge(cnt_made, 2)
            for par in range(2):
                sp.wait_ge(eo_out[par], ROWS_OUT)
            fullest = sp.value_load(most_u[0:1, 0:1], min_val=0, max_val=TOK)
            with sp.If(fullest > P):
                with sp.Fori(1, NQ) as c:
                    with sp.Fori(0, NE) as x:
                        one = bass.ds(x, 1)
                        sp.dma_start(idx[0][:, :], LISTS[bass.ds(c * P, P), bass.ds(x * 2, 2)]).then_inc(o_in, 16)
                        sp.dma_start(wgu[0][:, 0], w_exp_gate[0, one].rearrange("a (p k) f -> p (a k) f", k=KD)
                                     ).then_inc(o_in, 16)
                        sp.dma_start(wgu[0][:, 1], w_exp_up[0, one].rearrange("a (p k) f -> p (a k) f", k=KD)
                                     ).then_inc(o_in, 16)
                        sp.dma_start(wd[0][:, :], w_exp_down[0, one].rearrange("a f d -> f (a d)")
                                     ).then_inc(o_in, 16)
                        wait_apart(sp, o_out, ((c - 1) * NE + x) * 16 + 16, passed)

            def load_y(q, slot, uses, looped):
                wait(sp, f_made, q - 3)
                r = rows_of(q, looped)
                if r == NS:
                    src = out_dram[2 * SEQ:2 * TOK, :].rearrange("(p k) d -> p (k d)", k=2)
                else:
                    src = out_dram[0:2 * SEQ, :].rearrange("(t p k) d -> t p (k d)", p=P, k=2)[
                        bass.ds(q - 1, 1)].rearrange("t p d -> p (t d)")
                sp.dma_start(yg[0:r, slot].rearrange("p k d -> p (k d)"), src).then_inc(Y_IN[slot][0], 16)

            for q in range(4):
                load_y(q, q, 0, False)

            def store_y(q, s, quad, looped):
                sp.wait_ge(fo_made, q + 1)
                if not looped and q == 0:
                    sp.dma_start(y_sample.rearrange("b s d -> (b s) d"), fo[0:NS, 0, :]).then_inc(y_out[0], 16)
                else:
                    sp.dma_start(y_prompt[0, bass.ds((q - 1) * P, P), :], fo[:, s % 2, :]).then_inc(y_out[s % 2], 16)
                if looped or q + 4 < NQ:
                    load_y(q + 4, s, quad + 1, looped or True)

            run_steps(sp, store_y, 0, NQ, 1, NQ - 4, 4)
            sp.wait_ge(y_out[0], 16 * 5)
            sp.wait_ge(y_out[1], 16 * 4)
            sp.wait_ge(st_out, 32)
            sp.wait_ge(scat[1], 32 * 4 + SCAT_IN[1])
            sp.wait_ge(v_out[0], 16 * 5)

        @block.gpsimd
        def _(pool):
            pool.memset(ident[:, :], 0.0).then_inc(consts, 1)
            pool.wait_ge(consts, 1)
            pool.affine_select(out=ident[:, :], in_=ident[:, :], compare_op=ALU.not_equal, fill=1.0,
                               base=0, pattern=[[-1, P]], channel_multiplier=1).then_inc(consts, 1)
            pool.memset(mhalf[:, :], -0.5)
            pool.iota(inv_n[:, :], pattern=[[1, 16]], base=1, channel_multiplier=0,
                      allow_small_or_imprecise_dtypes=True)
            pool.iota(iota8[:, :], pattern=[[1, 8]], base=0, channel_multiplier=0,
                      allow_small_or_imprecise_dtypes=True)
            pool.iota(tid[:, :], pattern=[[0, 1]], base=SEQ, channel_multiplier=1,
                      allow_small_or_imprecise_dtypes=True)
            pool.memset(c_split[:, :, :].bitcast(F32), 0.0)
            pool.memset(c_high[:, :, :].bitcast(F32), 0.0)
            pool.memset(upper[:, :], 1.0)
            pool.memset(ones[:, :], 1.0)
            pool.memset(mrun[:, :], 0.0)
            pool.memset(wr[:, :, :], 0.0)
            pool.memset(none_u[:, :], PAST_ALL)
            pool.memset(biasr[:, :], -3e38).then_inc(consts, 1)
            pool.wait_ge(consts, 3)
            pool.affine_select(out=upper[:, :], in_=upper[:, :], compare_op=ALU.is_gt, fill=0.0,
                               base=0, pattern=[[1, P]], channel_multiplier=-1).then_inc(consts, 1)

            def root(n, src, tmp, scale, made, tmp_made, out, out_made):
                wait_apart(pool, made, n + 1, pool_passed)
                pool.tensor_scalar(tmp, src, scale, EPS, ALU.mult, ALU.add).then_inc(tmp_made, 1)
                pool.wait_ge(tmp_made, n + 1)
                pool.tensor_tensor(out, tmp, mhalf[0:tmp.shape[0], :], ALU.pow).then_inc(out_made, 1)

            def x_root(q, par, looped):
                rows = NS if not looped and q == 0 else P
                root(q, ss[0:rows, par:par + 1], ms[0:rows, par:par + 1], 1.0 / D, sum_made, sum_mean,
                     rstd[0:rows, par:par + 1], sum_root)

            def v_root(q, looped):
                rows = NS if not looped and q == 0 else P
                root(q, mv[0:rows, 1:2], ve[0:rows, :], 1.0, sum2_made, sum2_mean, vr[0:rows, :], sum2_root)

            def keep_h(q, par, looped):
                wait(pool, ht_lo_made, q + 1)
                if not looped and q == 0:
                    for src, dst in ((ht_hi, hT_hi), (ht_lo, hT_lo)):
                        pool.tensor_copy(dst[:, :, SEQ:TOK], src[par][:, :, 0:NS].bitcast(F32)).then_inc(hT_kept, 1)
                else:
                    at = bass.ds((q - 1) * P, P)
                    for src, dst in ((ht_hi, hT_hi), (ht_lo, hT_lo)):
                        pool.tensor_copy(dst[:, :, at], src[par][:, :, :].bitcast(F32)).then_inc(hT_kept, 1)

            def step(q, par, half, looped):
                if looped or q + 1 < NQ:
                    x_root(q + 1, 1 - par, looped)
                if looped or 2 <= q:
                    if looped or q - 2 < NQ:
                        v_root(q - 2, looped)
                if looped or q < NQ:
                    keep_h(q, par, looped)

            x_root(0, 0, False)
            run_steps(pool, step, 0, NQ + 2, 4, 8)

            pool.wait_ge(fc_in, 48)
            pool.affine_select(out=ws[:, :, :], in_=ws[:, :, :], compare_op=ALU.is_ge, fill=0.0, base=0,
                               pattern=[[0, HD], [-1, P]], channel_multiplier=1).then_inc(ws_masked, 1)
            pool.dma_start(pool_sample[0, :, 0:PST - 1, :], state_pool[0, :, 1:PST, :]
                           ).then_inc(scat[1], 16)

            def f_step(q, par, half, looped):
                wait_apart(pool, mod_made, q + (NADA_V + 1), pool_passed)
                pool.dma_start(mod_dram[:, bass.ds(q * 2 * CH, 2 * CH)], rowbuf[:, par, :]).then_inc(mod_out[par], 16)
                wait_apart(pool, mg_made, q + 1, pool_passed)
                pool.dma_start(merged_dram[bass.ds(q, 1)].rearrange("a p t -> p (a t)"),
                               mg[:, par, :]).then_inc(mg_out[par], 16)

            run_steps(pool, f_step, 0, HD, 0, HD - 2)

            def y_root(q, par, looped):
                r = rows_of(q, looped)
                root(q + NQ, ss2[0:r, par:par + 1], ms2[0:r, par:par + 1], 1.0 / D, sum_made, sum_mean,
                     rs2[0:r, par:par + 1], sum_root)

            def x2_root(q, par, looped):
                r = rows_of(q, looped)
                c = slice(2 + par, 3 + par)
                root(q + NQ, ss2[0:r, c], ms2[0:r, c], 1.0 / D, sum2_made, sum2_mean, rs2[0:r, c], sum2_root)

            def scatter(q, par, looped):
                r = rows_of(q, looped)
                wait_apart(pool, slot_made, q + 1, pool_passed)
                for k in range(2):
                    pool.indirect_dma_start(list_dram, bass.IndirectOffsetOnAxis(lrow[par][k][0:r, :], 0),
                                            tidu[0:r, par, k, :], None).then_inc(scat[par], 16)

            def w_step(q, par, half, looped):
                if looped or 1 <= q <= NQ:
                    y_root(q - 1, 1 - par, looped or q > 1)
                    x2_root(q - 1, 1 - par, looped or q > 1)
                if looped or q >= 3:
                    scatter(q - 3, 1 - par, looped or q > 3)

            pool.wait_ge(later_in, LATER)
            run_steps(pool, w_step, 0, NQ + 1, 4, 8)
            pool.wait_ge(x2_made, NQ)
            pool.wait_ge(h2_scaled, NQ)
            for t in hg:
                pool.memset(t[:, :], 0.0).then_inc(hg_zero, 1)
            for q in range(NQ + 1, NQ + 3):
                w_step(q, q % 2, q // 2, False)
            pool.wait_ge(hg_zero, HG)

            pool.wait_ge(h2_out[0], 16 * 5)
            pool.wait_ge(h2_out[1], 16 * 4)
            pool.wait_ge(scat[0], 32 * 5)
            pool.wait_ge(scat[1], 32 * 4 + SCAT_IN[1])
            pool.dma_start(lst[:, :, :].rearrange("p n o -> p (n o)"), LISTS[0:P, :]).then_inc(lst_in, 16)
            pool.wait_ge(lst_in, 16)

            def gather(n, s, oct_):
                wait_apart_if(pool, eo_out[s % 2], oct_ * (16 * RING // 2) + 16 * (s // 2 - (IX // 2 - 1)), pool_passed)
                pool.tensor_copy(idx[s % IX][:, :], lst[:, bass.ds(n, 1), :].rearrange("p a b -> p (a b)")
                                 ).then_inc(idx_made, 1)
                wait_apart_if(pool, hg_tr, n - (HG - 1), pool_passed)
                wait_apart(pool, idx_made, n + 1, pool_passed)
                pool.indirect_dma_start(hg[s % HG][:, :], None, h2_dram,
                                        bass.IndirectOffsetOnAxis(idx[s % IX][:, 0:1], 0),
                                        bounds_check=TOK - 1, oob_is_err=False).then_inc(hg_in[s % HG], 16)

            def answer(n, s):
                wait_apart(pool, ysb_made, n + 1, pool_passed)
                pool.indirect_dma_start(out_dram, bass.IndirectOffsetOnAxis(idx[s % IX][:, 1:2], 0),
                                        ysb[:, s % 2, :], None,
                                        bounds_check=2 * TOK - 1, oob_is_err=False).then_inc(eo_out[s % 2], 16)

            LAG = 4

            def e_step(n, s, oct_, looped):
                if looped or n < NE:
                    gather(n, s, oct_)
                if looped or n >= LAG:
                    answer(n - LAG, s + RING - LAG)

            run_steps(pool, e_step, 0, NE + LAG, RING, NE, RING)

            pool.wait_ge(cnt_made, 2)
            for j in range(HG):
                pool.wait_ge(hg_in[j], 16 * (NE // HG))
            for par in range(2):
                pool.wait_ge(eo_out[par], ROWS_OUT)
            fullest = pool.value_load(most_u[0:1, 0:1], min_val=0, max_val=TOK)
            with pool.If(fullest > P):
                with pool.Fori(1, NQ) as c:
                    with pool.Fori(0, NE) as x:
                        m = (c - 1) * NE + x
                        wait_apart(pool, o_in, m * 64 + 64, pool_passed)
                        pool.indirect_dma_start(hg[0][:, :], None, h2_dram,
                                                bass.IndirectOffsetOnAxis(idx[0][:, 0:1], 0),
                                                bounds_check=TOK - 1, oob_is_err=False).then_inc(o_gather, 16)
                        wait_apart(pool, o_dve, m * 3 + 3, pool_passed)
                        pool.indirect_dma_start(out_dram, bass.IndirectOffsetOnAxis(idx[0][:, 1:2], 0),
                                                ysb[:, 0, :], None,
                                                bounds_check=2 * TOK - 1, oob_is_err=False).then_inc(o_out, 16)
                        wait_apart(pool, o_out, m * 16 + 16, pool_passed)

            def f_root(q, par, looped):
                r = rows_of(q, looped)
                root(q + 2 * NQ, ss[0:r, par:par + 1], ms[0:r, par:par + 1], 1.0 / D, sum_made, sum_mean,
                     rstd[0:r, par:par + 1], sum_root)

            run_steps(pool, lambda q, par, half, looped: f_root(q, par, looped), 0, NQ, 1, NQ)

        @block.scalar
        def _(act):
            act.dma_start(vecs[0:2 * KD, :], b_ada[:, 0:2 * D].rearrange("o (m p) -> (o m) p", p=P)).then_inc(vec_in, 16)
            for n, g in (("pre_mix", g_pre_mix), ("pool_scale", pool_scale)):
                act.dma_start(vecs[VEC[n]:VEC[n] + KD, :], g.rearrange("o (k p) -> (o k) p", p=P)
                              ).then_inc(vec_in, 16)
            act.wait_ge(small_in, 32)
            act.activation(sc9[:, :], c9[:, :], ACT.Silu).then_inc(c_silu, 1)

            def x_norm(q, par, half, looped):
                rows = NS if not looped and q == 0 else P
                wait(act, x_in[par], half * 16 + 16)
                wait(act, xT_made, q)
                act.activation(xn[0:rows, :], xbuf[0:rows, par, :], ACT.Square,
                               accum_out=ss[0:rows, par:par + 1]).then_inc(sum_made, 1)
                wait(act, sum_root, q + 1)
                act.activation(xn[0:rows, :], xbuf[0:rows, par, :], ACT.Copy,
                               scale=rstd[0:rows, par:par + 1]).then_inc(x_normed, 1)

            def h_high(q, par, looped):
                cols = NS if not looped and q == 0 else P
                wait(act, h_made, q + 1)
                wait(act, v_mm, q - 1)
                wait(act, hT_kept, q * 2 - 2)
                act.activation(ht_hi[par][:, :, 0:cols], h[:, :, 0:cols], ACT.Copy).then_inc(ht_hi_made, 1)

            def v_gelu_of(q, par, half, looped):
                rows = NS if not looped and q == 0 else P
                wait(act, v_mm, q + 1)
                wait(act, v_out[par], half * 16)
                act.activation(vg[0:rows, par, :], banks(2 + 2 * par, 2)[0:rows, :], ACT.Gelu_apprx_tanh
                               ).then_inc(v_gelu, 1)

            def wv_high(first):
                for k in range(first, first + KD // 2):
                    act.wait_ge(w_in_rows[k // (KD // 2)], 16)
                    act.activation(wv_hi[:, k, :], wv_raw[:, k, :], ACT.Copy).then_inc(w_hi_k, 1)

            x_norm(0, 0, 0, False)
            wv_high(0)
            act.wait_ge(consts, 3)
            act.dma_start(wr[:, :, 0:NGR], w_router_grp[0].rearrange("(p k) g -> p k g", k=KD)).then_inc(later_in, 16)
            act.dma_start(wr[:, :, 8:NL], w_router_exp[0].rearrange("(p k) g -> p k g", k=KD)).then_inc(later_in, 16)
            act.dma_start(biasr[:, 0:NGR], b_router_grp.to_broadcast([P, NGR])).then_inc(later_in, 16)
            act.dma_start(biasr[:, 8:NL], b_router_exp.to_broadcast([P, NE])).then_inc(later_in, 16)
            act.dma_start(list_dram.rearrange("(p n) o -> p (n o)", p=P), none_u[:, :]).then_inc(later_in, 16)
            act.dma_start(lng[:, :], ln_v_g.to_broadcast([P, AW])).then_inc(later_in, 16)
            act.dma_start(lnb[:, :], ln_v_b.to_broadcast([P, AW])).then_inc(later_in, 16)
            with nc.allow_non_contiguous_dma(reason="eight numbers, for eight partitions"):
                act.dma_start(w00[:, :], w_spatial[:, :, 0, 0].to_broadcast([NS, HD])).then_inc(later_in, 16)
            act.wait_ge(pre_cp, 1)
            act.activation(c_high[:, :, 0:NC], cT[:, :, :], ACT.Copy)
            act.activation(c_split[:, :, 0:NC], cT[:, :, :], ACT.Copy).then_inc(c_hi_made, 1)

            def step(q, par, half, looped):
                if looped or q >= 2:
                    v_gelu_of(q - 2, par, half - 1, looped)
                if looped or q < NQ:
                    h_high(q, par, looped)
                if looped or q < NQ - 1:
                    x_norm(q + 1, 1 - par, half + par, looped)

            def high(n, slot, count, hslot):
                act.wait_ge(w_inn[slot], count * 16 + 16)
                wait(act, blk_mm, n - 1)
                act.activation(w_hi[hslot][:, :, :], wraw[:, slot], ACT.Copy).then_inc(w_hi_made, 1)

            step(0, 0, 0, False)
            wv_high(KD // 2)
            run_steps(act, step, 1, NQ + 1, 4, 8)
            high(0, 0, 0, 0)
            act.wait_ge(xT_made, NQ)
            high(1, 1, 0, 1)
            step(NQ + 1, (NQ + 1) % 2, (NQ + 1) // 2, False)

            def part_high(q, par, j):
                high(q * 3 + (NG + j), (NG + j) % 3, q + (NG + j) // 3, (par + j) % 2)

            def ada_high(q):
                for a in range(2):
                    act.wait_ge(ada_in[a], q * 16 + (ADA_IN + 16))
                    act.wait_ge(ada_mm, q * 2 + (NADA_V - 1 + a))
                    act.activation(ada_hi[a][:, :, :], ada_raw[a][:, :, :], ACT.Copy).then_inc(ada_hi_made, 1)

            v_over(act)
            for g in range(NG):
                act.wait_ge(blk_mm, g + 1)
                wait(act, p_done, g - 1)
                act.activation(in_thirds(pT[g % 2][:, 16:16 + TOK]), thirds(g % 2), ACT.Copy).then_inc(p_cp, 1)
                if g + 2 < NG:
                    high(g + 2, (g + 2) % 3, (g + 2) // 3, g % 2)
                else:
                    part_high(0, 0, g + 2 - NG)
                if g == 1:
                    ada_high(0)
            act.wait_ge(dS_made, 1)

            def f_step(q, par, half, looped):
                act.wait_ge(blk_mm, q * 3 + (NG + 1))
                wait(act, m1_made, q)
                act.activation(in_thirds(u[:, :]), thirds(par), ACT.Gelu_apprx_tanh).then_inc(u_made, 1)
                part_high(q, par, 2)
                act.wait_ge(ada_mm, q * 2 + (NADA_V + 2))
                wait(act, mod_made, q + NADA_V if looped or q > 0 else 0)
                act.activation(clo_rows[:, :], PS[CLO:CLO + NC, MIX, :], ACT.Copy).then_inc(clo_read, 1)
                act.wait_ge(blk_mm, q * 3 + (NG + 2))
                wait(act, m2_made, q)
                act.wait_ge(spare_read, q + 1)
                act.activation(in_thirds(ta[:, :]), thirds(1 - par), ACT.Tanh, scale=0.5).then_inc(ta_made, 1)
                if looped or q + 1 < HD:
                    part_high(q + 1, 1 - par, 0)
                    ada_high(q + 1)
                act.wait_ge(blk_mm, q * 3 + (NG + 3))
                wait(act, yb1_made, q)
                act.activation(in_thirds(tb[:, :]), thirds(par), ACT.Tanh, scale=0.5).then_inc(tb_made, 1)
                if looped or q + 1 < HD:
                    part_high(q + 1, 1 - par, 1)

            run_steps(act, f_step, 0, HD, 2, HD - 2)

            act.wait_ge(blk_mm, NG + 3 * HD)

            def m_high(q, par, half, looped):
                wait(act, y_mm, q - 1)
                if not looped and q == 0:
                    act.wait_ge(mS_made, HD)
                    src, cols = mS[:, :, :], NS
                else:
                    act.wait_ge(mt_in[par], (half + par) * 16)
                    src, cols = mt[:, par], P
                act.activation(mt_hi[par][:, :, 0:cols], src, ACT.Copy).then_inc(ht_hi_made, 1)

            def y_square(q, par, looped):
                r = rows_of(q, looped)
                wait_apart(act, y_mm, q + 1, passed)
                act.activation(x2[0:r, bass.ds(q, 1), :].rearrange("p a d -> p (a d)"), banks(2 * par, 2)[0:r, :],
                               ACT.Square, accum_out=ss2[0:r, par:par + 1]).then_inc(sum_made, 1)

            def x2_square(q, par, half, looped):
                r = rows_of(q, looped)
                wait_apart_if(act, h2_out[par], half * 16, passed)
                wait_apart_if(act, h2_tr, q - 1, passed)
                wait_apart(act, x2_made, q + 1, passed)
                act.activation(h2[0:r, par, :], x2[0:r, bass.ds(q, 1), :].rearrange("p a d -> p (a d)"),
                               ACT.Square, accum_out=ss2[0:r, 2 + par:3 + par]).then_inc(sum2_made, 1)

            def h2_turned(q, par, looped):
                cols = rows_of(q, looped)
                act.wait_ge(h2_tr, q + 1)
                wait(act, lg_mm, q - 1)
                act.activation(h2T[:, par, :, 0:cols],
                               banks(4, 2)[:, 0:KD * cols].rearrange("p (k n) -> p k n", n=cols), ACT.Copy
                               ).then_inc(h2T_made, 1)

            def exps(q, looped):
                r = rows_of(q, looped)
                act.wait_ge(route, q * RC + 7)
                act.activation(exg[0:r, :], lg[0:r, 0:NGR], ACT.Exp, bias=ngm[0:r, :],
                               accum_out=se[0:r, :])
                act.activation(e12[0:r, :], dm[0:r, :], ACT.Exp).then_inc(exp_made, 1)

            for half in range(2):
                cols = slice(half * 512, (half + 1) * 512)
                for k in range(KD):
                    act.wait_ge(w_in_rows[k // (KD // 2)], 32)
                    act.activation(wo_hi[:, k, cols], wo_raw[:, k, cols], ACT.Copy).then_inc(w_hi_k, 1)
                    if half == 0 and k == 1:
                        m_high(0, 0, 0, False)
            f_over(act)
            act.dma_start(rws[0:NS].rearrange("p a d -> p (a d)"), mod_dram[0:NS, :]).then_inc(rows_in, 16)
            act.dma_start(g_post1[:, :], g_post_mix.to_broadcast([P, D])).then_inc(rows_in, 16)
            act.dma_start(g_pre2[:, :], g_pre_ffn.to_broadcast([P, D])).then_inc(rows_in, 16)
            for t, a in ((G1b, R_G1), (A2b, R_A2), (B2b, R_B2)):
                act.dma_start(t[:, :], mod_dram[PRM:NC, a * D:(a + 1) * D].to_broadcast([P, D])
                              ).then_inc(more_rows_in, 16)

            def w_step(q, par, half, looped):
                if not looped and q == 3:
                    act.dma_start(G2b[:, :], mod_dram[PRM:NC, R_G2 * D:(R_G2 + 1) * D].to_broadcast([P, D])
                                  ).then_inc(more_rows_in, 16)
                if looped or 1 <= q <= NQ:
                    y_square(q - 1, 1 - par, looped or q > 1)
                if looped or q + 1 < NQ:
                    m_high(q + 1, 1 - par, half + par, looped or True)
                if not looped and q == NQ + 1:
                    act.wait_ge(y_mm, NQ)
                    act.dma_start(g_post2[:, :], g_post_ffn.to_broadcast([P, D])).then_inc(more_rows_in, 16)
                    h2_turned(q - 2, par, True)
                if looped or q >= 3:
                    exps(q - 3, looped or q > 3)
                if looped or 1 <= q <= NQ:
                    x2_square(q - 1, 1 - par, half - (1 - par), looped or q > 1)
                if looped or 2 <= q <= NQ:
                    h2_turned(q - 2, par, looped or q > 2)

            run_steps(act, w_step, 0, NQ + 3, 4, 8)

            act.wait_ge(lg_mm, NQ)
            act.wait_ge(h2_out[0], 16 * 5)
            act.wait_ge(h2_out[1], 16 * 4)

            def turned_b(n, s):
                par = s % 2
                act.wait_ge(hg_tr, n + 1)
                wait(act, gu_mm, n - 1)
                act.activation(hgT[par][:, 4:8, :].rearrange("p k n -> p (k n)"), PS[:, 1, :], ACT.Copy
                               ).then_inc(hgT_b, 1)

            def store_e(n, s, uses):
                par = s % 2
                act.wait_ge(down_mm, n + 1)
                wait(act, eo_out[par], uses * 16)
                act.activation(ysb[:, par, :], banks(5, 2), ACT.Copy).then_inc(ysb_made, 1)

            def e_step(n, s, oct_, looped):
                par = s % 2
                if looped or n + 1 < NE:
                    turned_b(n + 1, s + 1)
                if looped or n < NE:
                    act.wait_ge(gu_mm, n + 1)
                    wait(act, act_made, n - 1)
                    act.activation(sil[:, par, :], PS[:, 2 + par, 0:P], ACT.Silu).then_inc(silu_made, 1)
                if looped or n >= 1:
                    store_e(n - 1, s + 1, oct_ * (RING // 2) + (s - 1) // 2)

            turned_b(0, 0)
            run_steps(act, e_step, 0, NE + 1, RING, NE - RING, RING)

            act.wait_ge(cnt_made, 2)
            fullest = act.value_load(most_u[0:1, 0:1], min_val=0, max_val=TOK)
            with act.If(fullest > P):
                with act.Fori(1, NQ) as c:
                    with act.Fori(0, NE) as x:
                        act.wait_ge(o_pe, ((c - 1) * NE + x) * 3 + 2)
                        act.activation(sil[:, 0, :], PS[:, 2, 0:P], ACT.Silu).then_inc(o_act, 1)

            def f1_of(q, s, quad, looped):
                r = rows_of(q, looped)
                arrived, before = Y_IN[s]
                wait_apart(act, arrived, quad * 16 + (before + 16), passed)
                wait_apart_if(act, f_made, q - 1, passed)
                act.activation(f1[0:r, s % 2, :], yg[0:r, s, 0, :], ACT.Copy, scale=wts[0:r, bass.ds(q, 1), 0]
                               ).then_inc(f1_made, 1)

            f1_of(0, 0, 0, False)

            def end_step(q, s, quad, looped):
                r, par = rows_of(q, looped), s % 2
                if looped or q + 1 < NQ:
                    f1_of(q + 1, (s + 1) % 4, quad + (s + 1) // 4, looped or True)
                act.wait_ge(f_made, q + 1)
                act.activation(fj[0:r, par, :], ff[0:r, par, :], ACT.Square, accum_out=ss[0:r, par:par + 1]
                               ).then_inc(sum_made, 1)

            run_steps(act, end_step, 0, NQ, 4, 8, 4)

        @block.vector
        def _(dve):
            dve.wait_ge(pre_tr, KD)
            dve.tensor_copy(cT[:, :, :].rearrange("p k n -> p (k n)"), PS[:, 6, 0:KD * NC]).then_inc(pre_cp, 1)
            dve.wait_ge(pre_tr, KD + 1)
            dve.tensor_copy(vecT[:, :], PS[:, 7, 0:NV]).then_inc(pre_cp, 1)

            dve.wait_ge(pre_cp, 2)

            def row_chunk(n):
                dve.wait_ge(ada_mm, n + 1)
                dve.tensor_copy(rows0[:, n * CH:(n + 1) * CH], PS[0:NC, 2 + n % 4, 0:CH]).then_inc(mod_made, 1)

            def wv_low(k):
                dve.wait_ge(w_hi_k, k + 1)
                dve.tensor_tensor(wv_lo[:, k, :], wv_raw[:, k, :], wv_hi[:, k, :].bitcast(F32),
                                  ALU.subtract).then_inc(w_lo_k, 1)

            for n in range(NADA_V):
                row_chunk(n)
                if n >= 3 and n < 7:
                    wv_low(n - 3)
            dve.wait_ge(mod_tr, NADA_V)
            dve.tensor_tensor(modT[:, :, :], PS[:, 6, 0:2 * KD * NC].rearrange("p (m n) -> p m n", n=NC),
                              vecT[:, 0:2 * KD].unsqueeze(2).to_broadcast([P, 2 * KD, NC]), ALU.add
                              ).then_inc(prep_made, 1)
            dve.wait_ge(prep_made, 1)
            dve.scalar_tensor_tensor(A1T[:, :, :], modT[:, KD:2 * KD, :], 1.0,
                                     vecT[:, VEC["pre_mix"]:VEC["pre_mix"] + KD].unsqueeze(2)
                                     .to_broadcast([P, KD, NC]), ALU.add, ALU.mult).then_inc(prep_made, 1)
            dve.tensor_scalar(psh[:, :], vecT[:, VEC["pool_scale"]:VEC["pool_scale"] + KD], 0.5, None,
                              ALU.mult).then_inc(prep_made, 1)
            dve.wait_ge(consts, 3)
            dve.reciprocal(invc[:, :], inv_n[:, :]).then_inc(prep_made, 1)
            dve.wait_ge(c_hi_made, 1)
            dve.tensor_tensor(c_split[:, :, CLO:CLO + NC], cT[:, :, :], c_split[:, :, 0:NC].bitcast(F32), ALU.subtract
                              ).then_inc(c_lo_made, 1)
            dve.wait_ge(prep_made, 2)

            def h_of(q, par, looped):
                sample = not looped and q == 0
                cols = NS if sample else P
                sl = slice(0, NS) if sample else slice(PRM, PRM + 1)
                ps = banks(0, 2)[:, 0:KD * cols].rearrange("p (k n) -> p k n", n=cols)
                wait(dve, xT_made, q + 1)
                wait(dve, ht_lo_made, q)
                dve.tensor_tensor(h[:, :, 0:cols], ps, A1T[:, :, sl].to_broadcast([P, KD, cols]), ALU.mult
                                  ).then_inc(h_scaled, 1)
                dve.wait_ge(h_scaled, q + 1)
                dve.tensor_tensor(h[:, :, 0:cols], h[:, :, 0:cols],
                                  modT[:, 0:KD, sl].to_broadcast([P, KD, cols]), ALU.add
                                  ).then_inc(h_made, 1)

            def h_low(q, par, looped):
                cols = NS if not looped and q == 0 else P
                wait(dve, ht_hi_made, q + 1)
                dve.tensor_tensor(ht_lo[par][:, :, 0:cols], h[:, :, 0:cols],
                                  ht_hi[par][:, :, 0:cols].bitcast(F32), ALU.subtract).then_inc(ht_lo_made, 1)

            def v_stats(q, par, looped):
                rows = NS if not looped and q == 0 else P
                wait(dve, v_gelu, q + 1)
                for j in range(2):
                    b = dve.bn_stats(bn6[0:rows, j, :], vg[0:rows, par, j * 512:(j + 1) * 512])
                b.then_inc(v_bn, 1)
                wait_apart(dve, v_bn, q + 1, passed)
                dve.bn_aggr(mv[0:rows, :], bn6[0:rows, :, :].rearrange("p a b -> p (a b)")).then_inc(sum2_made, 1)

            def v_norm(q, par, looped):
                rows = NS if not looped and q == 0 else P
                t = vg[0:rows, par, :]
                wait(dve, sum2_root, q + 1)
                dve.tensor_scalar(t, t, mv[0:rows, 0:1], vr[0:rows, :], ALU.subtract, ALU.mult
                                  ).then_inc(v_step, 1)
                dve.wait_ge(v_step, q * 2 + 1)
                dve.tensor_tensor(t, t, lng[0:rows, :], ALU.mult).then_inc(v_step, 1)
                dve.wait_ge(v_step, q * 2 + 2)
                dve.tensor_tensor(t, t, lnb[0:rows, :], ALU.add).then_inc(v_made, 1)

            def step(q, par, half, looped):
                if looped or q < NQ:
                    h_of(q, par, looped)
                if looped or q >= 2:
                    v_stats(q - 2, par, looped)
                if looped or q < NQ:
                    h_low(q, par, looped)
                if looped or q >= 2:
                    v_norm(q - 2, par, looped)

            step(0, 0, 0, False)
            for k in range(KD // 2, KD):
                wv_low(k)
            dve.wait_ge(later_in, LATER)
            run_steps(dve, step, 1, NQ + 1, 4, 8)

            def low(n, slot, hslot):
                dve.wait_ge(w_hi_made, n + 1)
                dve.tensor_tensor(w_lo[hslot][:, :, :], wraw[:, slot], w_hi[hslot][:, :, :].bitcast(F32),
                                  ALU.subtract).then_inc(w_lo_made, 1)

            low(0, 0, 0)
            dve.wait_ge(later_in, LATER)
            dve.wait_ge(consts, 2)
            dve.tensor_tensor(w00d[:, :, :], w00[:, :].unsqueeze(2).to_broadcast([NS, HD, NS]),
                              ident[0:NS, 0:NS].unsqueeze(1).to_broadcast([NS, HD, NS]), ALU.mult
                              ).then_inc(prep_made, 1)
            dve.wait_ge(v_mm, NQ - 1)
            dve.wait_ge(hT_kept, 2 * NQ - 2)
            low(1, 1, 1)
            step(NQ + 1, (NQ + 1) % 2, (NQ + 1) // 2, False)
            v_over(dve)
            for t in pT:
                z = dve.memset(t[:, 0:16], 0.0)
            z.then_inc(p_step, 1)
            dve.wait_ge(p_step, 1)

            done = 1

            def link(ins):
                nonlocal done
                ins.then_inc(p_step, 1)
                done += 1
                dve.wait_ge(p_step, done)

            def pool_group(g):
                w = 2 << g
                src = pT[g % 2]
                dve.wait_ge(p_cp, g + 1)
                dve.tensor_copy(ptail[:, g, :], src[:, 16 + SEQ - PST:16 + SEQ])
                dve.tensor_copy(psm[:, g, :], src[:, 16 + SEQ:16 + TOK])
                at, wide = src, 1
                while wide < w:
                    out = pa if at is not pa else pb
                    low_ = 2 * wide - 1
                    link(dve.tensor_tensor(out[:, low_:16 + SEQ], at[:, low_:16 + SEQ],
                                           at[:, low_ - wide:16 + SEQ - wide], ALU.add))
                    at, wide = out, 2 * wide
                dst = dT[:, g, 0:SEQ]
                link(dve.scalar_tensor_tensor(dst, at[:, 16:16 + SEQ], 1.0 / w, src[:, 16:16 + SEQ], ALU.mult, ALU.subtract))
                link(dve.tensor_tensor(fix[:, 0:w], at[:, 16:16 + w], invc[:, 0:w], ALU.mult))
                dve.tensor_tensor(dT[:, g, 0:w], fix[:, 0:w], src[:, 16:16 + w], ALU.subtract
                                  ).then_inc(p_done, 1)

            dve.wait_ge(prep_made, 5)

            def part_low(q, par, j):
                low(q * 3 + (NG + j), (NG + j) % 3, (par + j) % 2)

            def ada_low(q):
                for a in range(2):
                    dve.wait_ge(ada_hi_made, q * 2 + (a + 1))
                    dve.tensor_tensor(ada_lo[a][:, :, :], ada_raw[a][:, :, :], ada_hi[a][:, :, :].bitcast(F32),
                                      ALU.subtract).then_inc(ada_lo_made, 1)

            def flat(ap):
                return ap.rearrange("p h n -> p (h n)")

            for g in range(NG):
                if g + 2 < NG:
                    low(g + 2, (g + 2) % 3, g % 2)
                else:
                    part_low(0, 0, g + 2 - NG)
                pool_group(g)
                if g == 1:
                    dve.wait_ge(ws_tr, 1)
                    dve.tensor_copy(flat(spT[:, :, :]), PS[:, MIX, 0:NG * NS * PST]).then_inc(ws_cp, 1)
                    dve.wait_ge(ws_tr, 2)
                    dve.tensor_copy(flat(wsT[:, 4:8, :]), PS[:, MIX + 1, :]).then_inc(ws_cp, 1)
                if g == 2:
                    ada_low(0)
                    dve.wait_ge(ws_tr, 3)
                    dve.tensor_copy(flat(wsT[:, 0:4, :]), PS[:, MIX, :]).then_inc(ws_cp, 1)
            for g in range(NG):
                w = 2 << g
                link(dve.tensor_reduce(pws[:, g, :], spT[:, g, :].rearrange("p (n r) -> p n r", r=PST)
                                       [:, :, PST - (w - 1):PST], AX_X, ALU.add))
            link(dve.tensor_tensor(pws[:, :, :], pws[:, :, :], psm[:, :, :], ALU.add))
            for g in range(NG):
                d = dve.scalar_tensor_tensor(dT[:, g, SEQ:TOK], pws[:, g, :], 1.0 / (2 << g), psm[:, g, :],
                                             ALU.mult, ALU.subtract)
            d.then_inc(dS_made, 1)

            def f_step(q, par, half, looped):
                part_low(q, par, 2)
                wait(dve, mod_out[par], half * 16)
                dve.wait_ge(wpl_in[par], half * 32 + 32)
                dve.wait_ge(ada_mm, q * 2 + (NADA_V + 2))
                dve.tensor_tensor(rowbuf[:, par, :], PS[0:NC, MIX, :], bias[:, par, :], ALU.add).then_inc(mod_part, 1)
                dve.wait_ge(mod_part, q + 1)
                dve.wait_ge(clo_read, q + 1)
                dve.tensor_tensor(rowbuf[:, par, :], rowbuf[:, par, :], clo_rows[:, :], ALU.add).then_inc(mod_made, 1)
                bank = REGION[1 - par]
                dve.wait_ge(blk_mm, q * 3 + (NG + 2))
                wait(dve, mg_made, q)
                dve.tensor_scalar(m0[:, SEQ:TOK], PS[:, bank, SMIX_AT:SMIX_AT + NS],
                                  bsb[:, bass.ds(q, 1), 0:1].rearrange("p a n -> p (a n)"), None, ALU.add)
                dve.tensor_copy(ybs[:, :], PS[:, bank, SYB_AT:SYB_AT + NS]).then_inc(spare_read, 1)
                if not looped and q == 0:
                    dve.wait_ge(tail_tr, 1)
                    dve.tensor_copy(ptok[:, :], PS[0:PST, MIX, :])
                    dve.tensor_copy(pstok[:, :], PS[0:NS, MIX + 1, :]).then_inc(tail_cp, 1)
                dve.wait_ge(mix_mm, q + 1)
                dve.tensor_tensor(m0[:, 0:SEQ].rearrange("p (t i) -> p t i", i=P),
                                  banks(MIX, 2).rearrange("p (t i) -> p t i", i=P),
                                  bsb[:, bass.ds(q, 1), :].to_broadcast([P, NT, P]), ALU.add
                                  ).then_inc(m0_made, 1)
                dve.wait_ge(m0_made, q + 1)
                dve.wait_ge(u_made, q + 1)
                dve.scalar_tensor_tensor(m0[:, :], m0[:, :], 0.5, u[:, :], ALU.mult, ALU.mult
                                         ).then_inc(m1_made, 1)
                dve.wait_ge(m1_made, q + 1)
                dve.wait_ge(ta_made, q + 1)
                dve.scalar_tensor_tensor(m0[:, :], ta[:, :], 1.0, m0[:, :], ALU.add, ALU.mult
                                         ).then_inc(m2_made, 1)
                if looped or q + 1 < HD:
                    part_low(q + 1, 1 - par, 0)
                    ada_low(q + 1)
                dve.wait_ge(tb_made, q + 1)
                dve.scalar_tensor_tensor(yb1[:, SEQ:TOK], tb[:, SEQ:TOK], 1.0, ybs[:, :], ALU.add, ALU.mult)
                dve.wait_ge(yb_mm, q + 1)
                dve.scalar_tensor_tensor(yb1[:, 0:SEQ], tb[:, 0:SEQ], 1.0, banks(MIX, 2), ALU.add, ALU.mult
                                         ).then_inc(yb1_made, 1)
                if looped or q + 1 < HD:
                    part_low(q + 1, 1 - par, 1)
                dve.wait_ge(yb1_made, q + 1)
                dve.wait_ge(m2_made, q + 1)
                wait(dve, mg_out[par], half * 16)
                if not looped and q == 1:
                    dve.wait_ge(st_out, 32)
                dve.scalar_tensor_tensor(mS[:, bass.ds(q, 1), :].rearrange("p a n -> p (a n)"), yb1[:, SEQ:TOK],
                                         psh[:, bass.ds(q, 1)], m0[:, SEQ:TOK], ALU.mult, ALU.add
                                         ).then_inc(mS_made, 1)
                dve.scalar_tensor_tensor(mg[:, par, :], yb1[:, :], psh[:, bass.ds(q, 1)], m0[:, :],
                                         ALU.mult, ALU.add).then_inc(mg_made, 1)

            run_steps(dve, f_step, 0, HD, 2, HD - 2)

            def m_low(q, par, looped):
                src, cols = (mS[:, :, :], NS) if rows_of(q, looped) == NS else (mt[:, par], P)
                dve.wait_ge(ht_hi_made, q + (NQ + 1))
                dve.tensor_tensor(mt_lo[par][:, :, 0:cols], src, mt_hi[par][:, :, 0:cols].bitcast(F32),
                                  ALU.subtract).then_inc(ht_lo_made, 1)

            def turned(ap):
                return ap.rearrange("q (p k) -> q k p", k=KD)

            def straight(ap):
                return ap.rearrange("q (k p) -> q k p", k=KD)

            def x2_at(q, r):
                return x2[0:r, bass.ds(q, 1), :].rearrange("p a d -> p (a d)")

            def residual(q, par, half, looped):
                r = rows_of(q, looped)
                g1 = rws[0:NS, R_G1, :] if r == NS else G1b[:, :]
                dve.wait_ge(sum_root, q + (NQ + 1))
                dve.scalar_tensor_tensor(x2_at(q, r), banks(2 * par, 2)[0:r, :], rs2[0:r, par:par + 1], g1,
                                         ALU.mult, ALU.mult).then_inc(y_scaled, 1)
                dve.wait_ge(y_scaled, q + 1)
                dve.wait_ge(x_in[par], half * 16 + (X_IN[par] + 16))
                dve.tensor_tensor(x2_at(q, r), x2_at(q, r), xw[0:r, par, :], ALU.add).then_inc(x2_made, 1)

            def modulate(q, par, looped):
                r = rows_of(q, looped)
                if r == NS:
                    a2, b2 = turned(rws[0:NS, R_A2, :]), turned(rws[0:NS, R_B2, :])
                else:
                    a2, b2 = turned(A2b[:, :]), turned(B2b[:, :])
                out = straight(h2[0:r, par, :])
                dve.wait_ge(sum2_root, q + (NQ + 1))
                dve.scalar_tensor_tensor(out, turned(x2_at(q, r)), rs2[0:r, 2 + par:3 + par], a2,
                                         ALU.mult, ALU.mult).then_inc(h2_scaled, 1)
                dve.wait_ge(h2_scaled, q + 1)
                dve.tensor_tensor(out, out, b2, ALU.add).then_inc(h2_made, 1)

            def chain(sm, base):
                n = 0

                def link(ins):
                    nonlocal n
                    n += 1
                    ins.then_inc(sm, 1)
                    wait_apart(dve, sm, base + n, passed)
                    return n
                return link

            def route_of(q, looped):
                r = rows_of(q, looped)
                link = chain(route, q * RC)
                dve.wait_ge(lg_mm, q + 1)
                dve.tensor_tensor(lg[0:r, :], PS[0:r, 6, 0:NL], biasr[0:r, :], ALU.add).then_inc(lg_made, 1)
                wait_apart(dve, lg_made, q + 1, passed)
                link(dve.max(gtop[0:r, :], lg[0:r, 0:8]))
                dve.tensor_scalar(ngm[0:r, :], gtop[0:r, 0:1], -1.0, None, ALU.mult)
                link(dve.max_index(gix[0:r, :], gtop[0:r, :], lg[0:r, 0:8]))
                dve.tensor_copy(gid[0:r, :], gix[0:r, 0:1])
                link(dve.tensor_tensor(ohg[0:r, :], iota8[0:r, 0:NGR], gix[0:r, 0:1].to_broadcast([r, NGR]),
                                       ALU.is_equal))
                link(dve.tensor_tensor(t32[0:r, :].rearrange("p (g e) -> p g e", e=EPG),
                                       lg[0:r, 8:NL].rearrange("p (g e) -> p g e", e=EPG),
                                       ohg[0:r, :].unsqueeze(2).to_broadcast([r, NGR, EPG]), ALU.mult))
                link(dve.tensor_reduce(s8[0:r, :], t32[0:r, :].rearrange("p (g e) -> p e g", e=EPG), AX_X, ALU.add))
                link(dve.max(etop[0:r, :], s8[0:r, :]))
                dve.tensor_tensor(dm[0:r, :], etop[0:r, 1:2], etop[0:r, 0:1], ALU.subtract)
                link(dve.max_index(eix[0:r, :], etop[0:r, :], s8[0:r, :]))
                dve.tensor_copy(ei[0:r, :], eix[0:r, 0:2])
                link(dve.tensor_tensor(oh12[0:r, :, :], iota8[0:r, :].unsqueeze(1).to_broadcast([r, 2, 8]),
                                       eix[0:r, 0:2].unsqueeze(2).to_broadcast([r, 2, 8]), ALU.is_equal))
                for j in range(2):
                    x = dve.tensor_tensor(m12[0:r, j, :].rearrange("p (g e) -> p g e", e=EPG),
                                          ohg[0:r, :].unsqueeze(2).to_broadcast([r, NGR, EPG]),
                                          oh12[0:r, j, :].unsqueeze(1).to_broadcast([r, NGR, EPG]), ALU.mult)
                n = link(x)
                assert n == RC - 3
                dve.tensor_tensor(mb[0:r, :], m12[0:r, 0, :], m12[0:r, 1, :], ALU.add).then_inc(m_made, 1)
                dve.scalar_tensor_tensor(eid[0:r, :], gid[0:r, :].to_broadcast([r, 2]), float(EPG), ei[0:r, :],
                                         ALU.mult, ALU.add).then_inc(eid_made, 1)

            def weights_of(q, looped):
                r = rows_of(q, looped)
                wait_apart(dve, exp_made, q + 1, passed)
                dve.tensor_scalar(e1[0:r, :], e12[0:r, :], 1.0, None, ALU.add)
                dve.reciprocal(pg[0:r, :], se[0:r, :]).then_inc(route, 1)
                wait_apart(dve, route, q * RC + 10, passed)
                dve.reciprocal(rw[0:r, :], e1[0:r, :]).then_inc(route, 1)
                wait_apart(dve, route, q * RC + 11, passed)
                dve.tensor_tensor(wts[0:r, bass.ds(q, 1), 0], rw[0:r, :], pg[0:r, :], ALU.mult).then_inc(route, 1)
                wait_apart(dve, route, q * RC + 12, passed)
                dve.tensor_tensor(wts[0:r, bass.ds(q, 1), 1], wts[0:r, bass.ds(q, 1), 0], e12[0:r, :], ALU.mult
                                  ).then_inc(wts_made, 1)

            def slots_of(q, par, half, looped):
                r = rows_of(q, looped)
                wait_apart(dve, pos_mm, q + 1, passed)
                dve.tensor_tensor(mp[0:r, :, :], PS[0:r, 7, 0:NE].unsqueeze(1).to_broadcast([r, 2, NE]),
                                  m12[0:r, :, :], ALU.mult).then_inc(mp_made, 1)
                dve.wait_ge(eid_made, q + 1)
                dve.tensor_tensor(mrun[0:r, :], mrun[0:r, :], mb[0:r, :], ALU.add).then_inc(mrun_made, 1)
                wait_apart(dve, mp_made, q + 1, passed)
                wait_apart_if(dve, scat[par], half * 32 + SCAT_IN[par], passed)
                dve.tensor_copy(tidu[0:r, par, :, 0], tid[0:r, :].to_broadcast([r, 2]))
                for j in range(2):
                    dve.tensor_scalar(tidu[0:r, par, j, 1:2], tid[0:r, :], 2.0, float(j), ALU.mult, ALU.add)
                dve.tensor_reduce(pos[0:r, :], mp[0:r, :, :], AX_X, ALU.add).then_inc(slot_step, 1)
                wait_apart(dve, slot_step, q * SC + 1, passed)
                for j in range(2):
                    z = dve.scalar_tensor_tensor(lrow[par][j][0:r, :], pos[0:r, j:j + 1], float(NE), eid[0:r, j:j + 1],
                                                 ALU.mult, ALU.add)
                z.then_inc(slot_made, 1)
                dve.tensor_scalar(tid[:, :], tid[:, :], float(-SEQ if r == NS else P), None, ALU.add
                                  ).then_inc(slot_step, 1)
                wait_apart(dve, slot_step, q * SC + 2, passed)

            for half in range(2):
                cols = slice(half * 512, (half + 1) * 512)
                for k in range(KD):
                    dve.wait_ge(w_hi_k, KD + half * KD + k + 1)
                    dve.tensor_tensor(wo_lo[:, k, cols], wo_raw[:, k, cols], wo_hi[:, k, cols].bitcast(F32),
                                      ALU.subtract).then_inc(w_lo_k, 1)
                    if half == 0 and k == 0:
                        m_low(0, 0, False)
            def w_step(q, par, half, looped):
                if looped or q >= 3:
                    route_of(q - 3, looped or q > 3)
                if looped or 1 <= q <= NQ:
                    residual(q - 1, 1 - par, half - (1 - par), looped or q > 1)
                if not looped and q > NQ:
                    slots_of(q - 3, 1 - par, half + par - 2, True)
                if looped or q + 1 < NQ:
                    m_low(q + 1, 1 - par, looped or True)
                if looped or q >= 3:
                    weights_of(q - 3, looped or q > 3)
                if looped or 1 <= q <= NQ:
                    modulate(q - 1, 1 - par, looped or q > 1)
                if looped or 3 <= q <= NQ:
                    slots_of(q - 3, 1 - par, half + par - 2, looped or q > 3)

            w_step(0, 0, 0, False)
            f_over(dve)
            dve.wait_ge(rows_in, 16 * 3)
            dve.tensor_tensor(rws[0:NS, R_G1], rws[0:NS, R_G1], g_post1[0:NS, :], ALU.mult).then_inc(rows_made, 1)
            dve.scalar_tensor_tensor(rws[0:NS, R_A2], rws[0:NS, R_A2], 1.0, g_pre2[0:NS, :], ALU.add, ALU.mult
                                     ).then_inc(rows_made, 1)
            dve.wait_ge(later_in, LATER)
            dve.wait_ge(more_rows_in, 16 * 3)
            dve.tensor_tensor(G1b[:, :], G1b[:, :], g_post1[:, :], ALU.mult).then_inc(rows_made, 1)
            dve.scalar_tensor_tensor(A2b[:, :], A2b[:, :], 1.0, g_pre2[:, :], ALU.add, ALU.mult).then_inc(rows_made, 1)
            dve.wait_ge(rows_made, 4)
            run_steps(dve, w_step, 1, NQ + 3, 4, 8)
            dve.wait_ge(cnt_mm, 1)
            dve.tensor_reduce(most[:, :], PS[:, 7, 0:NE], AX_X, ALU.max).then_inc(cnt_made, 1)
            dve.wait_ge(cnt_made, 1)
            dve.tensor_copy(most_u[:, :], most[:, :]).then_inc(cnt_made, 1)

            def turned_a(n, s):
                par = s % 2
                dve.wait_ge(hg_tr, n + 1)
                wait(dve, gu_mm, n - 1)
                dve.tensor_copy(hgT[par][:, 0:4, :].rearrange("p k n -> p (k n)"), PS[:, 0, :]).then_inc(hgT_a, 1)

            def e_step(n, s, oct_, looped):
                par = s % 2
                if looped or n + 1 < NE:
                    turned_a(n + 1, s + 1)
                dve.wait_ge(silu_made, n + 1)
                wait(dve, down_mm, n - 1)
                dve.tensor_tensor(actT[:, par, :], PS[:, 2 + par, P:2 * P], sil[:, par, :], ALU.mult
                                  ).then_inc(act_made, 1)

            turned_a(0, 0)
            run_steps(dve, e_step, 0, NE, RING, NE - RING, RING)

            dve.wait_ge(more_rows_in, 16 * 5)
            dve.tensor_tensor(G2b[:, :], G2b[:, :], g_post2[:, :], ALU.mult).then_inc(rows_made, 1)
            dve.tensor_tensor(rws[0:NS, R_G2], rws[0:NS, R_G2], g_post2[0:NS, :], ALU.mult).then_inc(rows_made, 1)
            dve.wait_ge(rows_made, 6)

            fullest = dve.value_load(most_u[0:1, 0:1], min_val=0, max_val=TOK)
            with dve.If(fullest > P):
                with dve.Fori(1, NQ) as c:
                    with dve.Fori(0, NE) as x:
                        m = (c - 1) * NE + x
                        dve.wait_ge(o_pe, m * 3 + 1)
                        dve.tensor_copy(hgT[0][:, :, :].rearrange("p k n -> p (k n)"), banks(0, 2)
                                        ).then_inc(o_dve, 1)
                        dve.wait_ge(o_act, m + 1)
                        dve.tensor_tensor(actT[:, 0, :], PS[:, 2, P:2 * P], sil[:, 0, :], ALU.mult
                                          ).then_inc(o_dve, 1)
                        dve.wait_ge(o_pe, m * 3 + 3)
                        dve.tensor_copy(ysb[:, 0, :], banks(5, 2)).then_inc(o_dve, 1)

            def sum_of(q, s, quad, looped):
                r, par = rows_of(q, looped), s % 2
                arrived, before = Y_IN[s]
                dve.wait_ge(f1_made, q + 1)
                dve.wait_ge(arrived, quad * 16 + (before + 16))
                wait(dve, f_scaled, q - 1)
                dve.scalar_tensor_tensor(ff[0:r, par, :], yg[0:r, s, 1, :], wts[0:r, bass.ds(q, 1), 1],
                                         f1[0:r, par, :], ALU.mult, ALU.add).then_inc(f_made, 1)

            def end_step(q, s, quad, looped):
                r, par = rows_of(q, looped), s % 2
                g2 = rws[0:NS, R_G2, :] if r == NS else G2b[:, :]
                if looped or q + 1 < NQ:
                    sum_of(q + 1, (s + 1) % 4, quad + (s + 1) // 4, looped or True)
                dve.wait_ge(sum_root, q + (2 * NQ + 1))
                wait(dve, y_out[par], quad * 32 + 16 * (s // 2))
                dve.scalar_tensor_tensor(fo[0:r, par, :], ff[0:r, par, :], rstd[0:r, par:par + 1], g2,
                                         ALU.mult, ALU.mult).then_inc(f_scaled, 1)
                dve.wait_ge(f_scaled, q + 1)
                dve.tensor_tensor(fo[0:r, par, :], fo[0:r, par, :], x2_at(q, r), ALU.add).then_inc(fo_made, 1)

            sum_of(0, 0, 0, False)
            run_steps(dve, end_step, 0, NQ, 4, 8, 4)

        @block.tensor
        def _(pe):
            pe.wait_ge(consts, 2)
            pe.wait_ge(c_silu, 1)
            for k in range(KD):
                pe.transpose(PS[:, 6, k * NC:(k + 1) * NC], sc9[:, k * P:(k + 1) * P], ident[0:NC, 0:NC]
                             ).then_inc(pre_tr, 1)
            pe.wait_ge(vec_in, 16 * 3)
            pe.transpose(PS[:, 7, 0:NV], vecs[:, :], ident[0:NV, 0:NV]).then_inc(pre_tr, 1)

            def ada_chunk(slot, ring, uses, bank, col):
                pe.wait_ge(ada_in[slot], uses * 16 + 16)
                for k in range(KD):
                    mm = pe.matmul(PS[0:NC, bank, col:col + CH], cT[:, k, :], ring[:, slot, k, :],
                                   start=(k == 0), stop=(k == KD - 1))
                mm.then_inc(ada_mm, 1)

            def turn_rows(n):
                pe.wait_ge(mod_made, n + 1)
                for m in range(n * CPM, (n + 1) * CPM):
                    mm = pe.transpose(PS[:, 6, m * NC:(m + 1) * NC], rows0[:, m * P:(m + 1) * P], ident[0:NC, 0:NC])
                mm.then_inc(mod_tr, 1)

            def x_turn(q, looped):
                rows = NS if not looped and q == 0 else P
                wait(pe, x_normed, q + 1)
                wait(pe, h_scaled, q)
                for k in range(KD):
                    mm = pe.transpose(banks(0, 2)[:, k * rows:(k + 1) * rows], xn[0:rows, k * P:(k + 1) * P],
                                      ident[0:rows, 0:rows])
                mm.then_inc(xT_made, 1)

            def v_products(q, par, looped, half, ks):
                rows = NS if not looped and q == 0 else P
                cols = slice(half * 512, (half + 1) * 512)
                for k in ks:
                    if not looped and q == 0:
                        pe.wait_ge(w_lo_k, k + 1)
                    for j, (a, b) in enumerate(((ht_hi, wv_hi), (ht_hi, wv_lo), (ht_lo, wv_hi))):
                        mm = pe.matmul(PS[0:rows, 2 + 2 * par + half, :], a[par][:, k, 0:rows], b[:, k, cols],
                                       start=(k == 0 and j == 0), stop=(k == KD - 1 and j == 2))
                return mm

            def v_of(q, par, looped):
                wait(pe, ht_lo_made, q + 1)
                wait(pe, v_gelu, q - 1)
                v_products(q, par, looped, 0, range(KD))
                v_products(q, par, looped, 1, range(KD)).then_inc(v_mm, 1)

            pe.wait_ge(pre_cp, 1)
            for n in range(NADA_V):
                wait(pe, mod_made, n - 3)
                ada_chunk(n % 4, adaV, n // 4, 2 + n % 4, 0)
                if n:
                    turn_rows(n - 1)
            turn_rows(NADA_V - 1)
            x_turn(0, False)

            def step(q, par, half, looped):
                if looped or q < NQ:
                    x_turn(q, looped)
                v_of(q - 1, 1 - par, looped or q > 1)

            pe.wait_ge(ht_lo_made, 1)
            for half in range(2):
                v_products(0, 0, False, half, range(KD // 2))
            x_turn(1, False)
            v_products(0, 0, False, 0, range(KD // 2, KD))
            v_products(0, 0, False, 1, range(KD // 2, KD)).then_inc(v_mm, 1)
            run_steps(pe, step, 2, NQ + 1, 4, 8)

            def project(n, hslot, region):
                pe.wait_ge(w_lo_made, n + 1)
                for k in range(KD):
                    for j, (a, b) in enumerate(((w_hi, hT_hi), (w_hi, hT_lo), (w_lo, hT_hi))):
                        for t in range(3):
                            mm = pe.matmul(PS[:, REGION[region] + t, 0:THIRD], a[hslot][:, k, :],
                                           b[:, k, t * THIRD:(t + 1) * THIRD], start=(k == 0 and j == 0),
                                           stop=(k == KD - 1 and j == 2))
                mm.then_inc(blk_mm, 1)

            pe.wait_ge(prep_made, 5)
            pe.wait_ge(c_lo_made, 1)
            pe.wait_ge(hT_kept, 2 * NQ)
            pe.wait_ge(v_gelu, NQ - 1)
            project(0, 0, 0)
            pe.wait_ge(v_gelu, NQ)
            project(1, 1, 1)
            pe.wait_ge(fc_in, 48)
            for g in range(NG):
                mm = pe.transpose(PS[:, MIX, g * NS * PST:(g + 1) * NS * PST], spr[:, g * P:(g + 1) * P],
                                  ident[0:NS * PST, 0:NS * PST])
            mm.then_inc(ws_tr, 1)

            def turn_maps(first, bank):
                for j in range(4):
                    mm = pe.transpose(PS[:, bank, j * P:(j + 1) * P], ws[:, first + j, :], ident[:, :])
                mm.then_inc(ws_tr, 1)

            pe.wait_ge(ws_masked, 1)
            turn_maps(4, MIX + 1)
            pe.wait_ge(p_cp, 1)
            project(2, 0, 0)
            pe.wait_ge(ws_cp, 1)
            turn_maps(0, MIX)
            pe.wait_ge(p_cp, 2)
            project(3, 1, 1)

            def ada_products(q, a):
                pe.wait_ge(ada_lo_made, q * 2 + (a + 1))
                cols = slice(a * CH, (a + 1) * CH)
                for k in range(KD):
                    pe.matmul(PS[0:CLO + NC, MIX, cols], c_split[:, k, :], ada_hi[a][:, k, :],
                              start=(k == 0), stop=False)
                    mm = pe.matmul(PS[0:CLO + NC, MIX, cols], c_high[:, k, :], ada_lo[a][:, k, :],
                                   start=False, stop=(k == KD - 1))
                mm.then_inc(ada_mm, 1)

            def part(q, par, j):
                project(q * 3 + (NG + j), (par + j) % 2, (par + j) % 2)

            def tails():
                for g in range(NG):
                    pe.transpose(PS[0:PST, MIX, g * P:(g + 1) * P], ptail[:, g, :], ident[:, :])
                for g in range(NG):
                    mm = pe.transpose(PS[0:NS, MIX + 1, g * P:(g + 1) * P], psm[:, g, :], ident[:, :])
                mm.then_inc(tail_tr, 1)

            def f_step(q, par, half, looped):
                first = not looped and q == 0
                if first:
                    pe.wait_ge(p_cp, NG - 1)
                else:
                    pe.wait_ge(ta_made, q)
                part(q, par, 0)
                if first:
                    pe.wait_ge(ws_cp, 3)
                else:
                    pe.wait_ge(yb1_made, q)
                for a in range(2):
                    ada_products(q, a)
                if first:
                    pe.wait_ge(p_cp, NG)
                    pe.wait_ge(dS_made, 1)
                else:
                    pe.wait_ge(tb_made, q)
                bank = REGION[1 - par]
                pe.wait_ge(vfs_in[par], half * 16 + 16)
                pe.matmul(PS[:, bank, SMIX_AT:SMIX_AT + NS], vfs[:, par, :],
                          w00d[:, bass.ds(q, 1), :].rearrange("p a i -> p (a i)"), start=True, stop=True)
                pe.wait_ge(wpl_in[par], half * 32 + 32)
                pe.matmul(PS[:, bank, SYB_AT:SYB_AT + NS], wpl[:, par, :],
                          dT[:, bass.ds(half, 1), SEQ:TOK].rearrange("p a n -> p (a n)"), start=True, stop=True)
                part(q, par, 1)
                pe.wait_ge(vf_in[par], half * 16 + 16)
                pe.wait_ge(mod_made, q + (NADA_V + 1))
                if first:
                    tails()
                    pe.wait_ge(tail_cp, 1)
                for t in range(NT):
                    mm = pe.matmul(banks(MIX, 2)[:, t * P:(t + 1) * P], vf[:, par, t, :],
                                   wsT[:, bass.ds(q, 1), :].rearrange("p a i -> p (a i)"), start=True, stop=True)
                mm.then_inc(mix_mm, 1)
                pe.wait_ge(u_made, q + 1)
                part(q, par, 2)
                pe.wait_ge(m0_made, q + 1)
                for j in range(2):
                    mm = pe.matmul(PS[:, MIX + j, :], wpl[:, par, :],
                                   dT[:, bass.ds(half, 1), j * 512:(j + 1) * 512].rearrange("p a n -> p (a n)"),
                                   start=True, stop=True)
                mm.then_inc(yb_mm, 1)

            run_steps(pe, f_step, 0, HD, 2, HD)

            pe.wait_ge(consts, 4)
            pe.wait_ge(tb_made, HD)
            pe.wait_ge(yb1_made, HD)

            def y_half(q, par, half, looped):
                r = rows_of(q, looped)
                n = 0
                for k in range(KD):
                    if not looped and q == 0:
                        pe.wait_ge(w_lo_k, KD + half * KD + k + 1)
                    for a, b in ((mt_hi, wo_hi), (mt_hi, wo_lo), (mt_lo, wo_hi)):
                        mm = pe.matmul(PS[0:r, 2 * par + half, :], a[par][:, k, 0:r],
                                       b[:, k, half * 512:(half + 1) * 512], start=(n == 0), stop=(n == 3 * KD - 1))
                        n += 1
                return mm

            def h2_turn(q, par, looped):
                r = rows_of(q, looped)
                pe.wait_ge(h2_made, q + 1)
                wait(pe, h2T_made, q)
                for k in range(KD):
                    mm = pe.transpose(banks(4, 2)[:, k * r:(k + 1) * r], h2[0:r, par, k * P:(k + 1) * P],
                                      ident[0:r, 0:r])
                mm.then_inc(h2_tr, 1)

            def places(q, looped):
                r = rows_of(q, looped)
                first = not looped and q == 0
                pe.wait_ge(m_made, q + 1)
                wait(pe, mrun_made, q)
                wait(pe, mp_made, q)
                mm = pe.matmul(PS[0:r, 7, 0:NE], upper[0:r, 0:r], mb[0:r, :], start=True, stop=first)
                if not first:
                    mm = pe.matmul(PS[0:r, 7, 0:NE], ones[:, 0:r], mrun[:, :], start=False, stop=True)
                mm.then_inc(pos_mm, 1)

            def logits(q, par, looped):
                r = rows_of(q, looped)
                pe.wait_ge(h2T_made, q + 1)
                wait(pe, lg_made, q)
                for k in range(KD):
                    mm = pe.matmul(PS[0:r, 6, 0:NL], h2T[:, par, k, 0:r], wr[:, k, :], start=(k == 0),
                                   stop=(k == KD - 1))
                mm.then_inc(lg_mm, 1)

            pe.wait_ge(later_in, LATER)

            def w_step(q, par, half, looped):
                if looped or q < NQ:
                    pe.wait_ge(ht_lo_made, q + (NQ + 1))
                    wait(pe, y_scaled, q - 1)
                    y_half(q, par, 0, looped)
                if looped or 2 <= q <= NQ + 1:
                    h2_turn(q - 2, par, looped or q > 2)
                if looped or q >= 3:
                    places(q - 3, looped or q > 3)
                if looped or q < NQ:
                    y_half(q, par, 1, looped).then_inc(y_mm, 1)
                if looped or 2 <= q <= NQ + 1:
                    logits(q - 2, par, looped or q > 2)

            run_steps(pe, w_step, 0, NQ + 3, 4, 8)
            pe.wait_ge(mrun_made, NQ)
            pe.wait_ge(mp_made, NQ)
            pe.matmul(PS[:, 7, 0:NE], ones[:, :], mrun[:, :], start=True, stop=True).then_inc(cnt_mm, 1)

            def turn_in(n, s, uses):
                par = s % HG
                pe.wait_ge(hg_in[par], uses * 16 + 16)
                wait(pe, hgT_a, n)
                wait(pe, hgT_b, n)
                for k in range(KD):
                    mm = pe.transpose(banks(0, 2)[:, k * P:(k + 1) * P], hg[par][:, k * P:(k + 1) * P], ident[:, :])
                mm.then_inc(hg_tr, 1)

            def gate_up(hgt, wgu_, bank):
                for j in range(2):
                    for k in range(KD):
                        mm = pe.matmul(PS[:, bank, j * P:(j + 1) * P], wgu_[:, j, k, :], hgt[:, k, :],
                                       start=(k == 0), stop=(k == KD - 1))
                return mm

            def down(n, s):
                par, slot = s % 2, s % RING
                pe.wait_ge(act_made, n + 1)
                wait(pe, ysb_made, n)
                for half in range(2):
                    mm = pe.matmul(PS[:, 5 + half, :], actT[:, par, :], wd[slot][:, half * 512:(half + 1) * 512],
                                   start=True, stop=True)
                mm.then_inc(down_mm, 1)

            def e_step(n, s, oct_, looped):
                par = s % 2
                if looped or n < NE:
                    pe.wait_ge(hgT_a, n + 1)
                    pe.wait_ge(hgT_b, n + 1)
                    pe.wait_ge(we_in[s], oct_ * 48 + 48)
                    wait(pe, act_made, n - 1)
                    gate_up(hgT[par], wgu[s], 2 + par).then_inc(gu_mm, 1)
                if looped or n + 1 < NE:
                    turn_in(n + 1, s + 1, oct_ * (RING // HG) + (s + 1) // HG)
                if looped or n >= 1:
                    down(n - 1, (s - 1) % RING)

            turn_in(0, 0, 0)
            run_steps(pe, e_step, 0, NE + 1, RING, NE - RING, RING)

            pe.wait_ge(cnt_made, 2)
            pe.wait_ge(ysb_made, NE)
            fullest = pe.value_load(most_u[0:1, 0:1], min_val=0, max_val=TOK)
            with pe.If(fullest > P):
                with pe.Fori(1, NQ) as c:
                    with pe.Fori(0, NE) as x:
                        m = (c - 1) * NE + x
                        pe.wait_ge(o_gather, m * 16 + 16)
                        for k in range(KD):
                            mm = pe.transpose(banks(0, 2)[:, k * P:(k + 1) * P], hg[0][:, k * P:(k + 1) * P],
                                              ident[:, :])
                        mm.then_inc(o_pe, 1)
                        pe.wait_ge(o_dve, m * 3 + 1)
                        pe.wait_ge(o_in, m * 64 + 64)
                        gate_up(hgT[0], wgu[0], 2).then_inc(o_pe, 1)
                        pe.wait_ge(o_dve, m * 3 + 2)
                        for half in range(2):
                            mm = pe.matmul(PS[:, 5 + half, :], actT[:, 0, :], wd[0][:, half * 512:(half + 1) * 512],
                                           start=True, stop=True)
                        mm.then_inc(o_pe, 1)


_INS = ["x_prompt", "x_sample", "c_prompt", "c_sample", "state_pool", "w_ada", "b_ada", "g_pre_mix",
        "g_post_mix", "g_pre_ffn", "g_post_ffn", "w_in", "ln_v_g", "ln_v_b", "w_spatial", "b_spatial",
        "w_pool", "pool_scale", "w_out", "w_router_grp", "b_router_grp", "w_router_exp",
        "b_router_exp", "w_exp_gate", "w_exp_up", "w_exp_down"]


def kernel(**inputs):
    import numpy as _np
    import concourse.bacc as _bacc
    from concourse import mybir as _mybir
    from concourse.bass_utils import run_bass_kernel_spmd as _run

    nc = _bacc.Bacc("TRN2", target_bir_lowering=False, num_devices=1)
    arrays, args = {}, []
    for name in _INS:
        a = _np.ascontiguousarray(inputs[name])
        arrays[f"in_{name}_dram"] = a
        args.append(nc.dram_tensor(f"in_{name}_dram", a.shape, _mybir.dt.from_np(a.dtype), kind="ExternalInput").ap())
    x_prompt, x_sample, state_pool = inputs["x_prompt"], inputs["x_sample"], inputs["state_pool"]
    depth, samples, rows, width = state_pool.shape
    outs = [x_prompt.shape, x_sample.shape, (depth, x_prompt.shape[0], rows, width), state_pool.shape,
            (depth, samples, 1, x_prompt.shape[2])]
    for i, shape in enumerate(outs):
        args.append(nc.dram_tensor(f"out_{i}_dram", shape, _mybir.dt.float32, kind="ExternalOutput").ap())
    trunk_step(nc, *args)
    r = _run(nc, [arrays], core_ids=[0])
    return tuple(r.results[0][f"out_{i}_dram"] for i in range(len(outs)))
```
